# Optimizing a Trainium2 kernel written in Bass

```python
import jax
import jax.numpy as jnp
from jax import lax
import numpy as np

D_MODEL = 1024
BATCH = 1
SEQ = 256
DEPTH = 2

MIX_WIDTH = 512
N_BRANCHES = 3
EPS = 1e-6
FOX_HEADS = 4
FOX_HEAD_DIM = 128
FOX_BLOCK = 128
FOX_FORGET_BIAS = 2.0
GLA_HEADS = 4
GLA_DK = 64
GLA_DV = 128
GLA_KDIM = GLA_HEADS * GLA_DK
GLA_RANK = 16
GLA_TAU = 16.0
GLA_CHUNK = 64
RET_HEADS = 4
RET_DK = 128
RET_DV = 128
RET_CHUNK = 64
ROPE_BASE = 10000.0
IN_SPLITS = (MIX_WIDTH, MIX_WIDTH, MIX_WIDTH, FOX_HEADS,
             GLA_KDIM, GLA_KDIM, MIX_WIDTH, GLA_RANK, MIX_WIDTH,
             MIX_WIDTH, MIX_WIDTH, MIX_WIDTH, MIX_WIDTH)
D_IN = sum(IN_SPLITS)
D_FF = 2816
N_EXPERTS = 8
TOP_K = 2
D_FF_EXPERT = 3584
N_DENSE = (DEPTH + 1) // 2
N_MOE = DEPTH // 2

kernel_name = 'fox_gla_retnet_gated_hybrid_moe'

def rmsnorm(x, g):
    xf = x.astype(jnp.float32)
    y = xf * lax.rsqrt(jnp.mean(xf * xf, axis=-1, keepdims=True) + EPS)
    return (y * g.astype(jnp.float32)).astype(x.dtype)

def head_rmsnorm(o):
    return o * lax.rsqrt(jnp.mean(o * o, axis=-1, keepdims=True) + EPS)

def head_groupnorm(o):
    mu = jnp.mean(o, axis=-1, keepdims=True)
    var = jnp.mean(jnp.square(o - mu), axis=-1, keepdims=True)
    return (o - mu) * lax.rsqrt(var + EPS)

def split_heads(t, n):
    b, s, _ = t.shape
    return t.reshape(b, s, n, -1).transpose(0, 2, 1, 3)

def merge_heads(t):
    b, n, s, d = t.shape
    return t.transpose(0, 2, 1, 3).reshape(b, s, n * d)

def to_chunks(t, c):
    b, h, s, d = t.shape
    return t.reshape(b, h, s // c, c, d)

def rotary(t, pos):
    half = t.shape[-1] // 2
    inv_freq = ROPE_BASE ** (-(jnp.arange(half, dtype=jnp.float32) / half))
    ang = pos[:, None] * inv_freq[None, :]
    cos, sin = jnp.cos(ang), jnp.sin(ang)
    t1, t2 = t[..., :half], t[..., half:]
    return jnp.concatenate([t1 * cos - t2 * sin, t1 * sin + t2 * cos], axis=-1)

def fox_attention(q, k, v, log_f):
    s_len = q.shape[2]
    scale = q.shape[-1] ** -0.5
    c = jnp.cumsum(log_f, axis=-1)
    outs = []
    for i in range(s_len // FOX_BLOCK):
        lo = i * FOX_BLOCK
        hi = lo + FOX_BLOCK
        s = jnp.einsum('bhqd,bhkd->bhqk', q[:, :, lo:hi], k[:, :, :hi]).astype(jnp.float32) * scale
        s = s + c[:, :, lo:hi, None] - c[:, :, None, :hi]
        causal = (lo + jnp.arange(FOX_BLOCK))[:, None] >= jnp.arange(hi)[None, :]
        p = jax.nn.softmax(jnp.where(causal, s, -jnp.inf), axis=-1)
        outs.append(jnp.einsum('bhqk,bhkd->bhqd', p.astype(v.dtype), v[:, :, :hi]))
    return jnp.concatenate(outs, axis=2)

def gla_chunked(q, k, v, log_a):
    b_, h_, s_len, dk = q.shape
    dv = v.shape[-1]
    c = GLA_CHUNK
    qc, kc, vc = to_chunks(q, c), to_chunks(k, c), to_chunks(v, c)
    bcum = jnp.cumsum(to_chunks(log_a, c), axis=3)
    q_dec = qc * jnp.exp(bcum)
    k_inv = kc * jnp.exp(-bcum)
    k_end = kc * jnp.exp(bcum[..., -1:, :] - bcum)
    a_end = jnp.exp(bcum[..., -1, :])
    mask = jnp.tril(jnp.ones((c, c), dtype=bool))
    att = jnp.where(mask, jnp.einsum('bhnqd,bhnkd->bhnqk', q_dec, k_inv), 0.0)
    o_intra = jnp.einsum('bhnqk,bhnkv->bhnqv', att, vc)

    def step(state, inp):
        q_i, k_i, v_i, a_i = inp
        o = jnp.einsum('bhqd,bhdv->bhqv', q_i, state)
        state = a_i[..., :, None] * state + jnp.einsum('bhkd,bhkv->bhdv', k_i, v_i)
        return state, o

    xs = (jnp.moveaxis(q_dec, 2, 0), jnp.moveaxis(k_end, 2, 0),
          jnp.moveaxis(vc, 2, 0), jnp.moveaxis(a_end, 2, 0))
    _, o_inter = lax.scan(step, jnp.zeros((b_, h_, dk, dv), jnp.float32), xs)
    o = o_intra + jnp.moveaxis(o_inter, 0, 2)
    return o.reshape(b_, h_, s_len, dv)

def retention_chunked(q, k, v, log_gamma):
    b_, h_, s_len, dk = q.shape
    dv = v.shape[-1]
    c = RET_CHUNK
    qc, kc, vc = to_chunks(q, c), to_chunks(k, c), to_chunks(v, c)
    idx = jnp.arange(c, dtype=jnp.float32)
    diff = idx[:, None] - idx[None, :]
    lg = log_gamma[:, None, None]
    dmat = jnp.where(diff >= 0, jnp.exp(jnp.maximum(diff, 0.0) * lg), 0.0)
    inner = jnp.einsum('bhnqd,bhnkd->bhnqk', qc, kc) * dmat[None, :, None]
    o_intra = jnp.einsum('bhnqk,bhnkv->bhnqv', inner, vc)
    q_dec = qc * jnp.exp((idx + 1.0)[None, :] * log_gamma[:, None])[None, :, None, :, None]
    k_dec = kc * jnp.exp((c - 1.0 - idx)[None, :] * log_gamma[:, None])[None, :, None, :, None]
    chunk_dec = jnp.exp(c * log_gamma)[None, :, None, None]

    def step(state, inp):
        q_i, k_i, v_i = inp
        o = jnp.einsum('bhqd,bhdv->bhqv', q_i, state)
        state = chunk_dec * state + jnp.einsum('bhkd,bhkv->bhdv', k_i, v_i)
        return state, o

    xs = (jnp.moveaxis(q_dec, 2, 0), jnp.moveaxis(k_dec, 2, 0), jnp.moveaxis(vc, 2, 0))
    _, o_inter = lax.scan(step, jnp.zeros((b_, h_, dk, dv), jnp.float32), xs)
    o = o_intra + jnp.moveaxis(o_inter, 0, 2)
    return o.reshape(b_, h_, s_len, dv)

def hybrid_mixer(h, w_in, b_forget, w_gla_a2, b_gla_a, w_gate, w_branch, w_o):
    f32 = jnp.float32
    s_len = h.shape[1]
    proj = h @ w_in
    cuts = np.cumsum(np.array(IN_SPLITS))[:-1].tolist()
    (fq, fk, fv, fz, gq, gk, gv, ga, gr, rq, rk, rv, rg) = jnp.split(proj, cuts, axis=-1)

    log_f = jax.nn.log_sigmoid((fz + b_forget).astype(f32)).transpose(0, 2, 1)
    o_fox = fox_attention(split_heads(fq, FOX_HEADS), split_heads(fk, FOX_HEADS),
                          split_heads(fv, FOX_HEADS), log_f)
    o_fox = merge_heads(o_fox).astype(h.dtype)

    log_a = jax.nn.log_sigmoid((ga @ w_gla_a2 + b_gla_a).astype(f32)) / GLA_TAU
    o_gla = gla_chunked(split_heads(gq.astype(f32), GLA_HEADS) * GLA_DK ** -0.5,
                        split_heads(gk.astype(f32), GLA_HEADS),
                        split_heads(gv.astype(f32), GLA_HEADS),
                        split_heads(log_a, GLA_HEADS))
    o_gla = (merge_heads(head_rmsnorm(o_gla)) * jax.nn.silu(gr.astype(f32))).astype(h.dtype)

    pos = jnp.arange(s_len, dtype=f32)
    log_gamma = jnp.log1p(-jnp.exp2(-5.0 - jnp.arange(RET_HEADS, dtype=f32)))
    r_q = rotary(split_heads(rq.astype(f32), RET_HEADS), pos)
    r_k = rotary(split_heads(rk.astype(f32), RET_HEADS), pos) * RET_DK ** -0.5
    o_ret = retention_chunked(r_q, r_k, split_heads(rv.astype(f32), RET_HEADS), log_gamma)
    o_ret = (merge_heads(head_groupnorm(o_ret)) * jax.nn.silu(rg.astype(f32))).astype(h.dtype)

    merged = None
    for i, o_b in enumerate((o_fox, o_gla, o_ret)):
        gate = jax.nn.sigmoid(h @ w_gate[:, i * D_MODEL:(i + 1) * D_MODEL])
        term = gate * (o_b @ w_branch[i])
        merged = term if merged is None else merged + term
    return merged @ w_o

def swiglu(h, w1, w3, w2):
    return (jax.nn.silu(h @ w1) * (h @ w3)) @ w2

def moe_swiglu(h, router_w, w1, w3, w2):
    logits = (h @ router_w).astype(jnp.float32)
    top_v, top_i = lax.top_k(logits, TOP_K)
    top_w = jax.nn.softmax(top_v, axis=-1)
    combine = jnp.sum(jax.nn.one_hot(top_i, N_EXPERTS, dtype=jnp.float32) * top_w[..., None], axis=-2)
    out = jnp.zeros_like(h)
    for e in range(N_EXPERTS):
        out = out + combine[..., e:e + 1].astype(h.dtype) * swiglu(h, w1[e], w3[e], w2[e])
    return out

def setup_inputs(seed: int = 0) -> dict:
    key = jax.random.key(seed)
    ks = jax.random.split(key, 20)
    f32 = jnp.float32

    def nrm(k, shape, fan_in):
        return jax.random.normal(k, shape, f32) * fan_in ** -0.5

    def gain(k, shape):
        return 1.0 + 0.02 * jax.random.normal(k, shape, f32)

    return {
        'x': jax.random.normal(ks[0], (BATCH, SEQ, D_MODEL), f32),
        'norm1_g': gain(ks[1], (DEPTH, D_MODEL)),
        'w_in': nrm(ks[2], (DEPTH, D_MODEL, D_IN), D_MODEL),
        'b_forget': FOX_FORGET_BIAS + 0.1 * jax.random.normal(ks[3], (DEPTH, FOX_HEADS), f32),
        'w_gla_a2': nrm(ks[4], (DEPTH, GLA_RANK, GLA_KDIM), GLA_RANK),
        'b_gla_a': 0.1 * jax.random.normal(ks[5], (DEPTH, GLA_KDIM), f32),
        'w_gate': nrm(ks[6], (DEPTH, D_MODEL, N_BRANCHES * D_MODEL), D_MODEL),
        'w_branch': nrm(ks[7], (DEPTH, N_BRANCHES, MIX_WIDTH, D_MODEL), MIX_WIDTH),
        'w_o': nrm(ks[8], (DEPTH, D_MODEL, D_MODEL), D_MODEL),
        'norm2_g': gain(ks[9], (DEPTH, D_MODEL)),
        'ffn_w1': nrm(ks[10], (N_DENSE, D_MODEL, D_FF), D_MODEL),
        'ffn_w3': nrm(ks[11], (N_DENSE, D_MODEL, D_FF), D_MODEL),
        'ffn_w2': nrm(ks[12], (N_DENSE, D_FF, D_MODEL), D_FF),
        'router_w': nrm(ks[13], (N_MOE, D_MODEL, N_EXPERTS), D_MODEL),
        'moe_w1': nrm(ks[14], (N_MOE, N_EXPERTS, D_MODEL, D_FF_EXPERT), D_MODEL),
        'moe_w3': nrm(ks[15], (N_MOE, N_EXPERTS, D_MODEL, D_FF_EXPERT), D_MODEL),
        'moe_w2': nrm(ks[16], (N_MOE, N_EXPERTS, D_FF_EXPERT, D_MODEL), D_FF_EXPERT),
        'final_g': gain(ks[17], (D_MODEL,)),
    }

def reference(x, norm1_g, w_in, b_forget, w_gla_a2, b_gla_a, w_gate, w_branch, w_o,
              norm2_g, ffn_w1, ffn_w3, ffn_w2, router_w, moe_w1, moe_w3, moe_w2, final_g):
    for layer in range(DEPTH):
        h = rmsnorm(x, norm1_g[layer])
        x = x + hybrid_mixer(h, w_in[layer], b_forget[layer], w_gla_a2[layer], b_gla_a[layer],
                             w_gate[layer], w_branch[layer], w_o[layer])
        h = rmsnorm(x, norm2_g[layer])
        j = layer // 2
        if layer % 2 == 0:
            x = x + swiglu(h, ffn_w1[j], ffn_w3[j], ffn_w2[j])
        else:
            x = x + moe_swiglu(h, router_w[j], moe_w1[j], moe_w3[j], moe_w2[j])
    return rmsnorm(x, final_g)


_drawn_inputs = setup_inputs


def setup_inputs(seed=0):
    import zlib

    import numpy as np

    out = dict(_drawn_inputs(seed))
    spreads = {}
    factors = {}
    for name, (base, spread) in spreads.items():
        noise = np.random.default_rng([zlib.crc32(name.encode()), seed]).standard_normal(out[name].shape)
        drawn = base * np.exp(spread * noise) if base else spread * noise
        out[name] = jnp.asarray(drawn.astype(out[name].dtype))
    for name, factor in factors.items():
        out[name] = (out[name] * factor).astype(out[name].dtype)
    return out
```

```python
from contextlib import ExitStack

import numpy as np

import concourse.bass as bass
from concourse import mybir
from concourse.alu_op_type import AluOpType as ALU

P = 128
SEQ, D = 256, 1024
NT = SEQ // P
KT_D = D // P
LAYERS = 2
EPS = 1e-6
HEADS, HD = 4, 128
MIX = HEADS * HD
GLA_DK, GLA_RANK, GLA_TAU, CHUNK = 64, 16, 16.0, 64
D_FF, N_EXP, D_FFE = 2816, 8, 3584

GRAN = 2048
RAW, RING = 6, 3
FF = 256
N_FF = D_FF // FF
EF = 512
N_EF = D_FFE // EF
MIX_G = 43
FFN_G0 = MIX_G
FFN_G = 3 * N_FF
LAYER_G0 = (0, FFN_G0 + FFN_G)
ROUTER_G = LAYER_G0[1] + MIX_G
MOE_G0 = ROUTER_G + 1
EXP_G = 6 * N_EF
TOTAL_G = MOE_G0 + N_EXP * EXP_G
assert MOE_G0 % 6 == 0 and EXP_G % 6 == 0 and TOTAL_G % 6 == 0

_W = (MIX, MIX, MIX, HEADS, HEADS * GLA_DK, HEADS * GLA_DK, MIX, GLA_RANK, MIX, MIX, MIX, MIX, MIX)
_AT = [sum(_W[:i]) for i in range(len(_W))]
FQ, FK, FV, FZ, GQ, GK, GV, GA, GR, RQ, RK, RV, RG = _AT
D_IN = sum(_W)
CHUNKS = (("rq", RQ), ("rk", RK), ("rv", RV), ("rg", RG), ("fq", FQ), ("fk", FK), ("fv", FV),
          ("gqk", GQ), ("gv", GV), ("gr", GR))
BY_FEATURE = ("fq", "fk", "gqk")
BRANCH_ORDER = (2, 0, 1)
N_GB = 2 * len(BRANCH_ORDER)
GATE_S0 = 1 + 2 * len(CHUNKS)
WO_S0 = GATE_S0 + 3 * N_GB
assert WO_S0 + 4 == MIX_G
READER = ["dve", "dve", "act", "act", "act", "act", "act", "dve", "act", "act"] + ["act", "dve"] * N_GB
AT_TILE = {2: 0, 0: 4, 1: 0}

C_ID, C_CAUSAL, C_CHUNK, C_STRICT, C_ONES, C_IOTA, C_COS = (P * i for i in range(7))
C_SIN = C_COS + NT * 64
C_DECAY = C_SIN + NT * P
C_ALL = C_DECAY + HEADS * SEQ
NEG = -1e30


def hybrid_decoder_kernel(nc, stream, x_in, const_in, gain_in, fin_gain, b_forget, gla_a2, out):
    f32, f32r, i32, u32 = mybir.dt.float32, mybir.dt.float32r, mybir.dt.int32, mybir.dt.uint32
    ACT, AX = mybir.ActivationFunctionType, mybir.AxisListType

    with ExitStack() as ctx:
        def sb(name, shape, dt=f32):
            return ctx.enter_context(nc.sbuf_tensor(name, shape, dt))

        def sem(name):
            return ctx.enter_context(nc.semaphore(name))

        raw = sb("raw", [P, RAW, GRAN])
        w_hi = sb("w_hi", [P, RING, GRAN], f32r)
        w_lo = sb("w_lo", [P, RING, GRAN], f32r)
        x = sb("x", [P, NT, D])
        xn = sb("xn", [P, NT, D])
        hT = [sb(f"hT_{h}", [P, KT_D, SEQ], f32r) for h in ("hi", "lo")]
        aT = [sb(f"aT_{h}", [P, 8, SEQ], f32r) for h in ("hi", "lo")]
        qT = sb("qT", [P, 2, HEADS, SEQ])
        kT = sb("kT", [P, 2, HEADS, SEQ])
        val = sb("val", [P, 2, NT, MIX])
        work = sb("work", [P, 2, 512])
        rot = sb("rot", [P, 2, 512])
        sgate = sb("sgate", [P, NT, MIX])
        o = sb("o", [P, NT, MIX])
        soft = sb("soft", [P, 2, 384])
        att = sb("att", [P, 2, 384])
        cst = sb("cst", [P, C_ALL])
        gain = sb("gain", [P, 4, KT_D])
        bf = sb("bf", [36, LAYERS])
        a2 = sb("a2", [GLA_RANK + 1, LAYERS, 256])
        gaT = sb("gaT", [32, SEQ])
        ncT = sb("ncT", [36, SEQ])
        cq = sb("cq", [P, 8])
        bend = sb("bend", [P, 8])
        aend = sb("aend", [P, 8])
        stats = sb("stats", [P, 8, 6])
        mv = sb("mv", [P, 8, 2])
        rs = sb("rs", [P, 4, 8])
        ss = sb("ss", [P, 3, NT])
        nmax = sb("nmax", [P, NT, HEADS])
        rsum = sb("rsum", [P, NT, HEADS])
        lgT = sb("lgT", [8, SEQ])
        lg = sb("lg", [P, NT, 8])
        top = sb("top", [P, NT, 8])
        topi = sb("topi", [P, NT, 8], u32)
        topf = sb("topf", [P, NT, 8])
        tw = sb("tw", [P, 3, NT])
        comb = sb("comb", [P, NT, N_EXP + 1])
        rank = sb("rank", [P, NT, N_EXP + 1])
        picked = sb("picked", [P, NT, N_EXP + 1])
        flag = sb("flag", [P, 1], i32)
        flagf = sb("flagf", [P, 1])

        ident = cst[:, C_ID:C_ID + P]
        causal = cst[:, C_CAUSAL:C_CAUSAL + P]
        chunk_tri = cst[:, C_CHUNK:C_CHUNK + P]
        strict = cst[:, C_STRICT:C_STRICT + P]
        ones = cst[:, C_ONES:C_ONES + P]
        iota = cst[:, C_IOTA:C_IOTA + P]
        cos = cst[:, C_COS:C_SIN].rearrange("p (t i) -> p t i", t=NT)
        sin = cst[:, C_SIN:C_DECAY].rearrange("p (t u i) -> p t u i", t=NT, u=2)
        decay = cst[:, C_DECAY:C_ALL].rearrange("p (h q) -> p h q", h=HEADS)
        gsc = soft[:, :, :].rearrange("p a b -> p (a b)")[:, 0:512]
        states = rot[:, :, :].rearrange("p a b -> p (a b)")[:, 0:768].rearrange("p (f c v) -> p f c v", f=2, c=3)
        q_dec, k_inv = (qT[:, 0, 2 * i:2 * i + 2, :] for i in range(2))
        k_end = kT[:, 0, 0:2, :]
        k_tok = kT[:, 0, 2:4, :]
        xgT = [h[:, 0:4, :].rearrange("p k (a s) -> p (k a) s", a=2) for h in hT]
        gT = [h[:, 0:2, :].rearrange("p k (a s) -> p (k a) s", a=2) for h in aT]
        pick = rot[:, 0, 0:SEQ].rearrange("p (t s) -> p t s", t=NT)
        pick_w = rot[:, 0, SEQ:512].rearrange("p (t s) -> p t s", t=NT)
        put_w = rot[:, 1, 0:SEQ]
        y_sb = val[:, 0, :, :]
        gfin = val[:, 1, :, :].rearrange("p t c -> p (t c)")

        M = [ctx.enter_context(nc.psum_tensor(f"M{i}", [P, 512], f32)) for i in range(4)]
        A = [ctx.enter_context(nc.psum_tensor(f"A{i}", [P, 512], f32)) for i in range(4)]

        loaded = [sem(f"loaded{i}") for i in range(RAW)]
        s_in = sem("inputs_loaded")
        s_const = sem("constants_loaded")
        hi_done, lo_done, gran_done = sem("hi_done"), sem("lo_done"), sem("gran_done")
        act_read, dve_read = sem("act_read"), sem("dve_read")
        act_own, dve_own = sem("act_own"), sem("dve_own")
        ready0 = sem("dve_ready")
        sumsq, normed, x_turned, hT_hi_done, hT_done = (sem(n) for n in ("sumsq", "normed", "x_turned", "hT_hi_done", "hT_done"))
        root_in, root_done = sem("root_in"), sem("root_done")
        x_new = sem("x_new")
        ga_done, z_done, fz_done, fln_done, c_done = (sem(n) for n in ("ga_done", "z_done", "fz_done", "fln_done", "c_done"))
        zln_done, loga_done, cum_done, cq_done, bend_done, exp_done = (
            sem(n) for n in ("zln_done", "loga_done", "cum_done", "cq_done", "bend_done", "exp_done"))
        rotated, rot_turned, rot_read = sem("rotated"), sem("rot_turned"), sem("rot_read")
        ret_scores, ret_att, ret_out = sem("ret_scores"), sem("ret_att"), sem("ret_out")
        val_done, silu_done, fq_done = sem("val_done"), sem("silu_done"), sem("fq_done")
        fox_scores, fox_rows, fox_exp, fox_turned, fox_att, fox_out = (
            sem(n) for n in ("fox_scores", "fox_rows", "fox_exp", "fox_turned", "fox_att", "fox_out"))
        gla_ops, kend_turned, kend_done, kv_done, state_done = (
            sem(n) for n in ("gla_ops", "kend_turned", "kend_done", "kv_done", "state_done"))
        gla_scores, gla_att, gla_out = sem("gla_scores"), sem("gla_att"), sem("gla_out")
        o_done, o_turned, oT_hi_done, oT_done = (sem(n) for n in ("o_done", "o_turned", "oT_hi_done", "oT_done"))
        gate_done, merged = sem("gate_done"), sem("merged")
        m_turned, mT_hi_done, mT_done = sem("m_turned"), sem("mT_hi_done"), sem("mT_done")
        f_silu, f_prod, f_hi, f_lo = (sem(n) for n in ("f_silu", "f_prod", "f_hi", "f_lo"))
        rt_copied, rt_turned, rt_top, rt_exp, rt_picked, rt_ranked, rt_flag = (
            sem(n) for n in ("rt_copied", "rt_turned", "rt_top", "rt_exp", "rt_picked", "rt_ranked", "rt_flag"))
        e_moved = sem("e_moved")
        e_pick, e_gather, e_xhi, e_xlo = (sem(n) for n in ("e_pick", "e_gather", "e_xhi", "e_xlo"))
        e_silu, e_prod, e_turned, e_hi, e_lo = (sem(n) for n in ("e_silu", "e_prod", "e_turned", "e_hi", "e_lo"))
        e_pickw, e_putw, e_putw_done, e_y0, e_y1, e_scatter, e_added = (
            sem(n) for n in ("e_pickw", "e_putw", "e_putw_done", "e_y0", "e_y1", "e_scatter", "e_added"))
        fin_sq, fin_done, stored = sem("fin_sq"), sem("fin_done"), sem("stored")
        block = ctx.enter_context(nc.Block())

        def reads(engine, layer, chunk):
            return layer * READER.count(engine) + READER[:chunk + 1].count(engine)

        def wait_read(pe, layer, chunk):
            if READER[chunk] == "act":
                pe.wait_ge(act_read, reads("act", layer, chunk))
            else:
                pe.wait_ge(dve_read, reads("dve", layer, chunk))

        def gla_result(t, h):
            at = (2 * t + h // 2) * HD
            return A[2 + h % 2][:, at:at + HD]

        def by_tile(t, h):
            return A[t][:, h * HD:(h + 1) * HD]

        def pair(chunk):
            return M[2 * (chunk % 2):2 * (chunk % 2) + 2]

        @block.sync
        def _(sp):
            def load(six, local, source, first=False):
                if not first:
                    sp.wait_ge(lo_done, 6 * six + local - RAW + 1)
                sp.dma_start(raw[:, local % RAW, :], source).then_inc(loaded[local % RAW], 16)

            for t in range(NT):
                sp.dma_start(x[:, t, :], x_in[:, t, :]).then_inc(s_in, 16)
            for g in range(RAW):
                load(0, g, stream[g], first=True)
            six_of = stream.rearrange("(s u) p n -> s u p n", u=6)
            with sp.Fori(1, TOTAL_G // 6) as six:
                for u in range(6):
                    load(six, u, six_of[six, u])
            for u in range(2):
                load(TOTAL_G // 6, u, stream[MOE_G0 + u])
            sp.wait_ge(rt_flag, 1)
            over = sp.value_load(flag[0:1, 0:1], min_val=0, max_val=P)
            with sp.If(over > 0):
                s1 = TOTAL_G // 6
                for u in range(2, 6):
                    load(s1, u, stream[MOE_G0 + u])
                with sp.Fori(1, N_EXP * EXP_G // 6) as six:
                    for u in range(6):
                        load(six + s1, u, six_of[six + MOE_G0 // 6, u])
                for u in range(2):
                    load(s1 + N_EXP * EXP_G // 6, u, stream[MOE_G0 + u])
            with sp.Else():
                sp.wait_ge(rt_flag, 1)
            for t in range(NT):
                sp.wait_ge(fin_done, t + 1)
                sp.dma_start(out[:, t, :], xn[:, t, :]).then_inc(stored, 16)
            sp.wait_ge(stored, 16 * NT)

        @block.gpsimd
        def _(pool):
            pool.dma_start(gain[:, :, :], gain_in).then_inc(s_const, 16)
            pool.dma_start(cst[:, :], const_in).then_inc(s_const, 16)
            pool.dma_start(bf[32:36, :], b_forget).then_inc(s_const, 16)
            pool.dma_start(a2[:, :, :], gla_a2).then_inc(s_const, 16)
            pool.wait_ge(x_new, 2 * NT + 2 * NT - NT)
            pool.dma_start(gfin, fin_gain.partition_broadcast(P)).then_inc(s_const, 16)

        @block.scalar
        def _(act):
            own = [0]

            def link(ins):
                own[0] += 1
                ins.then_inc(act_own, 1)
                act.wait_ge(act_own, own[0])

            def copy(dst, src, **kw):
                return act.activation(dst, src, ACT.Copy, **kw)

            def hi(six, local):
                act.wait_ge(loaded[local % RAW], 16 * (six + local // RAW) + 16)
                if not (isinstance(six, int) and 6 * six + local < RING):
                    act.wait_ge(gran_done, 6 * six + local - RING + 1)
                copy(w_hi[:, local % RING, :], raw[:, local % RAW, :]).then_inc(hi_done, 1)

            def norm(i):
                for t in range(NT):
                    if i == 0:
                        act.wait_ge(s_in, 16 * NT)
                    else:
                        act.wait_ge(x_new, NT * (i - 1) + t + 1)
                    act.activation(xn[:, t, :], x[:, t, :], ACT.Square, accum_out=ss[:, 0, t:t + 1]).then_inc(sumsq, 1)
                act.wait_ge(root_in, roots[0] + 1)
                act.activation(ss[:, 2, :], ss[:, 1, :], ACT.Sqrt).then_inc(root_done, 1)
                roots[0] += 1
                for kp in range(KT_D // 2):
                    act.wait_ge(x_turned, 4 * i + kp + 1)
                    for k in range(2 * kp, 2 * kp + 2):
                        act.activation(hT[0][:, k, :], A[kp][:, (k % 2) * SEQ:(k % 2 + 1) * SEQ], ACT.Copy,
                                       scale=gain[:, i, k:k + 1]).then_inc(hT_hi_done, 1)

            roots = [0]

            def root8(src, dst):
                act.wait_ge(root_in, roots[0] + 1)
                act.activation(dst, src, ACT.Sqrt).then_inc(root_done, 1)
                roots[0] += 1

            def turn_hi(n, bank, dst):
                act.wait_ge(o_turned, n)
                copy(dst, bank[:, :].rearrange("p (h q) -> p h q", h=HEADS)).then_inc(oT_hi_done, 1)

            def mixers(layer):
                g0 = LAYER_G0[layer]
                for s in range(MIX_G):
                    if s > 0:
                        act.wait_ge(gran_done, g0 + s)
                    if s == 1:
                        copy(gaT[0:GLA_RANK, :], A[0][0:GLA_RANK, 0:SEQ]).then_inc(ga_done, 1)
                    if s == 2:
                        act.wait_ge(fz_done, layer + 1)
                        e = att[32:36, 1, 0:SEQ]
                        link(act.activation(e, att[32:36, 0, 0:SEQ], ACT.Abs))
                        link(act.activation(e, e, ACT.Exp, scale=-1.0))
                        act.activation(e, e, ACT.Ln, bias=1.0).then_inc(fln_done, 1)
                    if s == 3:
                        act.wait_ge(z_done, layer + 1)
                        e = o[:, 0, :]
                        link(act.activation(e, A[1][:, :], ACT.Abs))
                        link(act.activation(e, e, ACT.Exp, scale=-1.0))
                        act.activation(e, e, ACT.Ln, bias=1.0).then_inc(zln_done, 1)
                    if 4 <= s < 8:
                        i = s - 4
                        act.wait_ge(rot_turned, 4 * layer + i + 1)
                        dst = (qT if i < 2 else kT)[:, 0, :, (i % 2) * P:(i % 2 + 1) * P]
                        copy(dst, A[2 + i % 2][:, :].rearrange("p (h q) -> p h q", h=HEADS)).then_inc(rot_read, 1)
                    if s in (7, 15, 19):
                        b, chunk = ((0, 2), (1, 6), (0, 8))[(7, 15, 19).index(s)]
                        if b == 0 and s == 19:
                            act.wait_ge(ret_out, layer * HEADS + HEADS)
                        act.wait_ge(fox_out, layer * HEADS) if layer and b else None
                        for t in range(NT):
                            ins = copy(val[:, b, t, :], pair(chunk)[t][:, :])
                        ins.then_inc(act_read, 1)
                    if s == 7:
                        act.wait_ge(bend_done, layer + 1)
                        act.wait_ge(rotated, 4 * layer + 4)
                        act.activation(work[:, 0, :], A[0][:, :], ACT.Exp, scale=1.0 / GLA_TAU)
                        act.activation(work[:, 1, :], A[0][:, :], ACT.Exp, scale=-1.0 / GLA_TAU)
                    if s == 8:
                        act.wait_ge(rot_turned, 4 * layer + 3)
                        for i in range(8):
                            act.activation(rot[:, 0, i * 64:(i + 1) * 64], A[0][:, i * 64:(i + 1) * 64], ACT.Exp,
                                           scale=-1.0 / GLA_TAU, bias=bend[:, i:i + 1])
                        act.activation(aend[:, :], bend[:, :], ACT.Exp).then_inc(exp_done, 1)
                    if s in (9, 21):
                        for t in range(NT):
                            ins = act.activation(sgate[:, t, :], pair(3 if s == 9 else 9)[t][:, :], ACT.Silu)
                        ins.then_inc(act_read, 1)
                    if s == 11:
                        for j in range(2):
                            ins = copy(qT[:, 1, 2 * j:2 * j + 2, :], pair(4)[j][:, :].rearrange("p (h q) -> p h q", h=2),
                                       scale=float(HD) ** -0.5)
                        ins.then_inc(act_read, 1)
                    if s == 13:
                        for j in range(2):
                            ins = copy(kT[:, 1, 2 * j:2 * j + 2, :], pair(5)[j][:, :].rearrange("p (h q) -> p h q", h=2))
                        ins.then_inc(act_read, 1)
                    if s == 14:
                        root8(rs[:, 0, :], rs[:, 1, :])
                    if s == 17:
                        for t in range(NT):
                            turn_hi(6 * layer + t + 1, A[2 + t], aT[0][:, 0:4, t * P:(t + 1) * P])
                    if 19 <= s < 19 + HEADS:
                        h = s - 19
                        act.wait_ge(fox_rows, HEADS * layer + h + 1)
                        act.activation(soft[:, h % 2, 0:P], soft[:, h % 2, 0:P], ACT.Exp, bias=nmax[:, 0, h:h + 1],
                                       accum_out=rsum[:, 0, h:h + 1])
                        act.activation(soft[:, h % 2, P:384], soft[:, h % 2, P:384], ACT.Exp, bias=nmax[:, 1, h:h + 1],
                                       accum_out=rsum[:, 1, h:h + 1]).then_inc(fox_exp, 1)
                    if s == 19:
                        act.wait_ge(kend_turned, layer + 1)
                        copy(k_tok, A[0][:, :].rearrange("p (t f) -> p t f", t=2)).then_inc(kend_done, 1)
                    if 20 <= s < 20 + HEADS:
                        h = s - 20
                        act.wait_ge(fox_turned, HEADS * layer + h + 1)
                        copy(att[:, h % 2, :], A[3][:, 0:384]).then_inc(fox_att, 1)
                    if s == 25:
                        for t in range(NT):
                            turn_hi(6 * layer + 2 + t + 1, A[2 + t], aT[0][:, 4:8, t * P:(t + 1) * P])
                    if s == 30:
                        root8(rs[:, 0, :], rs[:, 1, :])
                    if s == 32:
                        for t in range(NT):
                            turn_hi(6 * layer + 4 + t + 1, A[t], aT[0][:, 0:4, t * P:(t + 1) * P])
                    if s >= GATE_S0 + 2 and s < WO_S0 and (s - GATE_S0 - 2) % 3 == 0:
                        j = (s - GATE_S0 - 2) // 3
                        if j or layer:
                            act.wait_ge(merged, N_GB * layer + j)
                        else:
                            act.wait_ge(gla_ops, 1)
                        for t in range(NT):
                            ins = act.activation(work[:, t, :], pair(10 + 2 * j)[t][:, :], ACT.Sigmoid)
                        ins.then_inc(act_read, 1)
                    if s in (37, 40):
                        h = int(s == 40)
                        act.wait_ge(m_turned, 2 * layer + h + 1)
                        for a in range(2):
                            tile = (4, 0)[h] + 2 * a
                            copy(aT[0][:, tile:tile + 2, :],
                                 A[2 * h + a][:, :].rearrange("p (k q) -> p k q", k=2)).then_inc(mT_hi_done, 1)
                    hi(0, g0 + s + 2)

            def dense():
                g0 = FFN_G0

                def silu(f_expr, pair_no):
                    act.activation(work[:, 0, :], M[2 * pair_no][:, :], ACT.Silu).then_inc(f_silu, 1)

                hi(0, g0 + 2)
                act.wait_ge(gran_done, g0 + 1)
                silu(0, 0)
                hi(0, g0 + 3)
                with act.Fori(0, (N_FF - 1) // 2) as j:
                    for u in range(2):
                        f = 1 + 2 * j + u
                        act.wait_ge(gran_done, 6 * j + g0 + 2 + 3 * u)
                        act.wait_ge(f_prod, f)
                        copy(gT[0], work[:, 1, :].rearrange("p (k s) -> p k s", k=4)).then_inc(f_hi, 1)
                        hi(j, g0 + 4 + 3 * u)
                        act.wait_ge(gran_done, 6 * j + g0 + 3 + 3 * u)
                        silu(f, (1 + u) % 2)
                        hi(j, g0 + 5 + 3 * u)
                        hi(j, g0 + 6 + 3 * u)
                act.wait_ge(gran_done, g0 + FFN_G - 1)
                act.wait_ge(f_prod, N_FF)
                copy(gT[0], work[:, 1, :].rearrange("p (k s) -> p k s", k=4)).then_inc(f_hi, 1)
                hi(0, g0 + FFN_G + 1)

            def experts(block):
                e0, n0, six0 = N_EXP * block, (N_EXP + 1) * block, MOE_G0 // 6 + block * N_EXP * N_EF

                def gathered(n):
                    act.wait_ge(e_gather, n)
                    for k in range(KT_D):
                        ins = act.activation(xgT[0][:, k, :], M[2 + k // 4][:, (k % 4) * P:(k % 4 + 1) * P], ACT.Copy,
                                             scale=gain[:, 3, k:k + 1])
                        if k % 4 == 3:
                            ins.then_inc(e_xhi, 1)

                def product_hi(n):
                    act.wait_ge(e_turned, n)
                    copy(gT[0], A[2][:, :].rearrange("p (k s) -> p k s", k=4)).then_inc(e_hi, 1)

                def silu(done):
                    act.wait_ge(gran_done, done)
                    act.activation(work[:, 0, :], M[0][:, :], ACT.Silu).then_inc(e_silu, 1)

                gathered(n0 + 1)
                with act.Fori(0, N_EXP) as e:
                    six = 7 * e + six0
                    for L in range(4):
                        if L == 2:
                            silu(6 * six + 2)
                        hi(six, L + 2)
                    with act.Fori(1, N_EF) as f:
                        six_f = six + f - 1
                        for u in range(6):
                            if u == 0:
                                product_hi(N_EF * e + f + N_EF * e0)
                            if u == 2:
                                silu(6 * six_f + 4 + 2)
                            hi(six_f, 4 + u + 2)
                    product_hi(N_EF * e + N_EF + N_EF * e0)
                    hi(six, 42)
                    gathered(e + 2 + n0)
                    act.wait_ge(e_putw, e + 1 + e0)
                    copy(put_w, A[3][:, 0:SEQ]).then_inc(e_putw_done, 1)
                    hi(six, 43)
                    act.wait_ge(gran_done, 6 * six + 42)
                    copy(y_sb[:, 0, :], A[0][:, :]).then_inc(e_y0, 1)

            hi(0, 0)
            hi(0, 1)
            act.wait_ge(s_const, 64)
            norm(0)
            mixers(0)
            norm(1)
            dense()
            norm(2)
            mixers(1)
            norm(3)
            hi(0, ROUTER_G + 2)
            act.wait_ge(rt_top, 1)
            act.activation(tw[:, 1, :], tw[:, 0, :], ACT.Exp).then_inc(rt_exp, 1)
            experts(0)
            act.wait_ge(rt_flag, 1)
            over = act.value_load(flag[0:1, 0:1], min_val=0, max_val=P)
            with act.If(over > 0):
                experts(1)
            with act.Else():
                act.wait_ge(rt_flag, 1)
            act.wait_ge(fin_sq, 1)
            act.activation(ss[:, 2, :], ss[:, 1, :], ACT.Sqrt).then_inc(fin_sq, 1)

        @block.vector
        def _(dve):
            own = [0]

            def link(ins):
                own[0] += 1
                ins.then_inc(dve_own, 1)
                dve.wait_ge(dve_own, own[0])

            def lo(six, local):
                dve.wait_ge(hi_done, 6 * six + local + 1)
                dve.tensor_tensor(w_lo[:, local % RING, :], raw[:, local % RAW, :],
                                  w_hi[:, local % RING, :].bitcast(f32), ALU.subtract).then_inc(lo_done, 1)

            roots = [0]

            def inverse_root(var, n):
                dve.wait_ge(root_done, roots[0])
                link(dve.reciprocal(n, var))

            def norm(i):
                dve.wait_ge(sumsq, NT * (i + 1))
                roots[0] += 1
                dve.tensor_scalar(ss[:, 1, :], ss[:, 0, :], 1.0 / D, EPS, ALU.mult, ALU.add).then_inc(root_in, 1)
                inverse_root(ss[:, 2, :], ss[:, 0, :])
                for t in range(NT):
                    dve.tensor_scalar(xn[:, t, :], x[:, t, :], ss[:, 0, t:t + 1], None, ALU.mult).then_inc(normed, 1)
                for kp in range(KT_D // 2):
                    dve.wait_ge(hT_hi_done, KT_D * i + 2 * kp + 2)
                    for k in range(2 * kp, 2 * kp + 2):
                        dve.scalar_tensor_tensor(out=hT[1][:, k, :], in0=A[kp][:, (k % 2) * SEQ:(k % 2 + 1) * SEQ],
                                                 scalar=gain[:, i, k:k + 1], in1=hT[0][:, k, :].bitcast(f32),
                                                 op0=ALU.mult, op1=ALU.subtract).then_inc(hT_done, 1)

            def add_to_x(banks, n):
                for t in range(NT):
                    for c in range(2):
                        ins = dve.tensor_tensor(x[:, t, c * 512:(c + 1) * 512], banks[t][c][:, :],
                                                x[:, t, c * 512:(c + 1) * 512], ALU.add)
                    ins.then_inc(x_new, 1)

            def rotate(i, chunk, t):
                src = pair(chunk)[t]
                v = src[:, :].rearrange("p (h u i) -> p h u i", h=HEADS, u=2)
                w1 = work[:, 1, :].rearrange("p (h u i) -> p h u i", h=HEADS, u=2)
                dve.tensor_tensor(work[:, 0, :].rearrange("p (a i) -> p a i", i=64),
                                  src[:, :].rearrange("p (a i) -> p a i", i=64),
                                  cos[:, t:t + 1, :].to_broadcast([P, 8, 64]), ALU.mult)
                for u in range(2):
                    ins = dve.tensor_tensor(w1[:, :, u, :], v[:, :, 1 - u, :],
                                            sin[:, t, u:u + 1, :].to_broadcast([P, HEADS, 64]), ALU.mult)
                if t == NT - 1:
                    link_read(ins)
                else:
                    link(ins)
                if i >= 2:
                    dve.wait_ge(rot_turned, 4 * layer_no[0] + i - 1)
                dve.tensor_tensor(rot[:, t, :], work[:, 0, :], work[:, 1, :], ALU.add).then_inc(rotated, 1)
                dve.wait_ge(rotated, 4 * layer_no[0] + i + 1)

            layer_no = [0]
            n_read = [0]

            def link_read(ins):
                n_read[0] += 1
                ins.then_inc(dve_read, 1)
                dve.wait_ge(dve_read, n_read[0])

            def head_stats(result, centred):
                for t in range(NT):
                    for h in range(HEADS):
                        ins = dve.bn_stats(stats[:, 4 * t + h, :], result(t, h))
                link(ins)
                for i in range(8):
                    ins = dve.bn_aggr(mv[:, i, :], stats[:, i, :])
                link(ins)
                roots[0] += 1
                if centred:
                    dve.tensor_scalar(rs[:, 0, :], mv[:, :, 1], EPS, None, ALU.add).then_inc(root_in, 1)
                else:
                    link(dve.tensor_tensor(rs[:, 2, :], mv[:, :, 0], mv[:, :, 0], ALU.mult))
                    dve.scalar_tensor_tensor(out=rs[:, 0, :], in0=mv[:, :, 1], scalar=EPS, in1=rs[:, 2, :],
                                             op0=ALU.add, op1=ALU.add).then_inc(root_in, 1)

            def turn_lo(n, bank, hi_part, dst):
                dve.wait_ge(oT_hi_done, n)
                dve.tensor_tensor(dst, bank[:, :].rearrange("p (h q) -> p h q", h=HEADS), hi_part.bitcast(f32),
                                  ALU.subtract).then_inc(oT_done, 1)

            def mixers(layer):
                g0 = LAYER_G0[layer]
                layer_no[0] = layer
                zf, ef = att[32:36, 0, 0:SEQ], att[32:36, 1, 0:SEQ]
                for s in range(MIX_G):
                    if s > 0:
                        dve.wait_ge(gran_done, g0 + s)
                    if s == 1:
                        dve.tensor_scalar(zf, A[0][32:36, 0:SEQ], bf[32:36, layer:layer + 1], None,
                                          ALU.add).then_inc(fz_done, 1)
                    if s == 3:
                        dve.wait_ge(fln_done, layer + 1)
                        link(dve.scalar_tensor_tensor(out=ef, in0=zf, scalar=0.0, in1=ef, op0=ALU.min, op1=ALU.subtract))
                        cT = soft[32:36, 0, 0:SEQ]
                        link(dve.tensor_tensor_scan(cT, ones[32:36, 0:1].to_broadcast([HEADS, SEQ]), ef, 0.0,
                                                    ALU.mult, ALU.add))
                        dve.tensor_scalar(ncT[32:36, :], cT, -1.0, None, ALU.mult).then_inc(c_done, 1)
                    if 3 <= s < 7:
                        i = s - 3
                        rotate(i, i // 2, i % 2)
                    if s == 4:
                        dve.wait_ge(zln_done, layer + 1)
                        dve.scalar_tensor_tensor(out=o[:, 1, :], in0=A[1][:, :], scalar=0.0, in1=o[:, 0, :],
                                                 op0=ALU.min, op1=ALU.subtract).then_inc(loga_done, 1)
                    if s == 6:
                        dve.wait_ge(cum_done, layer + 1)
                        dve.tensor_scalar(bend[:, :], A[0][:, :].rearrange("p (b i) -> p b i", i=64)[:, :, 63],
                                          1.0 / GLA_TAU, None, ALU.mult).then_inc(bend_done, 1)
                        dve.tensor_copy(cq[:, :], A[1][:, 0:8]).then_inc(cq_done, 1)
                    if 9 <= s < 9 + HEADS:
                        h = s - 9
                        dve.wait_ge(ret_scores, HEADS * layer + h + 1)
                        if h >= 2:
                            dve.wait_ge(ret_out, HEADS * layer + h - 1)
                        src = A[2 + h % 2]
                        dve.tensor_tensor(att[:, h % 2, 0:SEQ], src[:, 0:SEQ], decay[:, h, :], ALU.mult)
                        dve.tensor_tensor(att[:, h % 2, SEQ:384], src[:, SEQ:384], decay[:, h, 0:P],
                                          ALU.mult).then_inc(ret_att, 1)
                    if s == 13:
                        dve.wait_ge(ret_out, HEADS * layer + HEADS)
                        head_stats(by_tile, True)
                    if s == 15:
                        dve.wait_ge(act_read, reads("act", layer, 3))
                        inverse_root(rs[:, 1, :], rs[:, 2, :])
                        for t in range(NT):
                            for h in range(HEADS):
                                i = 4 * t + h
                                ins = dve.tensor_scalar(o[:, t, h * HD:(h + 1) * HD], A[t][:, h * HD:(h + 1) * HD],
                                                        mv[:, i, 0:1], rs[:, 2, i:i + 1], ALU.subtract, ALU.mult)
                        link(ins)
                        for t in range(NT):
                            ins = dve.tensor_tensor(o[:, t, :], o[:, t, :], sgate[:, t, :], ALU.mult)
                        ins.then_inc(o_done, 1)
                    if s == 17:
                        dve.wait_ge(exp_done, layer + 1)
                        bq, bk = pair(7)
                        dve.scalar_tensor_tensor(out=q_dec, in0=bq[:, :].rearrange("p (f q) -> p f q", f=2),
                                                 scalar=float(GLA_DK) ** -0.5,
                                                 in1=work[:, 0, :].rearrange("p (f q) -> p f q", f=2),
                                                 op0=ALU.mult, op1=ALU.mult)
                        dve.tensor_tensor(k_inv, bk[:, :].rearrange("p (f q) -> p f q", f=2),
                                          work[:, 1, :].rearrange("p (f q) -> p f q", f=2), ALU.mult)
                        n_read[0] += 1
                        dve.tensor_tensor(k_end, bk[:, :].rearrange("p (f q) -> p f q", f=2),
                                          rot[:, 0, :].rearrange("p (f q) -> p f q", f=2), ALU.mult).then_inc(dve_read, 1)
                        for t in range(NT):
                            turn_lo(6 * layer + t + 1, A[2 + t], aT[0][:, 0:4, t * P:(t + 1) * P],
                                    aT[1][:, 0:4, t * P:(t + 1) * P])
                        dve.wait_ge(dve_read, n_read[0])
                        dve.tensor_copy(flagf[:, 0:1], bend[:, 0:1]).then_inc(gla_ops, 1)
                    if 18 <= s < 18 + HEADS:
                        h = s - 18
                        dve.wait_ge(fox_scores, HEADS * layer + h + 1)
                        if h >= 2:
                            dve.wait_ge(fox_turned, HEADS * layer + h - 1)
                        row = soft[:, h % 2, :]
                        dve.scalar_tensor_tensor(out=row[:, 0:P], in0=A[2][:, 0:P], scalar=cq[:, h:h + 1], in1=causal,
                                                 op0=ALU.add, op1=ALU.add)
                        dve.tensor_scalar(row[:, P:2 * P], A[2][:, P:2 * P], cq[:, 4 + h:5 + h], None, ALU.add)
                        link(dve.scalar_tensor_tensor(out=row[:, 2 * P:384], in0=A[2][:, 2 * P:384],
                                                      scalar=cq[:, 4 + h:5 + h], in1=causal, op0=ALU.add, op1=ALU.add))
                        dve.tensor_reduce(nmax[:, 0, h:h + 1], row[:, 0:P], AX.X, ALU.max, negate=True)
                        dve.tensor_reduce(nmax[:, 1, h:h + 1], row[:, P:384], AX.X, ALU.max,
                                          negate=True).then_inc(fox_rows, 1)
                    if s == 20:
                        dve.wait_ge(kv_done, 2 * layer + 1)
                        for c in range(2):
                            for f in range(2):
                                for half in range(2):
                                    p0 = 64 * half
                                    kv = A[c][p0:p0 + 64, f * SEQ + half * P:f * SEQ + (half + 1) * P]
                                    if c == 0:
                                        ins = dve.tensor_copy(states[p0:p0 + 64, f, 0, :], kv)
                                    else:
                                        ins = dve.scalar_tensor_tensor(
                                            out=states[p0:p0 + 64, f, 1, :], in0=states[p0:p0 + 64, f, 0, :],
                                            scalar=aend[p0:p0 + 64, 4 * f + 1:4 * f + 2], in1=kv,
                                            op0=ALU.mult, op1=ALU.add)
                            if c == 0:
                                link(ins)
                        ins.then_inc(state_done, 1)
                    if s == 24:
                        dve.wait_ge(fox_out, HEADS * layer + HEADS)
                        dve.wait_ge(fox_exp, HEADS * layer + HEADS)
                        link(dve.reciprocal(rs[:, 3, :], rsum[:, :, :].rearrange("p t h -> p (t h)")))
                        for t in range(NT):
                            for h in range(HEADS):
                                ins = dve.tensor_scalar(o[:, t, h * HD:(h + 1) * HD], A[t][:, h * HD:(h + 1) * HD],
                                                        rs[:, 3, 4 * t + h:4 * t + h + 1], None, ALU.mult)
                        ins.then_inc(o_done, 1)
                    if s == 25:
                        for t in range(NT):
                            turn_lo(6 * layer + 2 + t + 1, A[2 + t], aT[0][:, 4:8, t * P:(t + 1) * P],
                                    aT[1][:, 4:8, t * P:(t + 1) * P])
                        dve.memset(gsc, 0.0).then_inc(ready0, 1)
                    if s == 26:
                        dve.wait_ge(kv_done, 2 * layer + 2)
                        for f in range(2):
                            for half in range(2):
                                p0 = 64 * half
                                ins = dve.scalar_tensor_tensor(
                                    out=states[p0:p0 + 64, f, 2, :], in0=states[p0:p0 + 64, f, 1, :],
                                    scalar=aend[p0:p0 + 64, 4 * f + 2:4 * f + 3],
                                    in1=A[0][p0:p0 + 64, f * SEQ + half * P:f * SEQ + (half + 1) * P],
                                    op0=ALU.mult, op1=ALU.add)
                        ins.then_inc(state_done, 1)
                    if s in (27, 28):
                        t = s - 27
                        dve.wait_ge(gla_scores, 2 * layer + 2)
                        dve.wait_ge(ready0, layer + 1)
                        if t:
                            dve.wait_ge(gla_out, 2 * layer + 1)
                        for h in range(HEADS):
                            ins = dve.copy_predicated(gsc[:, h * P:(h + 1) * P], chunk_tri.bitcast(i32),
                                                      A[1 - h % 2][:, (h // 2 * 2 + t) * P:(h // 2 * 2 + t + 1) * P])
                        ins.then_inc(gla_att, 1)
                    if s == 29:
                        dve.wait_ge(gla_out, 2 * layer + 2)
                        head_stats(gla_result, False)
                    if s == 31:
                        dve.wait_ge(act_read, reads("act", layer, 9))
                        inverse_root(rs[:, 1, :], rs[:, 2, :])
                        for t in range(NT):
                            for h in range(HEADS):
                                ins = dve.scalar_tensor_tensor(
                                    out=o[:, t, h * HD:(h + 1) * HD], in0=gla_result(t, h),
                                    scalar=rs[:, 2, 4 * t + h:4 * t + h + 1], in1=sgate[:, t, h * HD:(h + 1) * HD],
                                    op0=ALU.mult, op1=ALU.mult)
                        ins.then_inc(o_done, 1)
                    if s == 32:
                        for t in range(NT):
                            turn_lo(6 * layer + 4 + t + 1, A[t], aT[0][:, 0:4, t * P:(t + 1) * P],
                                    aT[1][:, 0:4, t * P:(t + 1) * P])
                    if s >= GATE_S0 + 3 and s <= WO_S0 and (s - GATE_S0) % 3 == 0:
                        j = (s - GATE_S0 - 3) // 3
                        c = (j % 2) * 512
                        dve.wait_ge(act_read, reads("act", layer, 10 + 2 * j))
                        dst = [xn[:, t, c:c + 512] if j < 2 else work[:, t, :] for t in range(NT)]
                        for t in range(NT):
                            ins = dve.tensor_tensor(dst[t], pair(11 + 2 * j)[t][:, :], work[:, t, :], ALU.mult)
                        link_read(ins)
                        if j < 2:
                            dve.tensor_copy(flagf[:, 0:1], bend[:, 0:1]).then_inc(merged, 1)
                        else:
                            for t in range(NT):
                                ins = dve.tensor_tensor(xn[:, t, c:c + 512], xn[:, t, c:c + 512], work[:, t, :], ALU.add)
                            ins.then_inc(merged, 1)
                            dve.wait_ge(merged, N_GB * layer + j + 1)
                    if s in (37, 40):
                        h = int(s == 40)
                        for a in range(2):
                            tile = (4, 0)[h] + 2 * a
                            dve.wait_ge(mT_hi_done, 4 * layer + 2 * h + a + 1)
                            dve.tensor_tensor(aT[1][:, tile:tile + 2, :],
                                              A[2 * h + a][:, :].rearrange("p (k q) -> p k q", k=2),
                                              aT[0][:, tile:tile + 2, :].bitcast(f32), ALU.subtract).then_inc(mT_done, 1)
                    lo(0, g0 + s + 2)
                dve.wait_ge(gran_done, g0 + MIX_G)
                add_to_x([[pair(22)[t], pair(23)[t]] for t in range(NT)], layer)

            def dense():
                g0 = FFN_G0

                def product(f1, pair_no):
                    dve.wait_ge(f_silu, f1)
                    dve.tensor_tensor(work[:, 1, :], M[2 * pair_no + 1][:, :], work[:, 0, :], ALU.mult).then_inc(f_prod, 1)

                def product_lo(f1):
                    dve.wait_ge(f_hi, f1)
                    dve.tensor_tensor(gT[1], work[:, 1, :].rearrange("p (k s) -> p k s", k=4), gT[0].bitcast(f32),
                                      ALU.subtract).then_inc(f_lo, 1)

                lo(0, g0 + 2)
                lo(0, g0 + 3)
                dve.wait_ge(gran_done, g0 + 2)
                product(1, 0)
                with dve.Fori(0, (N_FF - 1) // 2) as j:
                    for u in range(2):
                        f = 1 + 2 * j + u
                        product_lo(f)
                        lo(j, g0 + 4 + 3 * u)
                        lo(j, g0 + 5 + 3 * u)
                        dve.wait_ge(gran_done, 6 * j + g0 + 4 + 3 * u)
                        dve.wait_ge(f_lo, f)
                        product(f + 1, (1 + u) % 2)
                        lo(j, g0 + 6 + 3 * u)
                product_lo(N_FF)
                lo(0, g0 + FFN_G + 1)
                dve.wait_ge(gran_done, g0 + FFN_G)
                add_to_x([[A[2 * t], A[2 * t + 1]] for t in range(NT)], 1)

            def router():
                lo(0, ROUTER_G + 2)
                dve.wait_ge(gran_done, ROUTER_G + 1)
                dve.tensor_copy(lgT[:, :], A[0][0:8, 0:SEQ]).then_inc(rt_copied, 1)
                dve.wait_ge(rt_turned, 1)
                link(dve.tensor_copy(lg[:, :, :], A[1][:, 0:16].rearrange("p (t e) -> p t e", t=NT)))
                for t in range(NT):
                    link(dve.max(top[:, t, :], lg[:, t, :]))
                    link(dve.max_index(topi[:, t, :], top[:, t, :], lg[:, t, :]))
                dve.tensor_tensor(tw[:, 0, :], top[:, :, 1], top[:, :, 0], ALU.subtract).then_inc(rt_top, 1)
                link(dve.tensor_copy(topf[:, :, :], topi[:, :, :]))
                dve.wait_ge(rt_exp, 1)
                link(dve.tensor_scalar(tw[:, 0, :], tw[:, 1, :], 1.0, None, ALU.add))
                link(dve.reciprocal(tw[:, 2, :], tw[:, 0, :]))
                link(dve.tensor_tensor(tw[:, 1, :], tw[:, 1, :], tw[:, 2, :], ALU.mult))
                for a in (comb, rank, picked):
                    ins = dve.memset(a[:, :, :], 0.0)
                link(ins)
                e8 = iota[:, 0:N_EXP]
                for t in range(NT):
                    dve.tensor_scalar(comb[:, t, 0:N_EXP], e8, topf[:, t, 0:1], tw[:, 2, t:t + 1], ALU.is_equal, ALU.mult)
                    dve.tensor_scalar(lg[:, t, :], e8, topf[:, t, 1:2], tw[:, 1, t:t + 1], ALU.is_equal, ALU.mult)
                    link(dve.tensor_scalar(picked[:, t, 0:N_EXP], e8, topf[:, t, 0:1], None, ALU.is_equal))
                    dve.tensor_tensor(comb[:, t, 0:N_EXP], comb[:, t, 0:N_EXP], lg[:, t, :], ALU.add)
                    ins = dve.scalar_tensor_tensor(out=picked[:, t, 0:N_EXP], in0=e8, scalar=topf[:, t, 1:2],
                                                   in1=picked[:, t, 0:N_EXP], op0=ALU.is_equal, op1=ALU.add)
                ins.then_inc(rt_picked, 1)
                dve.wait_ge(rt_ranked, 1)
                for t in range(NT):
                    ins = dve.tensor_copy(rank[:, t, 0:N_EXP], A[2][:, 8 * t:8 * t + 8])
                link(dve.tensor_reduce(flagf[:, :], A[2][:, 16:24], AX.X, ALU.max))
                link(dve.tensor_scalar(flagf[:, :], flagf[:, :], -float(P), 0.0, ALU.add, ALU.max))
                dve.tensor_copy(flag[:, :], flagf[:, :]).then_inc(rt_flag, 1)
                dve.wait_ge(rt_flag, 1)

            def experts(block):
                e0, n0, six0 = N_EXP * block, (N_EXP + 1) * block, MOE_G0 // 6 + block * N_EXP * N_EF

                def pick_matrix(dst, weight, e):
                    for t in range(NT):
                        ins = dve.tensor_scalar(dst[:, t, :], iota, rank[:, t, bass.ds(e, 1)],
                                                weight[:, t, bass.ds(e, 1)], ALU.is_equal, ALU.mult)
                    return ins

                def gathered(n):
                    for k in range(KT_D):
                        if k % 4 == 0:
                            dve.wait_ge(e_xhi, 2 * n - 1 + k // 4)
                        ins = dve.scalar_tensor_tensor(out=xgT[1][:, k, :], in0=M[2 + k // 4][:, (k % 4) * P:(k % 4 + 1) * P],
                                                       scalar=gain[:, 3, k:k + 1], in1=xgT[0][:, k, :].bitcast(f32),
                                                       op0=ALU.mult, op1=ALU.subtract)
                    ins.then_inc(e_xlo, 1)

                def product_lo(n):
                    dve.wait_ge(e_hi, n)
                    dve.tensor_tensor(gT[1], A[2][:, :].rearrange("p (k s) -> p k s", k=4), gT[0].bitcast(f32),
                                      ALU.subtract).then_inc(e_lo, 1)

                def product(n, done):
                    dve.wait_ge(gran_done, done)
                    dve.wait_ge(e_silu, n)
                    dve.tensor_tensor(work[:, 1, :], M[1][:, :], work[:, 0, :], ALU.mult).then_inc(e_prod, 1)

                if block:
                    dve.tensor_scalar(rank[:, :, :], rank[:, :, :], -float(P), None, ALU.add).then_inc(e_moved, 1)
                    dve.wait_ge(e_moved, 1)
                else:
                    dve.memset(flagf[:, :], 0.0).then_inc(e_added, 1)
                pick_matrix(pick, picked, 0).then_inc(e_pick, 1)
                gathered(n0 + 1)
                with dve.Fori(0, N_EXP) as e:
                    six = 7 * e + six0
                    for L in range(4):
                        lo(six, L + 2)
                    product(N_EF * e + 1 + N_EF * e0, 6 * six + 4)
                    pick_matrix(pick, picked, e + 1).then_inc(e_pick, 1)
                    pick_matrix(pick_w, comb, e).then_inc(e_pickw, 1)
                    with dve.Fori(1, N_EF) as f:
                        six_f = six + f - 1
                        for u in range(6):
                            if u == 0:
                                product_lo(N_EF * e + f + N_EF * e0)
                            if u == 4:
                                product(N_EF * e + f + 1 + N_EF * e0, 6 * six_f + 8)
                            lo(six_f, 4 + u + 2)
                    product_lo(N_EF * e + N_EF + N_EF * e0)
                    lo(six, 42)
                    gathered(e + 2 + n0)
                    lo(six, 43)
                    dve.wait_ge(gran_done, 6 * six + 42)
                    dve.tensor_copy(y_sb[:, 1, :], A[1][:, :]).then_inc(e_y1, 1)
                    for i, bank in enumerate((M[2], M[3], A[3], A[2])):
                        t, c = i // 2, (i % 2) * 512
                        dve.wait_ge(e_scatter, 4 * e + i + 1 + 4 * e0)
                        ins = dve.tensor_tensor(x[:, t, c:c + 512], bank[:, :], x[:, t, c:c + 512], ALU.add)
                    ins.then_inc(e_added, 1)
                    dve.wait_ge(e_added, e + 2 + e0)

            dve.memset(gaT[:, :], 1.0).then_inc(ready0, 0) if False else link(dve.memset(gaT[:, :], 1.0))
            dve.wait_ge(s_const, 64)
            lo(0, 0)
            lo(0, 1)
            norm(0)
            mixers(0)
            norm(1)
            dense()
            norm(2)
            mixers(1)
            norm(3)
            router()
            experts(0)
            over = dve.value_load(flag[0:1, 0:1], min_val=0, max_val=P)
            with dve.If(over > 0):
                experts(1)
            with dve.Else():
                dve.wait_ge(rt_flag, 1)
            for t in range(NT):
                ins = dve.tensor_tensor_reduce(xn[:, t, :], x[:, t, :], x[:, t, :], 1.0, 0.0, ALU.mult, ALU.add,
                                               ss[:, 0, t:t + 1])
            link(ins)
            dve.tensor_scalar(ss[:, 1, :], ss[:, 0, :], 1.0 / D, EPS, ALU.mult, ALU.add).then_inc(fin_sq, 1)
            dve.wait_ge(fin_sq, 2)
            link(dve.reciprocal(ss[:, 0, :], ss[:, 2, :]))
            dve.wait_ge(s_const, 80)
            for t in range(NT):
                dve.scalar_tensor_tensor(out=xn[:, t, :], in0=x[:, t, :], scalar=ss[:, 0, t:t + 1], in1=gfin,
                                         op0=ALU.mult, op1=ALU.mult).then_inc(fin_done, 1)

        @block.tensor
        def _(pe):
            def mm3(dst, stat, mov, start, stop):
                pe.matmul(dst, stat[0], mov[0], start=start, stop=False, skip_group_check=True)
                pe.matmul(dst, stat[0], mov[1], start=False, stop=False, skip_group_check=True)
                return pe.matmul(dst, stat[1], mov[0], start=False, stop=stop, skip_group_check=True)

            def weights(local, a, b):
                return w_hi[:, local % RING, a:b], w_lo[:, local % RING, a:b]

            def both(tile, k, a, b):
                return tile[0][:, k, a:b], tile[1][:, k, a:b]

            def arrived(six, local):
                pe.wait_ge(lo_done, 6 * six + local + 1)

            def rows_product(local, banks, source, k0, first, last):
                for t in range(len(banks)):
                    for k in range(4):
                        ins = mm3(banks[t][:, :], both(source, k0 + k, t * P, (t + 1) * P),
                                  weights(local, k * 512, (k + 1) * 512), first and k == 0, last and k == 3)
                ins.then_inc(gran_done, 1)

            def feature_product(local, banks, half):
                for ft in range(4):
                    for k in range(4):
                        a = k * 512 + ft * P
                        ins = mm3(banks[ft // 2][:, (ft % 2) * SEQ:(ft % 2 + 1) * SEQ], weights(local, a, a + P),
                                  both(hT, 4 * half + k, 0, SEQ), half == 0 and k == 0 and ft % 2 == 0,
                                  half == 1 and k == 3)
                ins.then_inc(gran_done, 1)

            def narrow_product(local):
                for k in range(KT_D):
                    ins = mm3(A[0][:, 0:SEQ], weights(local, k * 256, k * 256 + P), both(hT, k, 0, SEQ),
                              k == 0, k == KT_D - 1)
                ins.then_inc(gran_done, 1)

            def norm(i):
                for kp in range(KT_D // 2):
                    for k in range(2 * kp, 2 * kp + 2):
                        for t in range(NT):
                            if kp == 0 and k == 0:
                                pe.wait_ge(normed, NT * i + t + 1)
                            at = (k % 2) * SEQ + t * P
                            ins = pe.transpose(A[kp][:, at:at + P], xn[:, t, k * P:(k + 1) * P], ident)
                    ins.then_inc(x_turned, 1)

            def turn_tokens(src, bank):
                for h in range(HEADS):
                    ins = pe.transpose(bank[:, h * P:(h + 1) * P], src[:, h * P:(h + 1) * P], ident)
                return ins

            def head_out(h, b, att_h):
                v = val[:, b, :, h * HD:(h + 1) * HD]
                dst = slice(h * HD, (h + 1) * HD)
                pe.matmul(A[0][:, dst], att_h[:, 0:P], v[:, 0, :], start=True, stop=True)
                pe.matmul(A[1][:, dst], att_h[:, P:2 * P], v[:, 0, :], start=True, stop=False)
                return pe.matmul(A[1][:, dst], att_h[:, 2 * P:384], v[:, 1, :], start=False, stop=True)

            def mixers(layer):
                g0 = LAYER_G0[layer]
                for s in range(MIX_G):
                    arrived(0, g0 + s)
                    if s == 0:
                        pe.wait_ge(hT_done, KT_D * (2 * layer + 1))
                        narrow_product(g0)
                    elif s < GATE_S0:
                        chunk, half = (s - 1) // 2, (s - 1) % 2
                        if half == 0 and chunk >= 2:
                            wait_read(pe, layer, chunk - 2)
                        if CHUNKS[chunk][0] in BY_FEATURE:
                            feature_product(g0 + s, pair(chunk), half)
                        else:
                            rows_product(g0 + s, pair(chunk), hT, 4 * half, half == 0, half == 1)
                    elif s < WO_S0:
                        j, part = (s - GATE_S0) // 3, (s - GATE_S0) % 3
                        chunk = 10 + 2 * j + (part == 2)
                        if part != 1:
                            wait_read(pe, layer, chunk - 2)
                        if part < 2:
                            rows_product(g0 + s, pair(chunk), hT, 4 * part, part == 0, part == 1)
                        else:
                            b = j // 2
                            pe.wait_ge(oT_done, 6 * layer + 2 * b + 2)
                            rows_product(g0 + s, pair(chunk), aT, AT_TILE[BRANCH_ORDER[b]], True, True)
                    else:
                        half, n = (s - WO_S0) // 2, (s - WO_S0) % 2
                        if half == 0:
                            wait_read(pe, layer, 20 + n)
                        pe.wait_ge(mT_done, 4 * layer + 2 * half + 2)
                        rows_product(g0 + s, pair(22 + n), aT, (4, 0)[half], half == 0, half == 1)

                    if s == 1:
                        pe.wait_ge(ga_done, layer + 1)
                        for t in range(NT):
                            ins = pe.matmul(A[1][:, t * 256:(t + 1) * 256], gaT[0:GLA_RANK + 1, t * P:(t + 1) * P],
                                            a2[:, layer, :], start=True, stop=True)
                        ins.then_inc(z_done, 1)
                    if 3 <= s < 7:
                        i = s - 3
                        pe.wait_ge(rotated, 4 * layer + i + 1)
                        if i >= 2:
                            pe.wait_ge(rot_read, 4 * layer + i - 1)
                        turn_tokens(rot[:, i % 2, :], A[2 + i % 2]).then_inc(rot_turned, 1)
                    if s == 5:
                        pe.wait_ge(loga_done, layer + 1)
                        pe.wait_ge(fz_done, layer + 1)
                        for f in range(2):
                            for t in range(NT):
                                ins = pe.matmul(A[0][:, (2 * f + t) * P:(2 * f + t + 1) * P],
                                                o[:, 1, t * 256 + f * P:t * 256 + (f + 1) * P], chunk_tri,
                                                start=True, stop=True)
                        pe.wait_ge(c_done, layer + 1)
                        for t in range(NT):
                            ins = pe.transpose(A[1][:, 4 * t:4 * t + 4], soft[32:36, 0, t * P:(t + 1) * P],
                                               ident[32:36, 32:36])
                        ins.then_inc(cum_done, 1)
                    if 8 <= s < 8 + HEADS:
                        h = s - 8
                        if h == 0:
                            pe.wait_ge(rot_read, 4 * layer + 4)
                        if h >= 2:
                            pe.wait_ge(ret_att, HEADS * layer + h - 1)
                        bank = A[2 + h % 2]
                        pe.matmul(bank[:, 0:SEQ], kT[:, 0, h, 0:P], qT[:, 0, h, :], start=True, stop=True)
                        pe.matmul(bank[:, SEQ:384], kT[:, 0, h, P:SEQ], qT[:, 0, h, P:SEQ], start=True,
                                  stop=True).then_inc(ret_scores, 1)
                    if 9 <= s < 9 + HEADS:
                        h = s - 9
                        if h == 0:
                            pe.wait_ge(exp_done, layer + 1)
                            pe.wait_ge(cq_done, layer + 1)
                            pe.wait_ge(act_read, reads("act", layer, 2))
                        pe.wait_ge(ret_att, HEADS * layer + h + 1)
                        head_out(h, 0, att[:, h % 2, :]).then_inc(ret_out, 1)
                    if s == 16:
                        pe.wait_ge(o_done, 3 * layer + 1)
                        for t in range(NT):
                            turn_tokens(o[:, t, :], A[2 + t]).then_inc(o_turned, 1)
                    if 17 <= s < 17 + HEADS:
                        h = s - 17
                        if h == 0:
                            pe.wait_ge(oT_done, 6 * layer + 2)
                            pe.wait_ge(act_read, reads("act", layer, 5))
                        else:
                            pe.wait_ge(fox_rows, HEADS * layer + h)
                        for t in range(NT):
                            dst = A[2][:, t * P:t * P + (t + 1) * P]
                            pe.matmul(dst, qT[:, 1, h, t * P:(t + 1) * P], kT[:, 1, h, 0:(t + 1) * P],
                                      start=True, stop=False)
                            ins = pe.matmul(dst, ident[32:36, 32 + h:33 + h].to_broadcast([HEADS, P]),
                                            ncT[32:36, 0:(t + 1) * P], start=False, stop=True)
                        ins.then_inc(fox_scores, 1)
                    if s == 18:
                        pe.wait_ge(gla_ops, layer + 1)
                        for t in range(NT):
                            for f in range(2):
                                ins = pe.transpose(A[0][:, (2 * t + f) * P:(2 * t + f + 1) * P],
                                                   k_end[:, f, t * P:(t + 1) * P], ident)
                        ins.then_inc(kend_turned, 1)
                    if s == 19:
                        pe.wait_ge(kend_done, layer + 1)
                        pe.wait_ge(act_read, reads("act", layer, 8))
                        for f in range(2):
                            for c in range(2):
                                p0 = 64 * c
                                ins = pe.matmul(A[c][:, f * SEQ:(f + 1) * SEQ], k_tok[p0:p0 + 64, 0, f * P:(f + 1) * P],
                                                val[p0:p0 + 64, 0, 0, f * SEQ:(f + 1) * SEQ], start=True, stop=True)
                        ins.then_inc(kv_done, 1)
                    if 19 <= s < 19 + HEADS:
                        h = s - 19
                        pe.wait_ge(fox_exp, HEADS * layer + h + 1)
                        if h >= 1:
                            pe.wait_ge(fox_att, HEADS * layer + h)
                        for i in range(3):
                            ins = pe.transpose(A[3][:, i * P:(i + 1) * P], soft[:, h % 2, i * P:(i + 1) * P], ident)
                        ins.then_inc(fox_turned, 1)
                    if 20 <= s < 20 + HEADS:
                        h = s - 20
                        if h == 0:
                            pe.wait_ge(state_done, 2 * layer + 1)
                        pe.wait_ge(fox_att, HEADS * layer + h + 1)
                        head_out(h, 1, att[:, h % 2, :]).then_inc(fox_out, 1)
                    if s == 24:
                        pe.wait_ge(o_done, 3 * layer + 2)
                        for t in range(NT):
                            turn_tokens(o[:, t, :], A[2 + t]).then_inc(o_turned, 1)
                    if s == 25:
                        p0 = 0
                        for f in range(2):
                            ins = pe.matmul(A[0][:, f * SEQ:(f + 1) * SEQ], k_tok[p0:p0 + 64, 1, f * P:(f + 1) * P],
                                            val[p0:p0 + 64, 0, 1, f * SEQ:(f + 1) * SEQ], start=True, stop=True)
                        ins.then_inc(kv_done, 1)
                    if s in (27, 28):
                        t = s - 27
                        if t == 0:
                            pe.wait_ge(oT_done, 6 * layer + 4)
                        pe.wait_ge(state_done, 2 * layer + 1 + t)
                        pe.wait_ge(gla_att, 2 * layer + t + 1)
                        for h in range(HEADS):
                            f, p0 = h // 2, 64 * (h % 2)
                            out_h = gla_result(t, h)
                            pe.matmul(out_h, gsc[:, h * P:(h + 1) * P],
                                      val[:, 0, t, h * HD:(h + 1) * HD], start=True, stop=False, skip_group_check=True)
                            for c in range(2):
                                if 2 * t + c:
                                    ins = pe.matmul(out_h[64 * c:64 * c + 64, :],
                                                    q_dec[p0:p0 + 64, f, t * P + 64 * c:t * P + 64 * c + 64],
                                                    states[p0:p0 + 64, f, 2 * t + c - 1, :], start=False, stop=c == 1,
                                                    skip_group_check=True)
                        ins.then_inc(gla_out, 1)
                    if s in (25, 26):
                        odd = s - 25
                        if odd:
                            pe.wait_ge(state_done, 2 * layer + 2)
                        for f in range(2):
                            for t in range(NT):
                                p0 = 64 * odd
                                ins = pe.matmul(A[1 - odd][:, (2 * f + t) * P:(2 * f + t + 1) * P],
                                                k_inv[p0:p0 + 64, f, t * P:(t + 1) * P],
                                                q_dec[p0:p0 + 64, f, t * P:(t + 1) * P], start=True, stop=True)
                        ins.then_inc(gla_scores, 1)
                    if s == 31:
                        pe.wait_ge(o_done, 3 * layer + 3)
                        for t in range(NT):
                            turn_tokens(o[:, t, :], A[t]).then_inc(o_turned, 1)
                    if s in (36, 39):
                        h = int(s == 39)
                        pe.wait_ge(merged, N_GB * layer + 5 + h)
                        for a in range(2):
                            for k in range(2):
                                for t in range(NT):
                                    at = (4 * h + 2 * a + k) * P
                                    ins = pe.transpose(A[2 * h + a][:, k * SEQ + t * P:k * SEQ + (t + 1) * P],
                                                       xn[:, t, at:at + P], ident)
                        ins.then_inc(m_turned, 1)

            def dense():
                g0 = FFN_G0

                def hidden(six, local, bank):
                    arrived(six, local)
                    for ft in range(2):
                        for k in range(KT_D):
                            a = k * FF + ft * P
                            ins = mm3(bank[:, ft * SEQ:(ft + 1) * SEQ], weights(local, a, a + P), both(hT, k, 0, SEQ),
                                      k == 0 and ft == 0, k == KT_D - 1)
                    ins.then_inc(gran_done, 1)

                def back(six, local, n, first, last):
                    arrived(six, local)
                    pe.wait_ge(f_lo, n)
                    for t in range(NT):
                        for k in range(2):
                            for c in range(2):
                                stat = (gT[0][:, 2 * k + t, :], gT[1][:, 2 * k + t, :])
                                ins = mm3(A[2 * t + c][:, :], stat, weights(local, k * D + c * 512, k * D + (c + 1) * 512),
                                          first and k == 0, last and k == 1)
                    ins.then_inc(gran_done, 1)

                pe.wait_ge(hT_done, KT_D * 2)
                hidden(0, g0, M[0])
                hidden(0, g0 + 1, M[1])
                for first in (True, False):
                    if first:
                        hidden(0, g0 + 2, M[2])
                        hidden(0, g0 + 3, M[3])
                        back(0, g0 + 4, 1, True, False)
                        pe.wait_ge(f_prod, 1)
                        hidden(0, g0 + 5, M[0])
                        hidden(0, g0 + 6, M[1])
                        back(0, g0 + 7, 2, False, False)
                with pe.Fori(1, (N_FF - 1) // 2) as j:
                    for u in range(2):
                        f = 1 + 2 * j + u
                        m = 2 * ((1 + u) % 2)
                        pe.wait_ge(f_prod, f)
                        hidden(j, g0 + 2 + 3 * u, M[m])
                        hidden(j, g0 + 3 + 3 * u, M[m + 1])
                        back(j, g0 + 4 + 3 * u, f, False, False)
                back(0, g0 + FFN_G - 1, N_FF, False, True)

            def router():
                arrived(0, ROUTER_G)
                pe.wait_ge(hT_done, KT_D * 4)
                narrow_product(ROUTER_G)
                pe.wait_ge(rt_copied, 1)
                for t in range(NT):
                    ins = pe.transpose(A[1][:, 8 * t:8 * t + 8], lgT[:, t * P:(t + 1) * P], ident[0:8, 0:8])
                ins.then_inc(rt_turned, 1)
                pe.wait_ge(rt_picked, 1)
                p = [picked[:, t, 0:N_EXP] for t in range(NT)]
                pe.matmul(A[2][:, 0:8], strict, p[0], start=True, stop=True)
                pe.matmul(A[2][:, 8:16], ones, p[0], start=True, stop=False)
                pe.matmul(A[2][:, 8:16], strict, p[1], start=False, stop=True)
                pe.matmul(A[2][:, 16:24], ones, p[0], start=True, stop=False)
                pe.matmul(A[2][:, 16:24], ones, p[1], start=False, stop=True).then_inc(rt_ranked, 1)

            def experts(block):
                e0, n0, six0 = N_EXP * block, (N_EXP + 1) * block, MOE_G0 // 6 + block * N_EXP * N_EF

                def gather(n):
                    pe.wait_ge(e_pick, n)
                    for k in range(KT_D):
                        for t in range(NT):
                            ins = pe.matmul(M[2 + k // 4][:, (k % 4) * P:(k % 4 + 1) * P], xn[:, t, k * P:(k + 1) * P],
                                            pick[:, t, :], start=t == 0, stop=t == NT - 1)
                    ins.then_inc(e_gather, 1)

                def hidden(six, local, bank, half):
                    arrived(six, local)
                    rows_product(local, [bank], xgT, 4 * half, half == 0, half == 1)

                def turn_product(n):
                    pe.wait_ge(e_prod, n)
                    turn_tokens(work[:, 1, :], A[2]).then_inc(e_turned, 1)

                def back(six, local, part, first, last):
                    arrived(six, local)
                    for k in range(2):
                        for c in range(2):
                            stat = (gT[0][:, 2 * part + k, :], gT[1][:, 2 * part + k, :])
                            ins = mm3(A[c][:, :], stat, weights(local, k * D + c * 512, k * D + (c + 1) * 512),
                                      first and k == 0, last and k == 1)
                    ins.then_inc(gran_done, 1)

                def round_(six_f, e, f, first):
                    hidden(six_f, 4, M[0], 0)
                    hidden(six_f, 5, M[0], 1)
                    hidden(six_f, 6, M[1], 0)
                    hidden(six_f, 7, M[1], 1)
                    pe.wait_ge(e_lo, N_EF * e + f + N_EF * e0)
                    back(six_f, 8, 0, first, False)
                    back(six_f, 9, 1, False, False)
                    turn_product(N_EF * e + f + 1 + N_EF * e0)

                gather(n0 + 1)
                with pe.Fori(0, N_EXP) as e:
                    six = 7 * e + six0
                    pe.wait_ge(e_xlo, e + 1 + n0)
                    for L in range(4):
                        hidden(six, L, M[L // 2], L % 2)
                    pe.wait_ge(e_added, e + 1 + e0)
                    turn_product(N_EF * e + 1 + N_EF * e0)
                    round_(six, e, 1, True)
                    with pe.Fori(2, N_EF) as f:
                        round_(six + f - 1, e, f, False)
                    gather(e + 2 + n0)
                    pe.wait_ge(e_pickw, e + 1 + e0)
                    for t in range(NT):
                        ins = pe.transpose(A[3][:, t * P:(t + 1) * P], pick_w[:, t, :], ident)
                    ins.then_inc(e_putw, 1)
                    pe.wait_ge(e_lo, N_EF * e + N_EF + N_EF * e0)
                    back(six, 40, 0, False, False)
                    back(six, 41, 1, False, True)
                    pe.wait_ge(e_putw_done, e + 1 + e0)
                    pe.wait_ge(e_xlo, e + 2 + n0)
                    pe.wait_ge(e_y0, e + 1 + e0)
                    pe.wait_ge(e_y1, e + 1 + e0)
                    for i, bank in enumerate((M[2], M[3], A[3], A[2])):
                        t, c = i // 2, i % 2
                        pe.matmul(bank[:, :], put_w[:, t * P:(t + 1) * P], y_sb[:, c, :], start=True,
                                  stop=True).then_inc(e_scatter, 1)

            pe.wait_ge(s_const, 64)
            norm(0)
            mixers(0)
            norm(1)
            dense()
            norm(2)
            mixers(1)
            norm(3)
            router()
            experts(0)
            pe.wait_ge(rt_flag, 1)
            over = pe.value_load(flag[0:1, 0:1], min_val=0, max_val=P)
            with pe.If(over > 0):
                experts(1)
            with pe.Else():
                pe.wait_ge(rt_flag, 1)


def _constants():
    f = np.float32
    c = np.zeros((P, C_ALL), f)
    i = np.arange(P)
    c[:, C_ID:C_ID + P] = np.eye(P, dtype=f)
    c[:, C_CAUSAL:C_CAUSAL + P] = np.where(i[:, None] >= i[None, :], 0.0, NEG)
    c[:, C_CHUNK:C_CHUNK + P] = (i[:, None] <= i[None, :]) & (i[:, None] // CHUNK == i[None, :] // CHUNK)
    c[:, C_STRICT:C_STRICT + P] = i[:, None] < i[None, :]
    c[:, C_ONES:C_ONES + P] = 1.0
    c[:, C_IOTA:C_IOTA + P] = i[None, :]
    half = HD // 2
    inv_freq = f(10000.0) ** (-(np.arange(half, dtype=f) / f(half)))
    ang = np.arange(SEQ, dtype=f)[:, None] * inv_freq[None, :].astype(f)
    cos, sin = np.cos(ang).astype(f), np.sin(ang).astype(f)
    c[:, C_COS:C_SIN] = cos.reshape(NT, P, half).transpose(1, 0, 2).reshape(P, -1)
    signed = np.stack([-sin, sin], 1).reshape(NT, P, 2, half)
    c[:, C_SIN:C_DECAY] = signed.transpose(1, 0, 2, 3).reshape(P, -1)
    gamma = np.log1p(-np.exp2(-5.0 - np.arange(HEADS, dtype=np.float64)))
    diff = np.arange(SEQ)[None, :] - i[:, None]
    d = np.where(diff[:, None, :] >= 0, np.exp(np.maximum(diff, 0)[:, None, :] * gamma[None, :, None]), 0.0)
    c[:, C_DECAY:C_ALL] = (d * float(HD) ** -0.5).reshape(P, -1)
    return c


def _stream(w):
    out = np.zeros((TOTAL_G, P, GRAN), np.float32)
    n = 0

    def rows(matrix, k0, nk, c0, nc_):
        nonlocal n
        part = matrix[k0 * P:(k0 + nk) * P, c0:c0 + nc_].reshape(nk, P, nc_)
        out[n].reshape(P, nk, nc_)[:] = part.transpose(1, 0, 2)
        n += 1

    for layer in range(LAYERS):
        w_in = w["w_in"][layer]
        small = out[n].reshape(P, KT_D, 256)
        small[:, :, 0:GLA_RANK] = w_in[:, GA:GA + GLA_RANK].reshape(KT_D, P, GLA_RANK).transpose(1, 0, 2)
        small[:, :, 32:32 + HEADS] = w_in[:, FZ:FZ + HEADS].reshape(KT_D, P, HEADS).transpose(1, 0, 2)
        n += 1
        for _, c0 in CHUNKS:
            for half in range(2):
                rows(w_in, 4 * half, 4, c0, 512)
        for b in BRANCH_ORDER:
            for c in range(2):
                for half in range(2):
                    rows(w["w_gate"][layer], 4 * half, 4, b * D + c * 512, 512)
                rows(w["w_branch"][layer][b], 0, 4, c * 512, 512)
        for half in range(2):
            for c in range(2):
                rows(w["w_o"][layer], 4 * half, 4, c * 512, 512)
        if layer == 0:
            for f in range(N_FF + 1):
                if f < N_FF:
                    rows(w["ffn_w1"][0], 0, 8, f * FF, FF)
                    rows(w["ffn_w3"][0], 0, 8, f * FF, FF)
                if f > 0:
                    rows(w["ffn_w2"][0], 2 * (f - 1), 2, 0, D)
    out[n].reshape(P, KT_D, 256)[:, :, 0:N_EXP] = w["router_w"][0].reshape(KT_D, P, N_EXP).transpose(1, 0, 2)
    n += 1
    for e in range(N_EXP):
        for f in range(N_EF + 1):
            if f < N_EF:
                for m in ("moe_w1", "moe_w3"):
                    for half in range(2):
                        rows(w[m][0, e], 4 * half, 4, f * EF, EF)
            if f > 0:
                for part in range(2):
                    rows(w["moe_w2"][0, e], 4 * (f - 1) + 2 * part, 2, 0, D)
    assert n == TOTAL_G
    return out


def kernel(**inputs):
    import concourse.bacc as _bacc
    from concourse.bass_utils import run_bass_kernel_spmd as _run

    w = {k: np.asarray(v) for k, v in inputs.items()}
    gains = np.stack([w["norm1_g"][0], w["norm2_g"][0], w["norm1_g"][1], w["norm2_g"][1]])
    a2 = np.concatenate([w["w_gla_a2"], w["b_gla_a"][:, None, :]], axis=1)
    arrays = {
        "stream": _stream(w),
        "x_in": np.ascontiguousarray(w["x"][0].reshape(NT, P, D).transpose(1, 0, 2)),
        "const_in": _constants(),
        "gain_in": np.ascontiguousarray(gains.reshape(4, KT_D, P).transpose(2, 0, 1)),
        "fin_gain": np.ascontiguousarray(w["final_g"]),
        "b_forget_in": np.ascontiguousarray(w["b_forget"].T),
        "gla_a2_in": np.ascontiguousarray(a2.transpose(1, 0, 2)),
    }
    nc = _bacc.Bacc("TRN2", target_bir_lowering=False, num_devices=1)
    args = [nc.dram_tensor(name, a.shape, mybir.dt.from_np(a.dtype), kind="ExternalInput").ap()
            for name, a in arrays.items()]
    out = nc.dram_tensor("out", (P, NT, D), mybir.dt.float32, kind="ExternalOutput").ap()
    hybrid_decoder_kernel(nc, *args, out)
    r = _run(nc, [arrays], core_ids=[0])
    return r.results[0]["out"].transpose(1, 0, 2).reshape(1, SEQ, D)
```

```python
from contextlib import ExitStack

import numpy as np

import concourse.bass as bass
from concourse import mybir
from concourse.alu_op_type import AluOpType as ALU

P = 128
SEQ, D = 256, 1024
NT = SEQ // P
KT_D = D // P
LAYERS = 2
EPS = 1e-6
HEADS, HD = 4, 128
MIX = HEADS * HD
GLA_DK, GLA_RANK, GLA_TAU, CHUNK = 64, 16, 16.0, 64
D_FF, N_EXP, D_FFE = 2816, 8, 3584

GRAN = 2048
RAW, RING = 6, 3
FF = 256
N_FF = D_FF // FF
EF = 512
N_EF = D_FFE // EF
MIX_G = 43
FFN_G0 = MIX_G
FFN_G = 3 * N_FF
LAYER_G0 = (0, FFN_G0 + FFN_G)
ROUTER_G = LAYER_G0[1] + MIX_G
MOE_G0 = ROUTER_G + 1
EXP_G = 6 * N_EF
TOTAL_G = MOE_G0 + N_EXP * EXP_G
assert MOE_G0 % 6 == 0 and EXP_G % 6 == 0 and TOTAL_G % 6 == 0

_W = (MIX, MIX, MIX, HEADS, HEADS * GLA_DK, HEADS * GLA_DK, MIX, GLA_RANK, MIX, MIX, MIX, MIX, MIX)
_AT = [sum(_W[:i]) for i in range(len(_W))]
FQ, FK, FV, FZ, GQ, GK, GV, GA, GR, RQ, RK, RV, RG = _AT
D_IN = sum(_W)
CHUNKS = (("rq", RQ), ("rk", RK), ("rv", RV), ("rg", RG), ("fq", FQ), ("fk", FK), ("fv", FV),
          ("gqk", GQ), ("gv", GV), ("gr", GR))
BY_FEATURE = ("fq", "fk", "gqk")
BRANCH_ORDER = (2, 0, 1)
N_GB = 2 * len(BRANCH_ORDER)
GATE_S0 = 1 + 2 * len(CHUNKS)
WO_S0 = GATE_S0 + 3 * N_GB
assert WO_S0 + 4 == MIX_G
READER = ["dve", "dve", "act", "act", "act", "act", "act", "dve", "act", "act"] + ["act", "dve"] * N_GB
AT_TILE = {2: 0, 0: 4, 1: 0}

C_ID, C_CAUSAL, C_CHUNK, C_STRICT, C_ONES, C_IOTA, C_COS = (P * i for i in range(7))
C_SIN = C_COS + NT * 64
C_DECAY = C_SIN + NT * P
C_ALL = C_DECAY + HEADS * SEQ
NEG = -1e30


def hybrid_decoder_kernel(nc, stream, x_in, const_in, gains_in, b_forget, gla_a2, out):
    f32, f32r, i32, u32 = mybir.dt.float32, mybir.dt.float32r, mybir.dt.int32, mybir.dt.uint32
    ACT, AX = mybir.ActivationFunctionType, mybir.AxisListType

    with ExitStack() as ctx:
        def sb(name, shape, dt=f32):
            return ctx.enter_context(nc.sbuf_tensor(name, shape, dt))

        def sem(name):
            return ctx.enter_context(nc.semaphore(name))

        raw = sb("raw", [P, RAW, GRAN])
        w_hi = sb("w_hi", [P, RING, GRAN], f32r)
        w_lo = sb("w_lo", [P, RING, GRAN], f32r)
        x = sb("x", [P, NT, D])
        xn = sb("xn", [P, NT, D])
        hT = [sb(f"hT_{h}", [P, KT_D, SEQ], f32r) for h in ("hi", "lo")]
        aT = [sb(f"aT_{h}", [P, 8, SEQ], f32r) for h in ("hi", "lo")]
        qT = sb("qT", [P, 2, HEADS, SEQ])
        kT = sb("kT", [P, 2, HEADS, SEQ])
        val = sb("val", [P, 2, NT, MIX])
        work = sb("work", [P, 2, 512])
        rot = sb("rot", [P, 2, 512])
        sgate = sb("sgate", [P, NT, MIX])
        o = sb("o", [P, NT, MIX])
        soft = sb("soft", [P, 2, 384])
        att = sb("att", [P, 2, 384])
        cst = sb("cst", [P, C_ALL])
        bf = sb("bf", [36, LAYERS])
        a2 = sb("a2", [GLA_RANK + 1, LAYERS, 256])
        gaT = sb("gaT", [32, SEQ])
        ncT = sb("ncT", [36, SEQ])
        cq = sb("cq", [P, 8])
        bend = sb("bend", [P, 8])
        aend = sb("aend", [P, 8])
        stats = sb("stats", [P, 8, 6])
        mv = sb("mv", [P, 8, 2])
        rs = sb("rs", [P, 4, 8])
        sq = sb("sq", [P, NT, 2])
        ss = sb("ss", [P, 3, NT])
        spare = sb("spare", [P, 2])
        one = sb("one", [P, 1])
        w_place = sb("w_place", [P, 1])
        nmax = sb("nmax", [P, NT, HEADS])
        rsum = sb("rsum", [P, NT, HEADS])
        lgT = sb("lgT", [8, SEQ])
        lg = sb("lg", [P, NT, 8])
        top = sb("top", [P, NT, 8])
        topi = sb("topi", [P, NT, 8], u32)
        topf = sb("topf", [P, NT, 8])
        tw = sb("tw", [P, 3, NT])
        comb = sb("comb", [P, NT, N_EXP + 1])
        rank = sb("rank", [P, NT, N_EXP + 1])
        picked = sb("picked", [P, NT, N_EXP + 1])
        flag = sb("flag", [P, 1], i32)
        flagf = sb("flagf", [P, 1])

        ident = cst[:, C_ID:C_ID + P]
        causal = cst[:, C_CAUSAL:C_CAUSAL + P]
        chunk_tri = cst[:, C_CHUNK:C_CHUNK + P]
        strict = cst[:, C_STRICT:C_STRICT + P]
        ones = cst[:, C_ONES:C_ONES + P]
        iota = cst[:, C_IOTA:C_IOTA + P]
        cos = cst[:, C_COS:C_SIN].rearrange("p (t i) -> p t i", t=NT)
        sin = cst[:, C_SIN:C_DECAY].rearrange("p (t u i) -> p t u i", t=NT, u=2)
        decay = cst[:, C_DECAY:C_ALL].rearrange("p (h q) -> p h q", h=HEADS)
        gsc = soft[:, :, :].rearrange("p a b -> p (a b)")[:, 0:512]
        states = rot[:, :, :].rearrange("p a b -> p (a b)")[:, 0:768].rearrange("p (f c v) -> p f c v", f=2, c=3)
        q_dec, k_inv = (qT[:, 0, 2 * i:2 * i + 2, :] for i in range(2))
        k_end = kT[:, 0, 0:2, :]
        k_tok = kT[:, 0, 2:4, :]
        xgT = [h[:, 0:4, :].rearrange("p k (a s) -> p (k a) s", a=2) for h in hT]
        gT = [h[:, 0:2, :].rearrange("p k (a s) -> p (k a) s", a=2) for h in aT]
        pick = rot[:, 0, 0:SEQ].rearrange("p (t s) -> p t s", t=NT)
        pick_w = rot[:, 0, SEQ:512].rearrange("p (t s) -> p t s", t=NT)
        put = aT[0][:, 2, :]
        y_part = [h[:, 4:8, :].rearrange("p k s -> p (k s)") for h in aT]
        gain = o[:, :, :].rearrange("p t c -> p (t c)")
        gain_fin = val[:, 1, :, :].rearrange("p t c -> p (t c)")

        M = [ctx.enter_context(nc.psum_tensor(f"M{i}", [P, 512], f32)) for i in range(4)]
        A = [ctx.enter_context(nc.psum_tensor(f"A{i}", [P, 512], f32)) for i in range(4)]

        loaded = [sem(f"loaded{i}") for i in range(RAW)]
        s_in = [sem(f"x_loaded{t}") for t in range(NT)]
        s_ident, s_const = sem("identity_loaded"), sem("constants_loaded")
        s_gain, s_gain_fin = sem("gain_loaded"), sem("final_gain_loaded")
        hi_done, lo_done, gran_done = sem("hi_done"), sem("lo_done"), sem("gran_done")
        act_read, dve_read = sem("act_read"), sem("dve_read")
        act_own, dve_own = sem("act_own"), sem("dve_own")
        ready0 = sem("dve_ready")
        sumsq, normed, x_turned, hT_hi_done, hT_done = (sem(n) for n in ("sumsq", "normed", "x_turned", "hT_hi_done", "hT_done"))
        one_set, root_in, root_done = sem("one_set"), sem("root_in"), sem("root_done")
        x_new, tile0_done = sem("x_new"), sem("tile0_done")
        ga_done, z_done, fz_done, fln_done, c_done = (sem(n) for n in ("ga_done", "z_done", "fz_done", "fln_done", "c_done"))
        zln_done, loga_done, cum_done, cq_done, bend_done, exp_done = (
            sem(n) for n in ("zln_done", "loga_done", "cum_done", "cq_done", "bend_done", "exp_done"))
        rotated, rot_turned, rot_read = sem("rotated"), sem("rot_turned"), sem("rot_read")
        ret_scores, ret_att, ret_out = sem("ret_scores"), sem("ret_att"), sem("ret_out")
        val_done, silu_done, fq_done = sem("val_done"), sem("silu_done"), sem("fq_done")
        fox_scores, fox_rows, fox_exp, fox_turned, fox_att, fox_out = (
            sem(n) for n in ("fox_scores", "fox_rows", "fox_exp", "fox_turned", "fox_att", "fox_out"))
        gla_ops, kend_turned, kend_done, kv_done, state_done = (
            sem(n) for n in ("gla_ops", "kend_turned", "kend_done", "kv_done", "state_done"))
        gla_scores, gla_att, gla_out = sem("gla_scores"), sem("gla_att"), sem("gla_out")
        o_done, o_turned, oT_hi_done, oT_done = (sem(n) for n in ("o_done", "o_turned", "oT_hi_done", "oT_done"))
        gate_done, merged = sem("gate_done"), sem("merged")
        m_turned, mT_hi_done, mT_done = sem("m_turned"), sem("mT_hi_done"), sem("mT_done")
        f_silu, f_prod, f_hi, f_lo = (sem(n) for n in ("f_silu", "f_prod", "f_hi", "f_lo"))
        rt_top, rt_exp, rt_picked, rt_ranked, rt_counted, rt_flag = (
            sem(n) for n in ("rt_top", "rt_exp", "rt_picked", "rt_ranked", "rt_counted", "rt_flag"))
        e_moved = sem("e_moved")
        e_pick, e_gather, e_xhi, e_xlo = (sem(n) for n in ("e_pick", "e_gather", "e_xhi", "e_xlo"))
        e_silu, e_prod, e_turned, e_hi, e_lo = (sem(n) for n in ("e_silu", "e_prod", "e_turned", "e_hi", "e_lo"))
        e_pickw, e_putw, e_put, e_yhi, e_ylo, e_scatter, e_added = (
            sem(n) for n in ("e_pickw", "e_putw", "e_put", "e_yhi", "e_ylo", "e_scatter", "e_added"))
        fin_x, fin_sq, fin_var, fin_root, fin_done, stored = (
            sem(n) for n in ("fin_x", "fin_sq", "fin_var", "fin_root", "fin_done", "stored"))
        block = ctx.enter_context(nc.Block())

        def reads(engine, layer, chunk):
            return layer * READER.count(engine) + READER[:chunk + 1].count(engine)

        def wait_read(pe, layer, chunk):
            if READER[chunk] == "act":
                pe.wait_ge(act_read, reads("act", layer, chunk))
            else:
                pe.wait_ge(dve_read, reads("dve", layer, chunk))

        def gla_result(t, h):
            at = (2 * t + h // 2) * HD
            return A[2 + h % 2][:, at:at + HD]

        def by_tile(t, h):
            return A[t][:, h * HD:(h + 1) * HD]

        def pair(chunk):
            return M[2 * (chunk % 2):2 * (chunk % 2) + 2]

        @block.sync
        def _(sp):
            def load(six, local, source, first=False):
                if not first:
                    sp.wait_ge(lo_done, 6 * six + local - RAW + 1)
                sp.dma_start(raw[:, local % RAW, :], source).then_inc(loaded[local % RAW], 16)

            for t in range(NT):
                sp.dma_start(x[:, t, :], x_in[:, t, :]).then_inc(s_in[t], 16)
            sp.dma_start(ident, const_in[:, C_ID:C_ID + P]).then_inc(s_ident, 16)
            for g in range(RAW):
                load(0, g, stream[g], first=True)
            six_of = stream.rearrange("(s u) p n -> s u p n", u=6)
            with sp.Fori(1, TOTAL_G // 6) as six:
                for u in range(6):
                    load(six, u, six_of[six, u])
            sp.wait_ge(rt_flag, 1)
            over = sp.value_load(flag[0:1, 0:1], min_val=0, max_val=P)
            with sp.If(over > 0):
                with sp.Fori(0, N_EXP * EXP_G // 6) as six:
                    for u in range(6):
                        load(six + TOTAL_G // 6, u, six_of[six + MOE_G0 // 6, u])
            with sp.Else():
                sp.wait_ge(rt_flag, 1)
            for t in range(NT):
                for c in range(2):
                    sp.wait_ge(fin_done, 2 * t + c + 1)
                    sp.dma_start(out[:, t, c * 512:(c + 1) * 512], xn[:, t, c * 512:(c + 1) * 512]).then_inc(stored, 16)
            sp.wait_ge(stored, 16 * 2 * NT)

        @block.gpsimd
        def _(pool):
            def load_gain(i, dst, loaded):
                pool.dma_start(dst, gains_in[i].partition_broadcast(P)).then_inc(loaded, 16)

            load_gain(0, gain, s_gain)
            pool.dma_start(cst[:, P:C_ALL], const_in[:, P:C_ALL]).then_inc(s_const, 16)
            pool.dma_start(bf[32:36, :], b_forget).then_inc(s_const, 16)
            pool.dma_start(a2[:, :, :], gla_a2).then_inc(s_const, 16)
            pool.wait_ge(o_turned, 6)
            load_gain(1, gain, s_gain)
            pool.wait_ge(normed, 4 * 2)
            load_gain(2, gain, s_gain)
            pool.wait_ge(o_turned, 12)
            load_gain(3, gain, s_gain)
            load_gain(4, gain_fin, s_gain_fin)

        @block.scalar
        def _(act):
            own = [0]

            def link(ins):
                own[0] += 1
                ins.then_inc(act_own, 1)
                act.wait_ge(act_own, own[0])

            def copy(dst, src, **kw):
                return act.activation(dst, src, ACT.Copy, **kw)

            def hi(six, local):
                act.wait_ge(loaded[local % RAW], 16 * (six + local // RAW) + 16)
                if not (isinstance(six, int) and 6 * six + local < RING):
                    act.wait_ge(gran_done, 6 * six + local - RING + 1)
                copy(w_hi[:, local % RING, :], raw[:, local % RAW, :]).then_inc(hi_done, 1)

            def squares(t, i):
                for c in range(2):
                    if i == 0:
                        act.wait_ge(s_in[t], 16)
                    else:
                        act.wait_ge(x_new, 4 * (i - 1) + 2 * t + c + 1)
                    half = slice(c * 512, (c + 1) * 512)
                    act.activation(xn[:, t, half], x[:, t, half], ACT.Square, scale=float(D) ** -0.5,
                                   accum_out=sq[:, t, c:c + 1]).then_inc(sumsq, 1)

            def root(src, dst):
                act.wait_ge(root_in, roots[0] + 1)
                act.activation(dst, src, ACT.Sqrt).then_inc(root_done, 1)
                roots[0] += 1

            def before_norm():
                act.wait_ge(one_set, 1)
                act.activation(spare[:, 0:1], one[:, :], ACT.Sqrt)

            def norm(i, following):
                root(ss[:, 1, 0:1], ss[:, 2, 0:1])
                if i:
                    hi(0, following + 1)
                squares(1, i)
                root(ss[:, 1, 1:2], ss[:, 2, 1:2])
                if not i:
                    hi(0, following)
                for t in range(NT):
                    for a in range(2):
                        act.wait_ge(x_turned, 4 * i + 2 * t + a + 1)
                        copy(hT[0][:, 4 * a:4 * a + 4, t * P:(t + 1) * P],
                             A[2 * t + a][:, :].rearrange("p (k s) -> p k s", k=4)).then_inc(hT_hi_done, 1)
                if not i:
                    hi(0, following + 1)

            roots = [0]

            def turn_hi(n, bank, dst):
                act.wait_ge(o_turned, n)
                copy(dst, bank[:, :].rearrange("p (h q) -> p h q", h=HEADS)).then_inc(oT_hi_done, 1)

            def mixers(layer):
                g0 = LAYER_G0[layer]
                for s in range(MIX_G):
                    if 0 < s < MIX_G - 1:
                        act.wait_ge(gran_done, g0 + s)
                    if s == 1:
                        act.wait_ge(s_const, 48)
                        copy(gaT[0:GLA_RANK, :], A[0][0:GLA_RANK, 0:SEQ]).then_inc(ga_done, 1)
                    if s == 2:
                        act.wait_ge(fz_done, layer + 1)
                        e = att[32:36, 1, 0:SEQ]
                        link(act.activation(e, att[32:36, 0, 0:SEQ], ACT.Abs))
                        link(act.activation(e, e, ACT.Exp, scale=-1.0))
                        act.activation(e, e, ACT.Ln, bias=1.0).then_inc(fln_done, 1)
                    if s == 3:
                        act.wait_ge(z_done, layer + 1)
                        e = o[:, 0, :]
                        link(act.activation(e, A[1][:, :], ACT.Abs))
                        link(act.activation(e, e, ACT.Exp, scale=-1.0))
                        act.activation(e, e, ACT.Ln, bias=1.0).then_inc(zln_done, 1)
                    if 4 <= s < 8:
                        i = s - 4
                        act.wait_ge(rot_turned, 4 * layer + i + 1)
                        dst = (qT if i < 2 else kT)[:, 0, :, (i % 2) * P:(i % 2 + 1) * P]
                        copy(dst, A[2 + i % 2][:, :].rearrange("p (h q) -> p h q", h=HEADS)).then_inc(rot_read, 1)
                    if s in (7, 15, 19):
                        b, chunk = ((0, 2), (1, 6), (0, 8))[(7, 15, 19).index(s)]
                        if b == 0 and s == 19:
                            act.wait_ge(ret_out, layer * HEADS + HEADS)
                        act.wait_ge(fox_out, layer * HEADS) if layer and b else None
                        for t in range(NT):
                            ins = copy(val[:, b, t, :], pair(chunk)[t][:, :])
                        ins.then_inc(act_read, 1)
                    if s == 7:
                        act.wait_ge(bend_done, layer + 1)
                        act.wait_ge(rotated, 4 * layer + 4)
                        act.activation(work[:, 0, :], A[0][:, :], ACT.Exp, scale=1.0 / GLA_TAU)
                        act.activation(work[:, 1, :], A[0][:, :], ACT.Exp, scale=-1.0 / GLA_TAU)
                    if s == 8:
                        act.wait_ge(rot_turned, 4 * layer + 3)
                        for i in range(8):
                            act.activation(rot[:, 0, i * 64:(i + 1) * 64], A[0][:, i * 64:(i + 1) * 64], ACT.Exp,
                                           scale=-1.0 / GLA_TAU, bias=bend[:, i:i + 1])
                        act.activation(aend[:, :], bend[:, :], ACT.Exp).then_inc(exp_done, 1)
                    if s in (9, 21):
                        for t in range(NT):
                            ins = act.activation(sgate[:, t, :], pair(3 if s == 9 else 9)[t][:, :], ACT.Silu)
                        ins.then_inc(act_read, 1)
                    if s == 11:
                        for j in range(2):
                            ins = copy(qT[:, 1, 2 * j:2 * j + 2, :], pair(4)[j][:, :].rearrange("p (h q) -> p h q", h=2),
                                       scale=float(HD) ** -0.5)
                        ins.then_inc(act_read, 1)
                    if s == 13:
                        for j in range(2):
                            ins = copy(kT[:, 1, 2 * j:2 * j + 2, :], pair(5)[j][:, :].rearrange("p (h q) -> p h q", h=2))
                        ins.then_inc(act_read, 1)
                    if s == 14:
                        root(rs[:, 0, :], rs[:, 1, :])
                    if s == 17:
                        for t in range(NT):
                            turn_hi(6 * layer + t + 1, A[2 + t], aT[0][:, 0:4, t * P:(t + 1) * P])
                    if 19 <= s < 19 + HEADS:
                        h = s - 19
                        act.wait_ge(fox_rows, HEADS * layer + h + 1)
                        act.activation(soft[:, h % 2, 0:P], soft[:, h % 2, 0:P], ACT.Exp, bias=nmax[:, 0, h:h + 1],
                                       accum_out=rsum[:, 0, h:h + 1])
                        act.activation(soft[:, h % 2, P:384], soft[:, h % 2, P:384], ACT.Exp, bias=nmax[:, 1, h:h + 1],
                                       accum_out=rsum[:, 1, h:h + 1]).then_inc(fox_exp, 1)
                    if s == 19:
                        act.wait_ge(kend_turned, layer + 1)
                        copy(k_tok, A[0][:, :].rearrange("p (t f) -> p t f", t=2)).then_inc(kend_done, 1)
                    if 20 <= s < 20 + HEADS:
                        h = s - 20
                        act.wait_ge(fox_turned, HEADS * layer + h + 1)
                        copy(att[:, h % 2, :], A[3][:, 0:384]).then_inc(fox_att, 1)
                    if s == 25:
                        for t in range(NT):
                            turn_hi(6 * layer + 2 + t + 1, A[2 + t], aT[0][:, 4:8, t * P:(t + 1) * P])
                    if s == 30:
                        root(rs[:, 0, :], rs[:, 1, :])
                    if s == 32:
                        for t in range(NT):
                            turn_hi(6 * layer + 4 + t + 1, A[t], aT[0][:, 0:4, t * P:(t + 1) * P])
                    if s >= GATE_S0 + 2 and s < WO_S0 and (s - GATE_S0 - 2) % 3 == 0:
                        j = (s - GATE_S0 - 2) // 3
                        if j or layer:
                            act.wait_ge(merged, N_GB * layer + j)
                        else:
                            act.wait_ge(gla_ops, 1)
                        for t in range(NT):
                            ins = act.activation(work[:, t, :], pair(10 + 2 * j)[t][:, :], ACT.Sigmoid)
                        ins.then_inc(act_read, 1)
                    if s in (37, 40):
                        h = int(s == 40)
                        act.wait_ge(m_turned, 2 * layer + h + 1)
                        for a in range(2):
                            tile = (4, 0)[h] + 2 * a
                            copy(aT[0][:, tile:tile + 2, :],
                                 A[2 * h + a][:, :].rearrange("p (k q) -> p k q", k=2)).then_inc(mT_hi_done, 1)
                    if s == MIX_G - 1:
                        before_norm()
                        squares(0, 2 * layer + 1)
                    else:
                        hi(0, g0 + s + 2)

            def dense():
                g0 = FFN_G0

                def silu(f_expr, pair_no):
                    act.activation(work[:, 0, :], M[2 * pair_no][:, :], ACT.Silu).then_inc(f_silu, 1)

                hi(0, g0 + 2)
                act.wait_ge(gran_done, g0 + 1)
                silu(0, 0)
                hi(0, g0 + 3)
                with act.Fori(0, (N_FF - 1) // 2) as j:
                    for u in range(2):
                        f = 1 + 2 * j + u
                        act.wait_ge(gran_done, 6 * j + g0 + 2 + 3 * u)
                        act.wait_ge(f_prod, f)
                        copy(gT[0], work[:, 1, :].rearrange("p (k s) -> p k s", k=4)).then_inc(f_hi, 1)
                        hi(j, g0 + 4 + 3 * u)
                        act.wait_ge(gran_done, 6 * j + g0 + 3 + 3 * u)
                        silu(f, (1 + u) % 2)
                        hi(j, g0 + 5 + 3 * u)
                        hi(j, g0 + 6 + 3 * u)
                act.wait_ge(gran_done, g0 + FFN_G - 1)
                act.wait_ge(f_prod, N_FF)
                copy(gT[0], work[:, 1, :].rearrange("p (k s) -> p k s", k=4)).then_inc(f_hi, 1)
                before_norm()
                squares(0, 2)

            def experts(block):
                e0, six0 = N_EXP * block, MOE_G0 // 6 + block * N_EXP * N_EF

                def gathered(n):
                    act.wait_ge(e_gather, n)
                    for a in range(2):
                        copy(xgT[0][:, 4 * a:4 * a + 4, :],
                             M[2 + a][:, :].rearrange("p (k s) -> p k s", k=4)).then_inc(e_xhi, 1)

                def product_hi(n):
                    act.wait_ge(e_turned, n)
                    copy(gT[0], A[2][:, :].rearrange("p (k s) -> p k s", k=4)).then_inc(e_hi, 1)

                def silu(done):
                    act.wait_ge(gran_done, done)
                    act.activation(work[:, 0, :], M[0][:, :], ACT.Silu).then_inc(e_silu, 1)

                def rounds(six, e):
                    with act.Fori(1, N_EF) as f:
                        six_f = six + f - 1
                        for u in range(6):
                            if u == 2:
                                silu(6 * six_f + 4 + 2)
                            hi(six_f, 4 + u + 2)
                            if u == 0:
                                product_hi(N_EF * e + f + N_EF * e0)
                    act.wait_ge(gran_done, 6 * six + 40)
                    product_hi(N_EF * e + N_EF + N_EF * e0)

                def outputs(six, e):
                    act.wait_ge(gran_done, 6 * six + 42)
                    act.wait_ge(e_put, e + 1 + e0)
                    for c in range(2):
                        act.activation(y_part[0][:, c * 512:(c + 1) * 512], A[c][:, :], ACT.Copy,
                                       scale=w_place[:, 0:1]).then_inc(e_yhi, 1)

                if block:
                    hi(six0, 0)
                    hi(six0, 1)
                hi(six0, 2)
                gathered(e0 + 1)
                hi(six0, 3)
                silu(6 * six0 + 2)
                hi(six0, 4)
                hi(six0, 5)
                with act.Fori(0, N_EXP - 1) as e:
                    six = 7 * e + six0
                    rounds(six, e)
                    hi(six, 42)
                    gathered(e + 2 + e0)
                    hi(six, 43)
                    hi(six, 44)
                    outputs(six, e)
                    hi(six, 45)
                    silu(6 * six + 44)
                    hi(six, 46)
                    hi(six, 47)
                over = None
                if not block:
                    act.wait_ge(rt_flag, 1)
                    over = act.value_load(flag[0:1, 0:1], min_val=0, max_val=P)
                rounds(six0 + 7 * (N_EXP - 1), N_EXP - 1)
                before_norm()
                outputs(six0 + 7 * (N_EXP - 1), N_EXP - 1)
                return over

            before_norm()
            squares(0, 0)
            norm(0, 0)
            mixers(0)
            norm(1, FFN_G0)
            dense()
            norm(2, LAYER_G0[1])
            mixers(1)
            norm(3, ROUTER_G)
            hi(0, ROUTER_G + 2)
            act.wait_ge(rt_top, 1)
            act.activation(tw[:, 1, :], tw[:, 0, :], ACT.Exp).then_inc(rt_exp, 1)
            over = experts(0)
            with act.If(over > 0):
                experts(1)
            with act.Else():
                act.wait_ge(rt_flag, 1)
            act.wait_ge(fin_x, 1)
            act.activation(xn[:, 1, :], x[:, 1, :], ACT.Square, scale=float(D) ** -0.5,
                           accum_out=sq[:, 1, 0:1]).then_inc(fin_sq, 1)
            for t in range(NT):
                act.wait_ge(fin_var, t + 1)
                act.activation(ss[:, 2, t:t + 1], ss[:, 1, t:t + 1], ACT.Sqrt).then_inc(fin_root, 1)

        @block.vector
        def _(dve):
            own = [0]

            def link(ins):
                own[0] += 1
                ins.then_inc(dve_own, 1)
                dve.wait_ge(dve_own, own[0])

            def lo(six, local):
                dve.wait_ge(hi_done, 6 * six + local + 1)
                dve.tensor_tensor(w_lo[:, local % RING, :], raw[:, local % RAW, :],
                                  w_hi[:, local % RING, :].bitcast(f32), ALU.subtract).then_inc(lo_done, 1)

            roots = [0]

            def inverse_root(var, n):
                dve.wait_ge(root_done, roots[0])
                link(dve.reciprocal(n, var))

            def add_tile(banks, t):
                for c in range(2):
                    dve.tensor_tensor(x[:, t, c * 512:(c + 1) * 512], banks[c][:, :],
                                      x[:, t, c * 512:(c + 1) * 512], ALU.add).then_inc(x_new, 1)

            def norm_tile(i, t):
                dve.wait_ge(sumsq, 4 * i + 2 * t + 2)
                roots[0] += 1
                dve.scalar_tensor_tensor(out=ss[:, 1, t:t + 1], in0=sq[:, t, 0:1], scalar=EPS, in1=sq[:, t, 1:2],
                                         op0=ALU.add, op1=ALU.add).then_inc(root_in, 1)
                inverse_root(ss[:, 2, t:t + 1], ss[:, 0, t:t + 1])
                dve.wait_ge(s_gain, 16 * (i + 1))
                for c in range(2):
                    half = slice(c * 512, (c + 1) * 512)
                    dve.scalar_tensor_tensor(out=xn[:, t, half], in0=x[:, t, half], scalar=ss[:, 0, t:t + 1],
                                             in1=gain[:, half], op0=ALU.mult, op1=ALU.mult).then_inc(normed, 1)

            def norm(i, following, banks1=None):
                norm_tile(i, 0)
                if i:
                    dve.wait_ge(gran_done, (0, FFN_G0, LAYER_G0[1], ROUTER_G)[i])
                    add_tile(banks1, 1)
                norm_tile(i, 1)
                if not i:
                    lo(0, following)
                for t in range(NT):
                    for a in range(2):
                        dve.wait_ge(hT_hi_done, 4 * i + 2 * t + a + 1)
                        dst = (slice(None), slice(4 * a, 4 * a + 4), slice(t * P, (t + 1) * P))
                        dve.tensor_tensor(hT[1][dst], A[2 * t + a][:, :].rearrange("p (k s) -> p k s", k=4),
                                          hT[0][dst].bitcast(f32), ALU.subtract).then_inc(hT_done, 1)
                if i < 3:
                    lo(0, following + 1)

            def rotate(i, chunk, t):
                src = pair(chunk)[t]
                v = src[:, :].rearrange("p (h u i) -> p h u i", h=HEADS, u=2)
                w1 = work[:, 1, :].rearrange("p (h u i) -> p h u i", h=HEADS, u=2)
                dve.tensor_tensor(work[:, 0, :].rearrange("p (a i) -> p a i", i=64),
                                  src[:, :].rearrange("p (a i) -> p a i", i=64),
                                  cos[:, t:t + 1, :].to_broadcast([P, 8, 64]), ALU.mult)
                for u in range(2):
                    ins = dve.tensor_tensor(w1[:, :, u, :], v[:, :, 1 - u, :],
                                            sin[:, t, u:u + 1, :].to_broadcast([P, HEADS, 64]), ALU.mult)
                if t == NT - 1:
                    link_read(ins)
                else:
                    link(ins)
                if i >= 2:
                    dve.wait_ge(rot_turned, 4 * layer_no[0] + i - 1)
                dve.tensor_tensor(rot[:, t, :], work[:, 0, :], work[:, 1, :], ALU.add).then_inc(rotated, 1)
                dve.wait_ge(rotated, 4 * layer_no[0] + i + 1)

            layer_no = [0]
            n_read = [0]

            def link_read(ins):
                n_read[0] += 1
                ins.then_inc(dve_read, 1)
                dve.wait_ge(dve_read, n_read[0])

            def head_stats(result, centred):
                for t in range(NT):
                    for h in range(HEADS):
                        ins = dve.bn_stats(stats[:, 4 * t + h, :], result(t, h))
                link(ins)
                for i in range(8):
                    ins = dve.bn_aggr(mv[:, i, :], stats[:, i, :])
                link(ins)
                roots[0] += 1
                if centred:
                    dve.tensor_scalar(rs[:, 0, :], mv[:, :, 1], EPS, None, ALU.add).then_inc(root_in, 1)
                else:
                    link(dve.tensor_tensor(rs[:, 2, :], mv[:, :, 0], mv[:, :, 0], ALU.mult))
                    dve.scalar_tensor_tensor(out=rs[:, 0, :], in0=mv[:, :, 1], scalar=EPS, in1=rs[:, 2, :],
                                             op0=ALU.add, op1=ALU.add).then_inc(root_in, 1)

            def turn_lo(n, bank, hi_part, dst):
                dve.wait_ge(oT_hi_done, n)
                dve.tensor_tensor(dst, bank[:, :].rearrange("p (h q) -> p h q", h=HEADS), hi_part.bitcast(f32),
                                  ALU.subtract).then_inc(oT_done, 1)

            def mixers(layer):
                g0 = LAYER_G0[layer]
                layer_no[0] = layer
                wo_banks = [[pair(22)[t], pair(23)[t]] for t in range(NT)]
                zf, ef = att[32:36, 0, 0:SEQ], att[32:36, 1, 0:SEQ]
                for s in range(MIX_G):
                    if 0 < s < MIX_G - 1:
                        dve.wait_ge(gran_done, g0 + s)
                    if s == 1:
                        dve.wait_ge(s_const, 48)
                        dve.tensor_scalar(zf, A[0][32:36, 0:SEQ], bf[32:36, layer:layer + 1], None,
                                          ALU.add).then_inc(fz_done, 1)
                    if s == 3:
                        dve.wait_ge(fln_done, layer + 1)
                        link(dve.scalar_tensor_tensor(out=ef, in0=zf, scalar=0.0, in1=ef, op0=ALU.min, op1=ALU.subtract))
                        cT = soft[32:36, 0, 0:SEQ]
                        link(dve.tensor_tensor_scan(cT, ones[32:36, 0:1].to_broadcast([HEADS, SEQ]), ef, 0.0,
                                                    ALU.mult, ALU.add))
                        dve.tensor_scalar(ncT[32:36, :], cT, -1.0, None, ALU.mult).then_inc(c_done, 1)
                    if 3 <= s < 7:
                        i = s - 3
                        rotate(i, i // 2, i % 2)
                    if s == 4:
                        dve.wait_ge(zln_done, layer + 1)
                        dve.scalar_tensor_tensor(out=o[:, 1, :], in0=A[1][:, :], scalar=0.0, in1=o[:, 0, :],
                                                 op0=ALU.min, op1=ALU.subtract).then_inc(loga_done, 1)
                    if s == 6:
                        dve.wait_ge(cum_done, layer + 1)
                        dve.tensor_scalar(bend[:, :], A[0][:, :].rearrange("p (b i) -> p b i", i=64)[:, :, 63],
                                          1.0 / GLA_TAU, None, ALU.mult).then_inc(bend_done, 1)
                        dve.tensor_copy(cq[:, :], A[1][:, 0:8]).then_inc(cq_done, 1)
                    if 9 <= s < 9 + HEADS:
                        h = s - 9
                        dve.wait_ge(ret_scores, HEADS * layer + h + 1)
                        if h >= 2:
                            dve.wait_ge(ret_out, HEADS * layer + h - 1)
                        src = A[2 + h % 2]
                        dve.tensor_tensor(att[:, h % 2, 0:SEQ], src[:, 0:SEQ], decay[:, h, :], ALU.mult)
                        dve.tensor_tensor(att[:, h % 2, SEQ:384], src[:, SEQ:384], decay[:, h, 0:P],
                                          ALU.mult).then_inc(ret_att, 1)
                    if s == 13:
                        dve.wait_ge(ret_out, HEADS * layer + HEADS)
                        head_stats(by_tile, True)
                    if s == 15:
                        dve.wait_ge(act_read, reads("act", layer, 3))
                        inverse_root(rs[:, 1, :], rs[:, 2, :])
                        for t in range(NT):
                            for h in range(HEADS):
                                i = 4 * t + h
                                ins = dve.tensor_scalar(o[:, t, h * HD:(h + 1) * HD], A[t][:, h * HD:(h + 1) * HD],
                                                        mv[:, i, 0:1], rs[:, 2, i:i + 1], ALU.subtract, ALU.mult)
                        link(ins)
                        for t in range(NT):
                            ins = dve.tensor_tensor(o[:, t, :], o[:, t, :], sgate[:, t, :], ALU.mult)
                        ins.then_inc(o_done, 1)
                    if s == 17:
                        dve.wait_ge(exp_done, layer + 1)
                        bq, bk = pair(7)
                        dve.scalar_tensor_tensor(out=q_dec, in0=bq[:, :].rearrange("p (f q) -> p f q", f=2),
                                                 scalar=float(GLA_DK) ** -0.5,
                                                 in1=work[:, 0, :].rearrange("p (f q) -> p f q", f=2),
                                                 op0=ALU.mult, op1=ALU.mult)
                        dve.tensor_tensor(k_inv, bk[:, :].rearrange("p (f q) -> p f q", f=2),
                                          work[:, 1, :].rearrange("p (f q) -> p f q", f=2), ALU.mult)
                        n_read[0] += 1
                        dve.tensor_tensor(k_end, bk[:, :].rearrange("p (f q) -> p f q", f=2),
                                          rot[:, 0, :].rearrange("p (f q) -> p f q", f=2), ALU.mult).then_inc(dve_read, 1)
                        for t in range(NT):
                            turn_lo(6 * layer + t + 1, A[2 + t], aT[0][:, 0:4, t * P:(t + 1) * P],
                                    aT[1][:, 0:4, t * P:(t + 1) * P])
                        dve.wait_ge(dve_read, n_read[0])
                        dve.tensor_copy(flagf[:, 0:1], bend[:, 0:1]).then_inc(gla_ops, 1)
                    if 18 <= s < 18 + HEADS:
                        h = s - 18
                        dve.wait_ge(fox_scores, HEADS * layer + h + 1)
                        if h >= 2:
                            dve.wait_ge(fox_turned, HEADS * layer + h - 1)
                        row = soft[:, h % 2, :]
                        dve.scalar_tensor_tensor(out=row[:, 0:P], in0=A[2][:, 0:P], scalar=cq[:, h:h + 1], in1=causal,
                                                 op0=ALU.add, op1=ALU.add)
                        dve.tensor_scalar(row[:, P:2 * P], A[2][:, P:2 * P], cq[:, 4 + h:5 + h], None, ALU.add)
                        link(dve.scalar_tensor_tensor(out=row[:, 2 * P:384], in0=A[2][:, 2 * P:384],
                                                      scalar=cq[:, 4 + h:5 + h], in1=causal, op0=ALU.add, op1=ALU.add))
                        dve.tensor_reduce(nmax[:, 0, h:h + 1], row[:, 0:P], AX.X, ALU.max, negate=True)
                        dve.tensor_reduce(nmax[:, 1, h:h + 1], row[:, P:384], AX.X, ALU.max,
                                          negate=True).then_inc(fox_rows, 1)
                    if s == 20:
                        dve.wait_ge(kv_done, 2 * layer + 1)
                        for c in range(2):
                            for f in range(2):
                                for half in range(2):
                                    p0 = 64 * half
                                    kv = A[c][p0:p0 + 64, f * SEQ + half * P:f * SEQ + (half + 1) * P]
                                    if c == 0:
                                        ins = dve.tensor_copy(states[p0:p0 + 64, f, 0, :], kv)
                                    else:
                                        ins = dve.scalar_tensor_tensor(
                                            out=states[p0:p0 + 64, f, 1, :], in0=states[p0:p0 + 64, f, 0, :],
                                            scalar=aend[p0:p0 + 64, 4 * f + 1:4 * f + 2], in1=kv,
                                            op0=ALU.mult, op1=ALU.add)
                            if c == 0:
                                link(ins)
                        ins.then_inc(state_done, 1)
                    if s == 24:
                        dve.wait_ge(fox_out, HEADS * layer + HEADS)
                        dve.wait_ge(fox_exp, HEADS * layer + HEADS)
                        link(dve.reciprocal(rs[:, 3, :], rsum[:, :, :].rearrange("p t h -> p (t h)")))
                        for t in range(NT):
                            for h in range(HEADS):
                                ins = dve.tensor_scalar(o[:, t, h * HD:(h + 1) * HD], A[t][:, h * HD:(h + 1) * HD],
                                                        rs[:, 3, 4 * t + h:4 * t + h + 1], None, ALU.mult)
                        ins.then_inc(o_done, 1)
                    if s == 25:
                        for t in range(NT):
                            turn_lo(6 * layer + 2 + t + 1, A[2 + t], aT[0][:, 4:8, t * P:(t + 1) * P],
                                    aT[1][:, 4:8, t * P:(t + 1) * P])
                        dve.memset(gsc, 0.0).then_inc(ready0, 1)
                    if s == 26:
                        dve.wait_ge(kv_done, 2 * layer + 2)
                        for f in range(2):
                            for half in range(2):
                                p0 = 64 * half
                                ins = dve.scalar_tensor_tensor(
                                    out=states[p0:p0 + 64, f, 2, :], in0=states[p0:p0 + 64, f, 1, :],
                                    scalar=aend[p0:p0 + 64, 4 * f + 2:4 * f + 3],
                                    in1=A[0][p0:p0 + 64, f * SEQ + half * P:f * SEQ + (half + 1) * P],
                                    op0=ALU.mult, op1=ALU.add)
                        ins.then_inc(state_done, 1)
                    if s in (27, 28):
                        t = s - 27
                        dve.wait_ge(gla_scores, 2 * layer + 2)
                        dve.wait_ge(ready0, layer + 1)
                        if t:
                            dve.wait_ge(gla_out, 2 * layer + 1)
                        for h in range(HEADS):
                            ins = dve.copy_predicated(gsc[:, h * P:(h + 1) * P], chunk_tri.bitcast(i32),
                                                      A[1 - h % 2][:, (h // 2 * 2 + t) * P:(h // 2 * 2 + t + 1) * P])
                        ins.then_inc(gla_att, 1)
                    if s == 29:
                        dve.wait_ge(gla_out, 2 * layer + 2)
                        head_stats(gla_result, False)
                    if s == 31:
                        dve.wait_ge(act_read, reads("act", layer, 9))
                        inverse_root(rs[:, 1, :], rs[:, 2, :])
                        for t in range(NT):
                            for h in range(HEADS):
                                ins = dve.scalar_tensor_tensor(
                                    out=o[:, t, h * HD:(h + 1) * HD], in0=gla_result(t, h),
                                    scalar=rs[:, 2, 4 * t + h:4 * t + h + 1], in1=sgate[:, t, h * HD:(h + 1) * HD],
                                    op0=ALU.mult, op1=ALU.mult)
                        ins.then_inc(o_done, 1)
                    if s == 32:
                        for t in range(NT):
                            turn_lo(6 * layer + 4 + t + 1, A[t], aT[0][:, 0:4, t * P:(t + 1) * P],
                                    aT[1][:, 0:4, t * P:(t + 1) * P])
                    if s >= GATE_S0 + 3 and s <= WO_S0 and (s - GATE_S0) % 3 == 0:
                        j = (s - GATE_S0 - 3) // 3
                        c = (j % 2) * 512
                        dve.wait_ge(act_read, reads("act", layer, 10 + 2 * j))
                        dst = [xn[:, t, c:c + 512] if j < 2 else work[:, t, :] for t in range(NT)]
                        for t in range(NT):
                            ins = dve.tensor_tensor(dst[t], pair(11 + 2 * j)[t][:, :], work[:, t, :], ALU.mult)
                        link_read(ins)
                        if j < 2:
                            dve.tensor_copy(flagf[:, 0:1], bend[:, 0:1]).then_inc(merged, 1)
                        else:
                            for t in range(NT):
                                ins = dve.tensor_tensor(xn[:, t, c:c + 512], xn[:, t, c:c + 512], work[:, t, :], ALU.add)
                            ins.then_inc(merged, 1)
                            dve.wait_ge(merged, N_GB * layer + j + 1)
                    if s in (37, 40):
                        h = int(s == 40)
                        for a in range(2):
                            tile = (4, 0)[h] + 2 * a
                            dve.wait_ge(mT_hi_done, 4 * layer + 2 * h + a + 1)
                            dve.tensor_tensor(aT[1][:, tile:tile + 2, :],
                                              A[2 * h + a][:, :].rearrange("p (k q) -> p k q", k=2),
                                              aT[0][:, tile:tile + 2, :].bitcast(f32), ALU.subtract).then_inc(mT_done, 1)
                    if s == MIX_G - 1:
                        dve.wait_ge(tile0_done, 2 * layer + 1)
                        add_tile(wo_banks[0], 0)
                    else:
                        lo(0, g0 + s + 2)
                return wo_banks[1]

            def dense():
                g0 = FFN_G0

                def product(f1, pair_no):
                    dve.wait_ge(f_silu, f1)
                    dve.tensor_tensor(work[:, 1, :], M[2 * pair_no + 1][:, :], work[:, 0, :], ALU.mult).then_inc(f_prod, 1)

                def product_lo(f1):
                    dve.wait_ge(f_hi, f1)
                    dve.tensor_tensor(gT[1], work[:, 1, :].rearrange("p (k s) -> p k s", k=4), gT[0].bitcast(f32),
                                      ALU.subtract).then_inc(f_lo, 1)

                lo(0, g0 + 2)
                lo(0, g0 + 3)
                dve.wait_ge(gran_done, g0 + 2)
                product(1, 0)
                with dve.Fori(0, (N_FF - 1) // 2) as j:
                    for u in range(2):
                        f = 1 + 2 * j + u
                        product_lo(f)
                        lo(j, g0 + 4 + 3 * u)
                        lo(j, g0 + 5 + 3 * u)
                        dve.wait_ge(gran_done, 6 * j + g0 + 4 + 3 * u)
                        dve.wait_ge(f_lo, f)
                        product(f + 1, (1 + u) % 2)
                        lo(j, g0 + 6 + 3 * u)
                product_lo(N_FF)
                dve.wait_ge(tile0_done, 2)
                add_tile(A[0:2], 0)
                return A[2:4]

            def router():
                dve.wait_ge(gran_done, ROUTER_G + 1)
                link(dve.tensor_copy(lg[:, :, :], M[0][:, 0:16].rearrange("p (t e) -> p t e", t=NT)))
                for t in range(NT):
                    ins = dve.max(top[:, t, :], lg[:, t, :])
                link(ins)
                for t in range(NT):
                    ins = dve.max_index(topi[:, t, :], top[:, t, :], lg[:, t, :])
                link(ins)
                dve.tensor_tensor(tw[:, 0, :], top[:, :, 1], top[:, :, 0], ALU.subtract).then_inc(rt_top, 1)
                link(dve.tensor_copy(topf[:, :, :], topi[:, :, :]))
                e8 = iota[:, 0:N_EXP]
                for t in range(NT):
                    ins = dve.tensor_scalar(picked[:, t, 0:N_EXP], e8, topf[:, t, 0:1], None, ALU.is_equal)
                link(ins)
                for t in range(NT):
                    ins = dve.scalar_tensor_tensor(out=picked[:, t, 0:N_EXP], in0=e8, scalar=topf[:, t, 1:2],
                                                   in1=picked[:, t, 0:N_EXP], op0=ALU.is_equal, op1=ALU.add)
                ins.then_inc(rt_picked, 1)
                dve.wait_ge(rt_exp, 1)
                link(dve.tensor_scalar(tw[:, 0, :], tw[:, 1, :], 1.0, None, ALU.add))
                link(dve.reciprocal(tw[:, 2, :], tw[:, 0, :]))
                link(dve.tensor_tensor(tw[:, 1, :], tw[:, 1, :], tw[:, 2, :], ALU.mult))
                for t in range(NT):
                    dve.tensor_scalar(comb[:, t, 0:N_EXP], e8, topf[:, t, 0:1], tw[:, 2, t:t + 1], ALU.is_equal, ALU.mult)
                    ins = dve.tensor_scalar(lg[:, t, :], e8, topf[:, t, 1:2], tw[:, 1, t:t + 1], ALU.is_equal, ALU.mult)
                link(ins)
                dve.tensor_tensor(comb[:, :, 0:N_EXP], comb[:, :, 0:N_EXP], lg[:, :, :], ALU.add)
                dve.wait_ge(rt_ranked, 1)
                link(dve.tensor_copy(rank[:, :, 0:N_EXP], A[2][:, 0:16].rearrange("p (t e) -> p t e", t=NT)))

            def overflow():
                dve.wait_ge(rt_counted, 1)
                link(dve.tensor_reduce(flagf[:, :], A[2][:, 16:24], AX.X, ALU.max))
                link(dve.tensor_scalar(flagf[:, :], flagf[:, :], -float(P), 0.0, ALU.add, ALU.max))
                dve.tensor_copy(flag[:, :], flagf[:, :]).then_inc(rt_flag, 1)

            def experts(block):
                e0, six0 = N_EXP * block, MOE_G0 // 6 + block * N_EXP * N_EF

                def pick_matrix(dst, weight, e):
                    for t in range(NT):
                        ins = dve.tensor_scalar(dst[:, t, :], iota, rank[:, t, bass.ds(e, 1)],
                                                weight[:, t, bass.ds(e, 1)], ALU.is_equal, ALU.mult)
                    return ins

                def gathered(n):
                    for a in range(2):
                        dve.wait_ge(e_xhi, 2 * n - 1 + a)
                        dve.tensor_tensor(xgT[1][:, 4 * a:4 * a + 4, :],
                                          M[2 + a][:, :].rearrange("p (k s) -> p k s", k=4),
                                          xgT[0][:, 4 * a:4 * a + 4, :].bitcast(f32), ALU.subtract).then_inc(e_xlo, 1)

                def product_lo(n):
                    dve.wait_ge(e_hi, n)
                    dve.tensor_tensor(gT[1], A[2][:, :].rearrange("p (k s) -> p k s", k=4), gT[0].bitcast(f32),
                                      ALU.subtract).then_inc(e_lo, 1)

                def product(n, done):
                    dve.wait_ge(gran_done, done)
                    dve.wait_ge(e_silu, n)
                    dve.tensor_tensor(work[:, 1, :], M[1][:, :], work[:, 0, :], ALU.mult).then_inc(e_prod, 1)

                def round_start(six_f, n):
                    lo(six_f, 6)
                    product_lo(n)

                def round_rest(six_f, n):
                    for local in (7, 8, 9):
                        lo(six_f, local)
                    product(n, 6 * six_f + 8)
                    lo(six_f, 10)
                    lo(six_f, 11)

                def rounds(six, e):
                    round_rest(six, N_EF * e + 2 + N_EF * e0)
                    with dve.Fori(2, N_EF) as f:
                        six_f = six + f - 1
                        round_start(six_f, N_EF * e + f + N_EF * e0)
                        round_rest(six_f, N_EF * e + f + 1 + N_EF * e0)
                    product_lo(N_EF * e + N_EF + N_EF * e0)

                def places(e):
                    dve.wait_ge(e_putw, e + 1 + e0)
                    dve.tensor_reduce(w_place[:, :], A[3][:, 0:SEQ], AX.X, ALU.add)
                    dve.tensor_scalar(put, A[3][:, 0:SEQ], 0.0, None, ALU.is_gt).then_inc(e_put, 1)

                def outputs(e):
                    for c in range(2):
                        half = slice(c * 512, (c + 1) * 512)
                        dve.wait_ge(e_yhi, 2 * e + c + 1 + 2 * e0)
                        dve.scalar_tensor_tensor(out=y_part[1][:, half], in0=A[c][:, :], scalar=w_place[:, 0:1],
                                                 in1=y_part[0][:, half].bitcast(f32), op0=ALU.mult,
                                                 op1=ALU.subtract).then_inc(e_ylo, 1)

                def add_outputs(e):
                    for i, bank in enumerate((A[0], A[1], M[2], M[3])):
                        t, c = i // 2, (i % 2) * 512
                        dve.wait_ge(e_scatter, 4 * e + i + 1 + 4 * e0)
                        ins = dve.tensor_tensor(x[:, t, c:c + 512], bank[:, :], x[:, t, c:c + 512], ALU.add)
                    ins.then_inc(e_added, 1)
                    dve.wait_ge(e_added, e + 2 + e0)

                if block:
                    dve.tensor_scalar(rank[:, :, :], rank[:, :, :], -float(P), None, ALU.add).then_inc(e_moved, 1)
                    dve.wait_ge(e_moved, 1)
                else:
                    dve.memset(spare[:, 1:2], 0.0).then_inc(e_added, 1)
                pick_matrix(pick, picked, 0).then_inc(e_pick, 1)
                lo(six0, 0)
                gathered(e0 + 1)
                lo(six0, 1)
                if not block:
                    overflow()
                for L in range(2, 6):
                    lo(six0, L)
                product(1 + N_EF * e0, 6 * six0 + 4)
                pick_matrix(pick, picked, 1).then_inc(e_pick, 1)
                pick_matrix(pick_w, comb, 0).then_inc(e_pickw, 1)
                round_start(six0, 1 + N_EF * e0)
                with dve.Fori(0, N_EXP - 1) as e:
                    six = 7 * e + six0
                    rounds(six, e)
                    lo(six, 42)
                    gathered(e + 2 + e0)
                    places(e)
                    lo(six, 43)
                    lo(six, 44)
                    outputs(e)
                    lo(six, 45)
                    pick_matrix(pick, picked, e + 2).then_inc(e_pick, 1)
                    pick_matrix(pick_w, comb, e + 1).then_inc(e_pickw, 1)
                    lo(six, 46)
                    product(N_EF * e + N_EF + 1 + N_EF * e0, 6 * six + 46)
                    lo(six, 47)
                    round_start(six + 7, N_EF * e + N_EF + 1 + N_EF * e0)
                    add_outputs(e)
                over = None if block else dve.value_load(flag[0:1, 0:1], min_val=0, max_val=P)
                rounds(six0 + 7 * (N_EXP - 1), N_EXP - 1)
                places(N_EXP - 1)
                outputs(N_EXP - 1)
                add_outputs(N_EXP - 1)
                return over

            dve.memset(one[:, :], 1.0).then_inc(one_set, 1)
            for a in (comb, rank, picked):
                dve.memset(a[:, :, :], 0.0)
            link(dve.memset(gaT[:, :], 1.0))
            norm(0, 0)
            norm(1, FFN_G0, mixers(0))
            norm(2, LAYER_G0[1], dense())
            norm(3, ROUTER_G, mixers(1))
            router()
            over = experts(0)
            with dve.If(over > 0):
                experts(1)
            with dve.Else():
                dve.wait_ge(rt_flag, 1)
            dve.memset(spare[:, :], 0.0).then_inc(fin_x, 1)
            link(dve.tensor_tensor_reduce(xn[:, 0, :], x[:, 0, :], x[:, 0, :], 1.0, 0.0, ALU.mult, ALU.add,
                                          ss[:, 0, 0:1]))
            dve.tensor_scalar(ss[:, 1, 0:1], ss[:, 0, 0:1], 1.0 / D, EPS, ALU.mult, ALU.add).then_inc(fin_var, 1)
            dve.wait_ge(fin_sq, 1)
            dve.tensor_scalar(ss[:, 1, 1:2], sq[:, 1, 0:1], EPS, None, ALU.add).then_inc(fin_var, 1)
            dve.wait_ge(s_gain_fin, 16)
            for t in range(NT):
                dve.wait_ge(fin_root, t + 1)
                link(dve.reciprocal(ss[:, 0, t:t + 1], ss[:, 2, t:t + 1]))
                for c in range(2):
                    half = slice(c * 512, (c + 1) * 512)
                    dve.scalar_tensor_tensor(out=xn[:, t, half], in0=x[:, t, half], scalar=ss[:, 0, t:t + 1],
                                             in1=gain_fin[:, half], op0=ALU.mult, op1=ALU.mult).then_inc(fin_done, 1)

        @block.tensor
        def _(pe):
            def mm3(dst, stat, mov, start, stop):
                pe.matmul(dst, stat[0], mov[0], start=start, stop=False, skip_group_check=True)
                pe.matmul(dst, stat[0], mov[1], start=False, stop=False, skip_group_check=True)
                return pe.matmul(dst, stat[1], mov[0], start=False, stop=stop, skip_group_check=True)

            def weights(local, a, b):
                return w_hi[:, local % RING, a:b], w_lo[:, local % RING, a:b]

            def both(tile, k, a, b):
                return tile[0][:, k, a:b], tile[1][:, k, a:b]

            def arrived(six, local):
                pe.wait_ge(lo_done, 6 * six + local + 1)

            def rows_product(local, banks, source, k0, first, last):
                for t, bank in enumerate(banks):
                    ins = tile_product(local, bank, source, k0, t, first, last)
                ins.then_inc(gran_done, 1)

            def tile_product(local, bank, source, k0, t, first, last):
                for k in range(4):
                    ins = mm3(bank[:, :], both(source, k0 + k, t * P, (t + 1) * P),
                              weights(local, k * 512, (k + 1) * 512), first and k == 0, last and k == 3)
                return ins

            def feature_product(local, banks, half):
                for ft in range(4):
                    for k in range(4):
                        a = k * 512 + ft * P
                        ins = mm3(banks[ft // 2][:, (ft % 2) * SEQ:(ft % 2 + 1) * SEQ], weights(local, a, a + P),
                                  both(hT, 4 * half + k, 0, SEQ), half == 0 and k == 0 and ft % 2 == 0,
                                  half == 1 and k == 3)
                ins.then_inc(gran_done, 1)

            def narrow_product(local):
                for k in range(KT_D):
                    ins = mm3(A[0][:, 0:SEQ], weights(local, k * 256, k * 256 + P), both(hT, k, 0, SEQ),
                              k == 0, k == KT_D - 1)
                ins.then_inc(gran_done, 1)

            def norm(i):
                for t in range(NT):
                    for a in range(2):
                        pe.wait_ge(normed, 4 * i + 2 * t + a + 1)
                        turn_tokens(xn[:, t, a * 512:(a + 1) * 512], A[2 * t + a]).then_inc(x_turned, 1)

            def turn_tokens(src, bank):
                for h in range(HEADS):
                    ins = pe.transpose(bank[:, h * P:(h + 1) * P], src[:, h * P:(h + 1) * P], ident)
                return ins

            def head_out(h, b, att_h):
                v = val[:, b, :, h * HD:(h + 1) * HD]
                dst = slice(h * HD, (h + 1) * HD)
                pe.matmul(A[0][:, dst], att_h[:, 0:P], v[:, 0, :], start=True, stop=True)
                pe.matmul(A[1][:, dst], att_h[:, P:2 * P], v[:, 0, :], start=True, stop=False)
                return pe.matmul(A[1][:, dst], att_h[:, 2 * P:384], v[:, 1, :], start=False, stop=True)

            def mixers(layer):
                g0 = LAYER_G0[layer]
                for s in range(MIX_G):
                    arrived(0, g0 + s)
                    if s == 0:
                        pe.wait_ge(hT_done, 4 * (2 * layer + 1))
                        narrow_product(g0)
                    elif s < GATE_S0:
                        chunk, half = (s - 1) // 2, (s - 1) % 2
                        if half == 0 and chunk >= 2:
                            wait_read(pe, layer, chunk - 2)
                        if CHUNKS[chunk][0] in BY_FEATURE:
                            feature_product(g0 + s, pair(chunk), half)
                        else:
                            rows_product(g0 + s, pair(chunk), hT, 4 * half, half == 0, half == 1)
                    elif s < WO_S0:
                        j, part = (s - GATE_S0) // 3, (s - GATE_S0) % 3
                        chunk = 10 + 2 * j + (part == 2)
                        if part != 1:
                            wait_read(pe, layer, chunk - 2)
                        if part < 2:
                            rows_product(g0 + s, pair(chunk), hT, 4 * part, part == 0, part == 1)
                        else:
                            b = j // 2
                            pe.wait_ge(oT_done, 6 * layer + 2 * b + 2)
                            rows_product(g0 + s, pair(chunk), aT, AT_TILE[BRANCH_ORDER[b]], True, True)
                    else:
                        half, n = (s - WO_S0) // 2, (s - WO_S0) % 2
                        if half == 0:
                            wait_read(pe, layer, 20 + n)
                        pe.wait_ge(mT_done, 4 * layer + 2 * half + 2)
                        if half == 0:
                            rows_product(g0 + s, pair(22 + n), aT, 4, True, False)
                        elif n == 1:
                            for t in range(NT):
                                for m in range(2):
                                    ins = tile_product(g0 + s - 1 + m, pair(22 + m)[t], aT, 0, t, False, True)
                                    if t:
                                        ins.then_inc(gran_done, 1)
                                if t == 0:
                                    ins.then_inc(tile0_done, 1)

                    if s == 1:
                        pe.wait_ge(s_const, 48)
                        pe.wait_ge(ga_done, layer + 1)
                        for t in range(NT):
                            ins = pe.matmul(A[1][:, t * 256:(t + 1) * 256], gaT[0:GLA_RANK + 1, t * P:(t + 1) * P],
                                            a2[:, layer, :], start=True, stop=True)
                        ins.then_inc(z_done, 1)
                    if 3 <= s < 7:
                        i = s - 3
                        pe.wait_ge(rotated, 4 * layer + i + 1)
                        if i >= 2:
                            pe.wait_ge(rot_read, 4 * layer + i - 1)
                        turn_tokens(rot[:, i % 2, :], A[2 + i % 2]).then_inc(rot_turned, 1)
                    if s == 5:
                        pe.wait_ge(loga_done, layer + 1)
                        pe.wait_ge(fz_done, layer + 1)
                        for f in range(2):
                            for t in range(NT):
                                ins = pe.matmul(A[0][:, (2 * f + t) * P:(2 * f + t + 1) * P],
                                                o[:, 1, t * 256 + f * P:t * 256 + (f + 1) * P], chunk_tri,
                                                start=True, stop=True)
                        pe.wait_ge(c_done, layer + 1)
                        for t in range(NT):
                            ins = pe.transpose(A[1][:, 4 * t:4 * t + 4], soft[32:36, 0, t * P:(t + 1) * P],
                                               ident[32:36, 32:36])
                        ins.then_inc(cum_done, 1)
                    if 8 <= s < 8 + HEADS:
                        h = s - 8
                        if h == 0:
                            pe.wait_ge(rot_read, 4 * layer + 4)
                        if h >= 2:
                            pe.wait_ge(ret_att, HEADS * layer + h - 1)
                        bank = A[2 + h % 2]
                        pe.matmul(bank[:, 0:SEQ], kT[:, 0, h, 0:P], qT[:, 0, h, :], start=True, stop=True)
                        pe.matmul(bank[:, SEQ:384], kT[:, 0, h, P:SEQ], qT[:, 0, h, P:SEQ], start=True,
                                  stop=True).then_inc(ret_scores, 1)
                    if 9 <= s < 9 + HEADS:
                        h = s - 9
                        if h == 0:
                            pe.wait_ge(exp_done, layer + 1)
                            pe.wait_ge(cq_done, layer + 1)
                            pe.wait_ge(act_read, reads("act", layer, 2))
                        pe.wait_ge(ret_att, HEADS * layer + h + 1)
                        head_out(h, 0, att[:, h % 2, :]).then_inc(ret_out, 1)
                    if s == 16:
                        pe.wait_ge(o_done, 3 * layer + 1)
                        for t in range(NT):
                            turn_tokens(o[:, t, :], A[2 + t]).then_inc(o_turned, 1)
                    if 17 <= s < 17 + HEADS:
                        h = s - 17
                        if h == 0:
                            pe.wait_ge(oT_done, 6 * layer + 2)
                            pe.wait_ge(act_read, reads("act", layer, 5))
                        else:
                            pe.wait_ge(fox_rows, HEADS * layer + h)
                        for t in range(NT):
                            dst = A[2][:, t * P:t * P + (t + 1) * P]
                            pe.matmul(dst, qT[:, 1, h, t * P:(t + 1) * P], kT[:, 1, h, 0:(t + 1) * P],
                                      start=True, stop=False)
                            ins = pe.matmul(dst, ident[32:36, 32 + h:33 + h].to_broadcast([HEADS, P]),
                                            ncT[32:36, 0:(t + 1) * P], start=False, stop=True)
                        ins.then_inc(fox_scores, 1)
                    if s == 18:
                        pe.wait_ge(gla_ops, layer + 1)
                        for t in range(NT):
                            for f in range(2):
                                ins = pe.transpose(A[0][:, (2 * t + f) * P:(2 * t + f + 1) * P],
                                                   k_end[:, f, t * P:(t + 1) * P], ident)
                        ins.then_inc(kend_turned, 1)
                    if s == 19:
                        pe.wait_ge(kend_done, layer + 1)
                        pe.wait_ge(act_read, reads("act", layer, 8))
                        for f in range(2):
                            for c in range(2):
                                p0 = 64 * c
                                ins = pe.matmul(A[c][:, f * SEQ:(f + 1) * SEQ], k_tok[p0:p0 + 64, 0, f * P:(f + 1) * P],
                                                val[p0:p0 + 64, 0, 0, f * SEQ:(f + 1) * SEQ], start=True, stop=True)
                        ins.then_inc(kv_done, 1)
                    if 19 <= s < 19 + HEADS:
                        h = s - 19
                        pe.wait_ge(fox_exp, HEADS * layer + h + 1)
                        if h >= 1:
                            pe.wait_ge(fox_att, HEADS * layer + h)
                        for i in range(3):
                            ins = pe.transpose(A[3][:, i * P:(i + 1) * P], soft[:, h % 2, i * P:(i + 1) * P], ident)
                        ins.then_inc(fox_turned, 1)
                    if 20 <= s < 20 + HEADS:
                        h = s - 20
                        if h == 0:
                            pe.wait_ge(state_done, 2 * layer + 1)
                        pe.wait_ge(fox_att, HEADS * layer + h + 1)
                        head_out(h, 1, att[:, h % 2, :]).then_inc(fox_out, 1)
                    if s == 24:
                        pe.wait_ge(o_done, 3 * layer + 2)
                        for t in range(NT):
                            turn_tokens(o[:, t, :], A[2 + t]).then_inc(o_turned, 1)
                    if s == 25:
                        p0 = 0
                        for f in range(2):
                            ins = pe.matmul(A[0][:, f * SEQ:(f + 1) * SEQ], k_tok[p0:p0 + 64, 1, f * P:(f + 1) * P],
                                            val[p0:p0 + 64, 0, 1, f * SEQ:(f + 1) * SEQ], start=True, stop=True)
                        ins.then_inc(kv_done, 1)
                    if s in (27, 28):
                        t = s - 27
                        if t == 0:
                            pe.wait_ge(oT_done, 6 * layer + 4)
                        pe.wait_ge(state_done, 2 * layer + 1 + t)
                        pe.wait_ge(gla_att, 2 * layer + t + 1)
                        for h in range(HEADS):
                            f, p0 = h // 2, 64 * (h % 2)
                            out_h = gla_result(t, h)
                            pe.matmul(out_h, gsc[:, h * P:(h + 1) * P],
                                      val[:, 0, t, h * HD:(h + 1) * HD], start=True, stop=False, skip_group_check=True)
                            for c in range(2):
                                if 2 * t + c:
                                    ins = pe.matmul(out_h[64 * c:64 * c + 64, :],
                                                    q_dec[p0:p0 + 64, f, t * P + 64 * c:t * P + 64 * c + 64],
                                                    states[p0:p0 + 64, f, 2 * t + c - 1, :], start=False, stop=c == 1,
                                                    skip_group_check=True)
                        ins.then_inc(gla_out, 1)
                    if s in (25, 26):
                        odd = s - 25
                        if odd:
                            pe.wait_ge(state_done, 2 * layer + 2)
                        for f in range(2):
                            for t in range(NT):
                                p0 = 64 * odd
                                ins = pe.matmul(A[1 - odd][:, (2 * f + t) * P:(2 * f + t + 1) * P],
                                                k_inv[p0:p0 + 64, f, t * P:(t + 1) * P],
                                                q_dec[p0:p0 + 64, f, t * P:(t + 1) * P], start=True, stop=True)
                        ins.then_inc(gla_scores, 1)
                    if s == 31:
                        pe.wait_ge(o_done, 3 * layer + 3)
                        for t in range(NT):
                            turn_tokens(o[:, t, :], A[t]).then_inc(o_turned, 1)
                    if s in (36, 39):
                        h = int(s == 39)
                        pe.wait_ge(merged, N_GB * layer + 5 + h)
                        for a in range(2):
                            for k in range(2):
                                for t in range(NT):
                                    at = (4 * h + 2 * a + k) * P
                                    ins = pe.transpose(A[2 * h + a][:, k * SEQ + t * P:k * SEQ + (t + 1) * P],
                                                       xn[:, t, at:at + P], ident)
                        ins.then_inc(m_turned, 1)

            def dense():
                g0 = FFN_G0

                def hidden(six, local, bank):
                    arrived(six, local)
                    for ft in range(2):
                        for k in range(KT_D):
                            a = k * FF + ft * P
                            ins = mm3(bank[:, ft * SEQ:(ft + 1) * SEQ], weights(local, a, a + P), both(hT, k, 0, SEQ),
                                      k == 0 and ft == 0, k == KT_D - 1)
                    ins.then_inc(gran_done, 1)

                def back(six, local, n, first, last):
                    arrived(six, local)
                    pe.wait_ge(f_lo, n)
                    for t in range(NT):
                        for k in range(2):
                            for c in range(2):
                                stat = (gT[0][:, 2 * k + t, :], gT[1][:, 2 * k + t, :])
                                ins = mm3(A[2 * t + c][:, :], stat, weights(local, k * D + c * 512, k * D + (c + 1) * 512),
                                          first and k == 0, last and k == 1)
                        if last and t == 0:
                            ins.then_inc(tile0_done, 1)
                    ins.then_inc(gran_done, 1)

                pe.wait_ge(hT_done, 4 * 2)
                hidden(0, g0, M[0])
                hidden(0, g0 + 1, M[1])
                hidden(0, g0 + 2, M[2])
                hidden(0, g0 + 3, M[3])
                back(0, g0 + 4, 1, True, False)
                pe.wait_ge(f_prod, 1)
                hidden(0, g0 + 5, M[0])
                hidden(0, g0 + 6, M[1])
                back(0, g0 + 7, 2, False, False)
                with pe.Fori(1, (N_FF - 1) // 2) as j:
                    for u in range(2):
                        f = 1 + 2 * j + u
                        m = 2 * ((1 + u) % 2)
                        pe.wait_ge(f_prod, f)
                        hidden(j, g0 + 2 + 3 * u, M[m])
                        hidden(j, g0 + 3 + 3 * u, M[m + 1])
                        back(j, g0 + 4 + 3 * u, f, False, False)
                back(0, g0 + FFN_G - 1, N_FF, False, True)

            def router():
                arrived(0, ROUTER_G)
                for t in range(NT):
                    pe.wait_ge(hT_done, 4 * 3 + 2 * t + 2)
                    for k in range(KT_D):
                        ins = mm3(M[0][:, 8 * t:8 * t + 8], both(hT, k, t * P, (t + 1) * P),
                                  weights(ROUTER_G, k * 256, k * 256 + N_EXP), k == 0, k == KT_D - 1)
                ins.then_inc(gran_done, 1)
                pe.wait_ge(rt_picked, 1)
                pe.matmul(A[2][:, 0:8], strict, picked[:, 0, 0:N_EXP], start=True, stop=True)
                pe.matmul(A[2][:, 8:16], ones, picked[:, 0, 0:N_EXP], start=True, stop=False)
                pe.matmul(A[2][:, 8:16], strict, picked[:, 1, 0:N_EXP], start=False, stop=True).then_inc(rt_ranked, 1)

            def counts():
                pe.matmul(A[2][:, 16:24], ones, picked[:, 0, 0:N_EXP], start=True, stop=False)
                pe.matmul(A[2][:, 16:24], ones, picked[:, 1, 0:N_EXP], start=False, stop=True).then_inc(rt_counted, 1)

            def experts(block):
                e0, six0 = N_EXP * block, MOE_G0 // 6 + block * N_EXP * N_EF

                def gather(n):
                    pe.wait_ge(e_pick, n + block)
                    for k in range(KT_D):
                        for t in range(NT):
                            ins = pe.matmul(M[2 + k // 4][:, (k % 4) * P:(k % 4 + 1) * P], xn[:, t, k * P:(k + 1) * P],
                                            pick[:, t, :], start=t == 0, stop=t == NT - 1)
                    ins.then_inc(e_gather, 1)

                def hidden(six, local, bank, half):
                    arrived(six, local)
                    rows_product(local, [bank], xgT, 4 * half, half == 0, half == 1)

                def turn_product(n):
                    pe.wait_ge(e_prod, n)
                    turn_tokens(work[:, 1, :], A[2]).then_inc(e_turned, 1)

                def back(six, local, part, first, last):
                    arrived(six, local)
                    for k in range(2):
                        for c in range(2):
                            stat = (gT[0][:, 2 * part + k, :], gT[1][:, 2 * part + k, :])
                            ins = mm3(A[c][:, :], stat, weights(local, k * D + c * 512, k * D + (c + 1) * 512),
                                      first and k == 0, last and k == 1)
                    ins.then_inc(gran_done, 1)

                def round0(six, local, e):
                    pe.wait_ge(e_xlo, 2 * e + 2 + 2 * e0)
                    for L in range(4):
                        hidden(six, local + L, M[L // 2], L % 2)

                def round_(six_f, e, f, first):
                    hidden(six_f, 4, M[0], 0)
                    hidden(six_f, 5, M[0], 1)
                    hidden(six_f, 6, M[1], 0)
                    hidden(six_f, 7, M[1], 1)
                    pe.wait_ge(e_lo, N_EF * e + f + N_EF * e0)
                    if first:
                        pe.wait_ge(e_added, e + 1 + e0)
                    back(six_f, 8, 0, first, False)
                    turn_product(N_EF * e + f + 1 + N_EF * e0)
                    back(six_f, 9, 1, False, False)

                def rounds(six, e, following):
                    round_(six, e, 1, True)
                    with pe.Fori(2, N_EF) as f:
                        round_(six + f - 1, e, f, False)
                    if following:
                        gather(e + 2 + e0)
                    pe.wait_ge(e_pickw, e + 1 + e0)
                    for t in range(NT):
                        ins = pe.transpose(A[3][:, t * P:(t + 1) * P], pick_w[:, t, :], ident)
                    ins.then_inc(e_putw, 1)
                    pe.wait_ge(e_lo, N_EF * e + N_EF + N_EF * e0)
                    back(six, 40, 0, False, False)
                    back(six, 41, 1, False, True)

                def scatter(e):
                    pe.wait_ge(e_ylo, 2 * e + 2 + 2 * e0)
                    for i, bank in enumerate((A[0], A[1], M[2], M[3])):
                        t, c = i // 2, i % 2
                        for h in range(2):
                            ins = pe.matmul(bank[:, :], put[:, t * P:(t + 1) * P], y_part[h][:, c * 512:(c + 1) * 512],
                                            start=h == 0, stop=h == 1)
                        ins.then_inc(e_scatter, 1)

                gather(e0 + 1)
                if not block:
                    counts()
                round0(six0, 0, 0)
                turn_product(1 + N_EF * e0)
                with pe.Fori(0, N_EXP - 1) as e:
                    six = 7 * e + six0
                    rounds(six, e, True)
                    round0(six, 42, e + 1)
                    scatter(e)
                    turn_product(N_EF * e + N_EF + 1 + N_EF * e0)
                over = None
                if not block:
                    pe.wait_ge(rt_flag, 1)
                    over = pe.value_load(flag[0:1, 0:1], min_val=0, max_val=P)
                rounds(six0 + 7 * (N_EXP - 1), N_EXP - 1, False)
                scatter(N_EXP - 1)
                return over

            pe.wait_ge(s_ident, 16)
            norm(0)
            mixers(0)
            norm(1)
            dense()
            norm(2)
            mixers(1)
            norm(3)
            router()
            over = experts(0)
            with pe.If(over > 0):
                experts(1)
            with pe.Else():
                pe.wait_ge(rt_flag, 1)


def _constants():
    f = np.float32
    c = np.zeros((P, C_ALL), f)
    i = np.arange(P)
    c[:, C_ID:C_ID + P] = np.eye(P, dtype=f)
    c[:, C_CAUSAL:C_CAUSAL + P] = np.where(i[:, None] >= i[None, :], 0.0, NEG)
    c[:, C_CHUNK:C_CHUNK + P] = (i[:, None] <= i[None, :]) & (i[:, None] // CHUNK == i[None, :] // CHUNK)
    c[:, C_STRICT:C_STRICT + P] = i[:, None] < i[None, :]
    c[:, C_ONES:C_ONES + P] = 1.0
    c[:, C_IOTA:C_IOTA + P] = i[None, :]
    half = HD // 2
    inv_freq = f(10000.0) ** (-(np.arange(half, dtype=f) / f(half)))
    ang = np.arange(SEQ, dtype=f)[:, None] * inv_freq[None, :].astype(f)
    cos, sin = np.cos(ang).astype(f), np.sin(ang).astype(f)
    c[:, C_COS:C_SIN] = cos.reshape(NT, P, half).transpose(1, 0, 2).reshape(P, -1)
    signed = np.stack([-sin, sin], 1).reshape(NT, P, 2, half)
    c[:, C_SIN:C_DECAY] = signed.transpose(1, 0, 2, 3).reshape(P, -1)
    gamma = np.log1p(-np.exp2(-5.0 - np.arange(HEADS, dtype=np.float64)))
    diff = np.arange(SEQ)[None, :] - i[:, None]
    d = np.where(diff[:, None, :] >= 0, np.exp(np.maximum(diff, 0)[:, None, :] * gamma[None, :, None]), 0.0)
    c[:, C_DECAY:C_ALL] = (d * float(HD) ** -0.5).reshape(P, -1)
    return c


def _stream(w):
    out = np.zeros((TOTAL_G, P, GRAN), np.float32)
    n = 0

    def rows(matrix, k0, nk, c0, nc_):
        nonlocal n
        part = matrix[k0 * P:(k0 + nk) * P, c0:c0 + nc_].reshape(nk, P, nc_)
        out[n].reshape(P, nk, nc_)[:] = part.transpose(1, 0, 2)
        n += 1

    for layer in range(LAYERS):
        w_in = w["w_in"][layer]
        small = out[n].reshape(P, KT_D, 256)
        small[:, :, 0:GLA_RANK] = w_in[:, GA:GA + GLA_RANK].reshape(KT_D, P, GLA_RANK).transpose(1, 0, 2)
        small[:, :, 32:32 + HEADS] = w_in[:, FZ:FZ + HEADS].reshape(KT_D, P, HEADS).transpose(1, 0, 2)
        n += 1
        for _, c0 in CHUNKS:
            for half in range(2):
                rows(w_in, 4 * half, 4, c0, 512)
        for b in BRANCH_ORDER:
            for c in range(2):
                for half in range(2):
                    rows(w["w_gate"][layer], 4 * half, 4, b * D + c * 512, 512)
                rows(w["w_branch"][layer][b], 0, 4, c * 512, 512)
        for half in range(2):
            for c in range(2):
                rows(w["w_o"][layer], 4 * half, 4, c * 512, 512)
        if layer == 0:
            for f in range(N_FF + 1):
                if f < N_FF:
                    rows(w["ffn_w1"][0], 0, 8, f * FF, FF)
                    rows(w["ffn_w3"][0], 0, 8, f * FF, FF)
                if f > 0:
                    rows(w["ffn_w2"][0], 2 * (f - 1), 2, 0, D)
    out[n].reshape(P, KT_D, 256)[:, :, 0:N_EXP] = w["router_w"][0].reshape(KT_D, P, N_EXP).transpose(1, 0, 2)
    n += 1
    for e in range(N_EXP):
        for f in range(N_EF + 1):
            if f < N_EF:
                for m in ("moe_w1", "moe_w3"):
                    for half in range(2):
                        rows(w[m][0, e], 4 * half, 4, f * EF, EF)
            if f > 0:
                for part in range(2):
                    rows(w["moe_w2"][0, e], 4 * (f - 1) + 2 * part, 2, 0, D)
    assert n == TOTAL_G
    return out


def kernel(**inputs):
    import concourse.bacc as _bacc
    from concourse.bass_utils import run_bass_kernel_spmd as _run

    w = {k: np.asarray(v) for k, v in inputs.items()}
    gains = np.stack([w["norm1_g"][0], w["norm2_g"][0], w["norm1_g"][1], w["norm2_g"][1],
                      w["final_g"]])
    a2 = np.concatenate([w["w_gla_a2"], w["b_gla_a"][:, None, :]], axis=1)
    arrays = {
        "stream": _stream(w),
        "x_in": np.ascontiguousarray(w["x"][0].reshape(NT, P, D).transpose(1, 0, 2)),
        "const_in": _constants(),
        "gains_in": gains,
        "b_forget_in": np.ascontiguousarray(w["b_forget"].T),
        "gla_a2_in": np.ascontiguousarray(a2.transpose(1, 0, 2)),
    }
    nc = _bacc.Bacc("TRN2", target_bir_lowering=False, num_devices=1)
    args = [nc.dram_tensor(name, a.shape, mybir.dt.from_np(a.dtype), kind="ExternalInput").ap()
            for name, a in arrays.items()]
    out = nc.dram_tensor("out", (P, NT, D), mybir.dt.float32, kind="ExternalOutput").ap()
    hybrid_decoder_kernel(nc, *args, out)
    r = _run(nc, [arrays], core_ids=[0])
    return r.results[0]["out"].transpose(1, 0, 2).reshape(1, SEQ, D)
```

```python
from contextlib import ExitStack

import numpy as np

import concourse.bass as bass
from concourse import mybir
from concourse.alu_op_type import AluOpType as ALU

P = 128
SEQ, D = 256, 1024
NT = SEQ // P
KT_D = D // P
LAYERS = 2
EPS = 1e-6
HEADS, HD = 4, 128
MIX = HEADS * HD
GLA_DK, GLA_RANK, GLA_TAU, CHUNK = 64, 16, 16.0, 64
D_FF, N_EXP, D_FFE = 2816, 8, 3584

GRAN = 2048
NARROW = 64
RAW, RING = 6, 3
FF = 256
N_FF = D_FF // FF
EF = 512
N_EF = D_FFE // EF
IDLE_START, IDLE_TILE, IDLE_NORM, IDLE_PLACES, IDLE_GATHER = 15, 8, 5, 6, 3
MIX_G = 43
FFN_G0 = MIX_G
FFN_G = 3 * N_FF
LAYER_G0 = (0, FFN_G0 + FFN_G)
ROUTER_G = LAYER_G0[1] + MIX_G
MOE_G0 = ROUTER_G + 1
EXP_G = 6 * N_EF
TOTAL_G = MOE_G0 + N_EXP * EXP_G
N_EARLY = 6
EARLY_LOCAL = EXP_G + 1
assert N_EARLY < N_EXP and EARLY_LOCAL % RAW == 1
assert MOE_G0 % 6 == 0 and EXP_G % 6 == 0 and TOTAL_G % 6 == 0

_W = (MIX, MIX, MIX, HEADS, HEADS * GLA_DK, HEADS * GLA_DK, MIX, GLA_RANK, MIX, MIX, MIX, MIX, MIX)
_AT = [sum(_W[:i]) for i in range(len(_W))]
FQ, FK, FV, FZ, GQ, GK, GV, GA, GR, RQ, RK, RV, RG = _AT
D_IN = sum(_W)
CHUNKS = (("rq", RQ), ("rk", RK), ("rv", RV), ("rg", RG), ("fq", FQ), ("fk", FK), ("fv", FV),
          ("gqk", GQ), ("gv", GV), ("gr", GR))
BY_FEATURE = ("fq", "fk", "gqk")
BRANCH_ORDER = (2, 0, 1)
N_GB = 2 * len(BRANCH_ORDER)
GATE_S0 = 1 + 2 * len(CHUNKS)
WO_S0 = GATE_S0 + 3 * N_GB
assert WO_S0 + 4 == MIX_G
READER = ["dve", "dve", "act", "act", "act", "act", "act", "dve", "act", "act"] + ["act", "dve"] * N_GB
AT_TILE = {2: 0, 0: 4, 1: 0}

C_ID, C_STRICT, C_ONES, C_IOTA, C_CAUSAL, C_CHUNK, C_COS = (P * i for i in range(7))
C_SIN = C_COS + NT * 64
C_DECAY = C_SIN + NT * P
C_ALL = C_DECAY + HEADS * SEQ
NEG = -1e30


def hybrid_decoder_kernel(nc, stream, x_in, const_in, gains_in, b_forget, gla_a2, out):
    f32, f32r, i32, u32 = mybir.dt.float32, mybir.dt.float32r, mybir.dt.int32, mybir.dt.uint32
    ACT, AX = mybir.ActivationFunctionType, mybir.AxisListType

    with ExitStack() as ctx:
        def sb(name, shape, dt=f32):
            return ctx.enter_context(nc.sbuf_tensor(name, shape, dt))

        def sem(name):
            return ctx.enter_context(nc.semaphore(name))

        raw = sb("raw", [P, RAW, GRAN])
        w_hi = sb("w_hi", [P, RING, GRAN], f32r)
        w_lo = sb("w_lo", [P, RING, GRAN], f32r)
        x = sb("x", [P, NT, D])
        xn = sb("xn", [P, NT, D])
        hT = [sb(f"hT_{h}", [P, KT_D, SEQ], f32r) for h in ("hi", "lo")]
        aT = [sb(f"aT_{h}", [P, 8, SEQ], f32r) for h in ("hi", "lo")]
        mix = sb("mix", [P, C_ALL - C_CAUSAL + 4 * 384 + 2 * NT * MIX + 2 * 2 * HEADS * SEQ + 2 * NT * MIX
                         + LAYERS * 256 + 2 * SEQ])
        places_left = [0]

        def carve(*shape):
            n = int(np.prod(shape))
            at = places_left[0]
            places_left[0] += n
            if len(shape) == 1:
                return mix[:, at:at + n]
            names = "abc"[:len(shape)]
            return mix[:, at:at + n].rearrange(f"p ({' '.join(names)}) -> p {' '.join(names)}",
                                               **dict(zip(names, shape)))

        causal, chunk_tri = carve(P), carve(P)
        cos, sin, decay = carve(NT, 64), carve(NT, 2, 64), carve(HEADS, SEQ)
        soft = carve(2, 384)
        att = carve(2, 384)
        sgate = carve(NT, MIX)
        places_o = places_left[0]
        o = carve(NT, MIX)
        qT, kT = ([carve(HEADS, SEQ) for _ in range(2)] for _ in range(2))
        val = [carve(NT, MIX) for _ in range(2)]
        a2 = carve(LAYERS, 256)[0:GLA_RANK + 1]
        gaT = carve(SEQ)[0:32]
        ncT = carve(SEQ)[0:36]
        work = sb("work", [P, 2, 512])
        rot = sb("rot", [P, 2, 512])
        cst = sb("cst", [P, C_CAUSAL])
        bf = sb("bf", [36, LAYERS])
        cq = sb("cq", [P, 8])
        bend = sb("bend", [P, 8])
        aend = sb("aend", [P, 8])
        stats = sb("stats", [P, 8, 6])
        mv = sb("mv", [P, 8, 2])
        rs = sb("rs", [P, 4, 8])
        sq = sb("sq", [P, NT, 2])
        ss = sb("ss", [P, 3, NT])
        spare = sb("spare", [P, 3])
        one = sb("one", [P, 1])
        zeros = sb("zeros", [P, P])
        w_place = sb("w_place", [P, 1])
        nmax = sb("nmax", [P, NT, HEADS])
        rsum = sb("rsum", [P, NT, HEADS])
        lgT = sb("lgT", [8, SEQ])
        lg = sb("lg", [P, NT, 8])
        top = sb("top", [P, NT, 8])
        topi = sb("topi", [P, NT, 8], u32)
        topf = sb("topf", [P, NT, 8])
        tw = sb("tw", [P, 3, NT])
        comb = sb("comb", [P, NT, N_EXP + 1])
        rank = sb("rank", [P, NT, N_EXP + 1])
        picked = sb("picked", [P, NT, N_EXP + 1])
        flag = sb("flag", [P, 1], i32)
        flagf = sb("flagf", [P, 1])

        ident = cst[:, C_ID:C_ID + P]
        strict = cst[:, C_STRICT:C_STRICT + P]
        ones = cst[:, C_ONES:C_ONES + P]
        iota = cst[:, C_IOTA:C_IOTA + P]
        gsc = mix[:, C_ALL - C_CAUSAL:C_ALL - C_CAUSAL + 512]
        states = rot[:, :, :].rearrange("p a b -> p (a b)")[:, 0:768].rearrange("p (f c v) -> p f c v", f=2, c=3)
        q_dec, k_inv = (qT[0][:, 2 * i:2 * i + 2, :] for i in range(2))
        k_end = kT[0][:, 0:2, :]
        k_tok = kT[0][:, 2:4, :]
        xgT = [h[:, 0:4, :].rearrange("p k (a s) -> p (k a) s", a=2) for h in hT]
        gT = [h[:, 0:2, :].rearrange("p k (a s) -> p (k a) s", a=2) for h in aT]
        pick = rot[:, 0, 0:SEQ].rearrange("p (t s) -> p t s", t=NT)
        pick_w = rot[:, 0, SEQ:512].rearrange("p (t s) -> p t s", t=NT)
        gT_last = [h[:, 4:6, :].rearrange("p k (a s) -> p (k a) s", a=2) for h in hT]
        gT_end = [h[:, 2:4, :].rearrange("p k (a s) -> p (k a) s", a=2) for h in aT]
        put = aT[0][:, 2, :]
        y_part = [h[:, 4:8, :].rearrange("p k s -> p (k s)") for h in aT]
        gain = mix[:, places_o:places_o + D]
        gain_exp = rot[:, :, :].rearrange("p a b -> p (a b)")
        gain_fin = raw[:, 0, 0:D]

        M = [ctx.enter_context(nc.psum_tensor(f"M{i}", [P, 512], f32)) for i in range(4)]
        A = [ctx.enter_context(nc.psum_tensor(f"A{i}", [P, 512], f32)) for i in range(4)]

        loaded = [sem(f"loaded{i}") for i in range(RAW)]
        early_loaded = sem("early_loaded")
        s_in = [sem(f"x_loaded{t}") for t in range(NT)]
        s_ident, s_const, s_tables = sem("identity_loaded"), sem("constants_loaded"), sem("tables_loaded")
        s_gain, s_gain_fin = sem("gain_loaded"), sem("final_gain_loaded")
        hi_done, lo_done, gran_done = sem("hi_done"), sem("lo_done"), sem("gran_done")
        act_read, dve_read = sem("act_read"), sem("dve_read")
        act_own, dve_own = sem("act_own"), sem("dve_own")
        ready0 = sem("dve_ready")
        sumsq, normed, x_turned, hT_hi_done, hT_done = (
            sem(n) for n in ("sumsq", "normed", "x_turned", "hT_hi_done", "hT_done"))
        zeros_set, one_set, root_in, root_done = sem("zeros_set"), sem("one_set"), sem("root_in"), sem("root_done")
        x_new, tile0_done, left_done = sem("x_new"), sem("tile0_done"), sem("left_done")
        ga_done, z_done, fz_done, fln_done, c_done = (sem(n) for n in ("ga_done", "z_done", "fz_done", "fln_done", "c_done"))
        zln_done, loga_done, cum_done, cq_done, bend_done, exp_done = (
            sem(n) for n in ("zln_done", "loga_done", "cum_done", "cq_done", "bend_done", "exp_done"))
        rotated, rot_turned, rot_read = sem("rotated"), sem("rot_turned"), sem("rot_read")
        ret_scores, ret_att, ret_out = sem("ret_scores"), sem("ret_att"), sem("ret_out")
        val_done, silu_done, fq_done = sem("val_done"), sem("silu_done"), sem("fq_done")
        fox_scores, fox_rows, fox_exp, fox_turned, fox_att, fox_out = (
            sem(n) for n in ("fox_scores", "fox_rows", "fox_exp", "fox_turned", "fox_att", "fox_out"))
        gla_ops, kend_turned, kend_done, kv_done, state_done = (
            sem(n) for n in ("gla_ops", "kend_turned", "kend_done", "kv_done", "state_done"))
        gla_scores, gla_att, gla_out = sem("gla_scores"), sem("gla_att"), sem("gla_out")
        o_done, o_turned, oT_hi_done, oT_done = (sem(n) for n in ("o_done", "o_turned", "oT_hi_done", "oT_done"))
        gate_done, merged = sem("gate_done"), sem("merged")
        m_turned, mT_hi_done, mT_done = sem("m_turned"), sem("mT_hi_done"), sem("mT_done")
        f_silu, f_prod, f_hi, f_lo = (sem(n) for n in ("f_silu", "f_prod", "f_hi", "f_lo"))
        rt_copied, rt_turned, rt_top, rt_exp, rt_picked, rt_ranked, rt_counted, rt_flag = (
            sem(n) for n in ("rt_copied", "rt_turned", "rt_top", "rt_exp", "rt_picked", "rt_ranked", "rt_counted", "rt_flag"))
        e_moved, e_left = sem("e_moved"), sem("e_left")
        e_pick, e_gather, e_xhi, e_xlo = (sem(n) for n in ("e_pick", "e_gather", "e_xhi", "e_xlo"))
        e_silu, e_prod, e_turned, e_hi, e_lo = (sem(n) for n in ("e_silu", "e_prod", "e_turned", "e_hi", "e_lo"))
        e_pickw, e_putw, e_put, e_yhi, e_ylo, e_scatter = (
            sem(n) for n in ("e_pickw", "e_putw", "e_put", "e_yhi", "e_ylo", "e_scatter"))
        e_added = [sem(f"e_added{c}") for c in range(2)]
        fin_x, fin_sq, fin_var, fin_root, fin_done, stored = (
            sem(n) for n in ("fin_x", "fin_sq", "fin_var", "fin_root", "fin_done", "stored"))
        block = ctx.enter_context(nc.Block())

        def reads(engine, layer, chunk):
            return layer * READER.count(engine) + READER[:chunk + 1].count(engine)

        def wait_read(pe, layer, chunk):
            if READER[chunk] == "act":
                pe.wait_ge(act_read, reads("act", layer, chunk))
            else:
                pe.wait_ge(dve_read, reads("dve", layer, chunk))

        def gla_result(t, h):
            at = (2 * t + h // 2) * HD
            return A[2 + h % 2][:, at:at + HD]

        def by_tile(t, h):
            return A[t][:, h * HD:(h + 1) * HD]

        def pair(chunk):
            return M[2 * (chunk % 2):2 * (chunk % 2) + 2]

        @block.sync
        def _(sp):
            def load(six, local, source, first=False):
                if not first:
                    sp.wait_ge(lo_done, 6 * six + local - RAW + 1)
                sp.dma_start(raw[:, local % RAW, :], source).then_inc(loaded[local % RAW], 16)

            def load_early(e):
                sp.dma_start(mix[:, e * GRAN:(e + 1) * GRAN],
                             stream[MOE_G0 + e * EXP_G + EARLY_LOCAL]).then_inc(early_loaded, 16)

            for t in range(NT):
                sp.dma_start(x[:, t, :], x_in[:, t, :]).then_inc(s_in[t], 16)
            sp.dma_start(ident, const_in[:, C_ID:C_ID + P]).then_inc(s_ident, 16)
            used = KT_D * NARROW
            sp.dma_start(raw[:, 0, 0:used], stream[0][:, 0:used]).then_inc(loaded[0], 16)
            for g in range(1, RAW):
                load(0, g, stream[g], first=True)
            six_of = stream.rearrange("(s u) p n -> s u p n", u=6)
            with sp.Fori(1, MOE_G0 // 6) as six:
                for u in range(6):
                    load(six, u, six_of[six, u])
            sp.wait_ge(o_turned, 12)
            for e in range(N_EARLY):
                load_early(e)
            for u in range(6):
                load(0, MOE_G0 + u, stream[MOE_G0 + u])

            def load_group(shift, six):
                for u in range(6):
                    load(six + MOE_G0 // 6 + shift, u, six_of[six + MOE_G0 // 6, u])

            def load_experts(shift):
                load_group(shift, 1)
                with sp.Fori(0, N_EARLY) as e:
                    with sp.Fori(2, N_EF) as k:
                        load_group(shift, N_EF * e + k)
                    first = N_EF * e + N_EF
                    for u in range(6):
                        if u != EARLY_LOCAL % 6:
                            load(first + MOE_G0 // 6 + shift, u, six_of[first + MOE_G0 // 6, u])
                    for u in range(6):
                        local = u if u != EARLY_LOCAL % 6 else u - 6
                        sp.wait_ge(lo_done, 6 * (first + MOE_G0 // 6 + shift + 1) + local - RAW + 1)
                        sp.dma_start(raw[:, u, :], six_of[first + MOE_G0 // 6 + 1, u]).then_inc(loaded[u], 16)
                with sp.Fori(N_EF * N_EARLY + 2, N_EF * N_EXP) as k:
                    load_group(shift, k)

            load_experts(0)
            sp.wait_ge(rt_flag, 1)
            over = sp.value_load(flag[0:1, 0:1], min_val=0, max_val=P)
            with sp.If(over > 0):
                load_group(N_EXP * N_EF, 0)
                load_experts(N_EXP * N_EF)
                sp.wait_ge(lo_done, TOTAL_G + N_EXP * EXP_G - 5)
            with sp.Else():
                sp.wait_ge(lo_done, TOTAL_G - 5)
            sp.dma_start(gain_fin, gains_in[4].partition_broadcast(P)).then_inc(s_gain_fin, 16)
            for t in range(NT):
                for c in range(2):
                    sp.wait_ge(fin_done, 2 * t + c + 1)
                    sp.dma_start(out[:, t, c * 512:(c + 1) * 512], xn[:, t, c * 512:(c + 1) * 512]).then_inc(stored, 16)
            sp.wait_ge(stored, 16 * 2 * NT)

        @block.gpsimd
        def _(pool):
            def load_gain(i, dst):
                pool.dma_start(dst, gains_in[i].partition_broadcast(P)).then_inc(s_gain, 16)

            load_gain(0, gain)
            pool.dma_start(bf[32:36, :], b_forget).then_inc(s_const, 16)
            pool.dma_start(a2[:, :, :], gla_a2).then_inc(s_const, 16)
            pool.dma_start(cst[:, P:C_CAUSAL], const_in[:, P:C_CAUSAL]).then_inc(s_const, 16)
            pool.dma_start(mix[:, 0:C_ALL - C_CAUSAL], const_in[:, C_CAUSAL:C_ALL]).then_inc(s_tables, 16)
            pool.wait_ge(o_turned, 6)
            load_gain(1, gain)
            pool.wait_ge(normed, 4 * 2)
            load_gain(2, gain)
            pool.wait_ge(o_turned, 12)
            load_gain(3, gain_exp)

        @block.scalar
        def _(act):
            own = [0]

            def link(ins):
                own[0] += 1
                ins.then_inc(act_own, 1)
                act.wait_ge(act_own, own[0])

            def copy(dst, src, **kw):
                return act.activation(dst, src, ACT.Copy, **kw)

            def hi(six, local, loads=None, width=GRAN):
                act.wait_ge(loaded[local % RAW], 16 * ((six if loads is None else loads) + local // RAW + 1))
                if not (isinstance(six, int) and 6 * six + local < RING):
                    act.wait_ge(gran_done, 6 * six + local - RING + 1)
                copy(w_hi[:, local % RING, 0:width], raw[:, local % RAW, 0:width]).then_inc(hi_done, 1)

            def hi_early(six, e):
                act.wait_ge(gran_done, 6 * six + EARLY_LOCAL - RING + 1)
                copy(w_hi[:, EARLY_LOCAL % RING, :], mix[:, bass.ds(e * GRAN, GRAN)]).then_inc(hi_done, 1)

            def squares(t, i):
                for c in range(2):
                    if i == 0:
                        act.wait_ge(s_in[t], 16)
                    else:
                        act.wait_ge(x_new, 4 * (i - 1) + 2 * t + c + 1)
                    half = slice(c * 512, (c + 1) * 512)
                    act.activation(xn[:, t, half], x[:, t, half], ACT.Square, scale=float(D) ** -0.5,
                                   accum_out=sq[:, t, c:c + 1]).then_inc(sumsq, 1)

            def root(src, dst):
                act.wait_ge(root_in, roots[0] + 1)
                act.activation(dst, src, ACT.Sqrt).then_inc(root_done, 1)
                roots[0] += 1

            def before_norm():
                act.wait_ge(one_set, 1)
                act.activation(spare[:, 0:1], one[:, :], ACT.Sqrt)

            def norm(i, following):
                root(ss[:, 1, 0:1], ss[:, 2, 0:1])
                if i:
                    hi(0, following + 1)
                squares(1, i)
                root(ss[:, 1, 1:2], ss[:, 2, 1:2])
                for t in range(NT):
                    if not i and t:
                        hi(0, following, width=KT_D * NARROW)
                    for a in range(2):
                        act.wait_ge(x_turned, 4 * i + 2 * t + a + 1)
                        copy(hT[0][:, 4 * a:4 * a + 4, t * P:(t + 1) * P],
                             A[2 * t + a][:, :].rearrange("p (k s) -> p k s", k=4)).then_inc(hT_hi_done, 1)
                if not i:
                    hi(0, following + 1)

            roots = [0]

            def turn_hi(n, bank, dst):
                act.wait_ge(o_turned, n)
                copy(dst, bank[:, :].rearrange("p (h q) -> p h q", h=HEADS)).then_inc(oT_hi_done, 1)

            def mixers(layer):
                g0 = LAYER_G0[layer]
                for s in range(MIX_G):
                    if 0 < s < MIX_G - 1:
                        act.wait_ge(gran_done, g0 + s)
                    if s == 1:
                        act.wait_ge(s_const, 48)
                        copy(gaT[0:GLA_RANK, :], A[0][0:GLA_RANK, 0:SEQ]).then_inc(ga_done, 1)
                    if s == 2:
                        act.wait_ge(fz_done, layer + 1)
                        e = att[32:36, 1, 0:SEQ]
                        link(act.activation(e, att[32:36, 0, 0:SEQ], ACT.Abs))
                        link(act.activation(e, e, ACT.Exp, scale=-1.0))
                        act.activation(e, e, ACT.Ln, bias=1.0).then_inc(fln_done, 1)
                    if s == 3:
                        act.wait_ge(z_done, layer + 1)
                        e = o[:, 0, :]
                        link(act.activation(e, A[1][:, :], ACT.Abs))
                        link(act.activation(e, e, ACT.Exp, scale=-1.0))
                        act.activation(e, e, ACT.Ln, bias=1.0).then_inc(zln_done, 1)
                    if 4 <= s < 8:
                        i = s - 4
                        act.wait_ge(rot_turned, 4 * layer + i + 1)
                        dst = (qT if i < 2 else kT)[0][:, :, (i % 2) * P:(i % 2 + 1) * P]
                        copy(dst, A[2 + i % 2][:, :].rearrange("p (h q) -> p h q", h=HEADS)).then_inc(rot_read, 1)
                    if s in (7, 15, 19):
                        b, chunk = ((0, 2), (1, 6), (0, 8))[(7, 15, 19).index(s)]
                        if b == 0 and s == 19:
                            act.wait_ge(ret_out, layer * HEADS + HEADS)
                        act.wait_ge(fox_out, layer * HEADS) if layer and b else None
                        for t in range(NT):
                            ins = copy(val[b][:, t, :], pair(chunk)[t][:, :])
                        ins.then_inc(act_read, 1)
                    if s == 7:
                        act.wait_ge(bend_done, layer + 1)
                        act.wait_ge(rotated, 4 * layer + 4)
                        act.activation(work[:, 0, :], A[0][:, :], ACT.Exp, scale=1.0 / GLA_TAU)
                        act.activation(work[:, 1, :], A[0][:, :], ACT.Exp, scale=-1.0 / GLA_TAU)
                    if s == 8:
                        act.wait_ge(rot_turned, 4 * layer + 3)
                        for i in range(8):
                            act.activation(rot[:, 0, i * 64:(i + 1) * 64], A[0][:, i * 64:(i + 1) * 64], ACT.Exp,
                                           scale=-1.0 / GLA_TAU, bias=bend[:, i:i + 1])
                        act.activation(aend[:, :], bend[:, :], ACT.Exp).then_inc(exp_done, 1)
                    if s in (9, 21):
                        for t in range(NT):
                            ins = act.activation(sgate[:, t, :], pair(3 if s == 9 else 9)[t][:, :], ACT.Silu)
                        ins.then_inc(act_read, 1)
                    if s == 11:
                        for j in range(2):
                            ins = copy(qT[1][:, 2 * j:2 * j + 2, :], pair(4)[j][:, :].rearrange("p (h q) -> p h q", h=2),
                                       scale=float(HD) ** -0.5)
                        ins.then_inc(act_read, 1)
                    if s == 13:
                        for j in range(2):
                            ins = copy(kT[1][:, 2 * j:2 * j + 2, :], pair(5)[j][:, :].rearrange("p (h q) -> p h q", h=2))
                        ins.then_inc(act_read, 1)
                    if s == 14:
                        root(rs[:, 0, :], rs[:, 1, :])
                    if s == 17:
                        for t in range(NT):
                            turn_hi(6 * layer + t + 1, A[2 + t], aT[0][:, 0:4, t * P:(t + 1) * P])
                    if 19 <= s < 19 + HEADS:
                        h = s - 19
                        act.wait_ge(fox_rows, HEADS * layer + h + 1)
                        act.activation(soft[:, h % 2, 0:P], soft[:, h % 2, 0:P], ACT.Exp, bias=nmax[:, 0, h:h + 1],
                                       accum_out=rsum[:, 0, h:h + 1])
                        act.activation(soft[:, h % 2, P:384], soft[:, h % 2, P:384], ACT.Exp, bias=nmax[:, 1, h:h + 1],
                                       accum_out=rsum[:, 1, h:h + 1]).then_inc(fox_exp, 1)
                    if s == 19:
                        act.wait_ge(kend_turned, layer + 1)
                        copy(k_tok, A[0][:, :].rearrange("p (t f) -> p t f", t=2)).then_inc(kend_done, 1)
                    if 20 <= s < 20 + HEADS:
                        h = s - 20
                        act.wait_ge(fox_turned, HEADS * layer + h + 1)
                        copy(att[:, h % 2, :], A[3][:, 0:384]).then_inc(fox_att, 1)
                    if s == 25:
                        for t in range(NT):
                            turn_hi(6 * layer + 2 + t + 1, A[2 + t], aT[0][:, 4:8, t * P:(t + 1) * P])
                    if s == 30:
                        root(rs[:, 0, :], rs[:, 1, :])
                    if s == 32:
                        for t in range(NT):
                            turn_hi(6 * layer + 4 + t + 1, A[t], aT[0][:, 0:4, t * P:(t + 1) * P])
                    if s >= GATE_S0 + 2 and s < WO_S0 and (s - GATE_S0 - 2) % 3 == 0:
                        j = (s - GATE_S0 - 2) // 3
                        if j or layer:
                            act.wait_ge(merged, N_GB * layer + j)
                        else:
                            act.wait_ge(gla_ops, 1)
                        for t in range(NT):
                            ins = act.activation(work[:, t, :], pair(10 + 2 * j)[t][:, :], ACT.Sigmoid)
                        ins.then_inc(act_read, 1)
                    if s in (37, 40):
                        h = int(s == 40)
                        act.wait_ge(m_turned, 2 * layer + h + 1)
                        for a in range(2):
                            tile = (4, 0)[h] + 2 * a
                            copy(aT[0][:, tile:tile + 2, :],
                                 A[2 * h + a][:, :].rearrange("p (k q) -> p k q", k=2)).then_inc(mT_hi_done, 1)
                    if s == MIX_G - 1:
                        before_norm()
                        squares(0, 2 * layer + 1)
                    else:
                        hi(0, g0 + s + 2)

            def dense():
                g0 = FFN_G0

                def silu(f_expr, pair_no):
                    act.activation(work[:, 0, :], M[2 * pair_no][:, :], ACT.Silu).then_inc(f_silu, 1)

                hi(0, g0 + 2)
                act.wait_ge(gran_done, g0 + 1)
                silu(0, 0)
                hi(0, g0 + 3)
                with act.Fori(0, (N_FF - 1) // 2) as j:
                    for u in range(2):
                        f = 1 + 2 * j + u
                        act.wait_ge(gran_done, 6 * j + g0 + 2 + 3 * u)
                        act.wait_ge(f_prod, f)
                        copy(gT[0], work[:, 1, :].rearrange("p (k s) -> p k s", k=4)).then_inc(f_hi, 1)
                        hi(j, g0 + 4 + 3 * u)
                        act.wait_ge(gran_done, 6 * j + g0 + 3 + 3 * u)
                        silu(f, (1 + u) % 2)
                        hi(j, g0 + 5 + 3 * u)
                        hi(j, g0 + 6 + 3 * u)
                act.wait_ge(f_prod, N_FF)
                copy(gT_end[0], work[:, 1, :].rearrange("p (k s) -> p k s", k=4)).then_inc(f_hi, 1)
                before_norm()
                squares(0, 2)

            def experts(block):
                e0, six0 = N_EXP * block, MOE_G0 // 6 + block * N_EXP * N_EF
                loads0 = six0 - N_EARLY * block

                def gathered(n):
                    for a in range(2):
                        act.wait_ge(e_gather, 2 * n - 1 + a)
                        copy(xgT[0][:, 4 * a:4 * a + 4, :],
                             M[2 + a][:, :].rearrange("p (k s) -> p k s", k=4)).then_inc(e_xhi, 1)

                def product_hi(n, dst=gT):
                    act.wait_ge(e_turned, n)
                    copy(dst[0], A[2][:, :].rearrange("p (k s) -> p k s", k=4)).then_inc(e_hi, 1)

                def silu(done):
                    act.wait_ge(gran_done, done)
                    act.activation(work[:, 0, :], M[0][:, :], ACT.Silu).then_inc(e_silu, 1)

                def split(six_f, local, loads):
                    hi(six_f, local, loads if local % RAW == EARLY_LOCAL % RAW else six_f)

                def round_(six_f, loads, n, product_after, last=False):
                    for u in range(6):
                        if u == 2:
                            silu(6 * six_f + 4 + 2)
                        if u == 5 and last:
                            product_hi(n + 1, gT_last)
                        split(six_f, 6 + u, loads)
                        if u == product_after:
                            product_hi(n)

                def rounds(six, e, loads):
                    n = N_EF * e + N_EF * e0
                    round_(six, loads, n + 1, 1)
                    with act.Fori(2, N_EF - 1) as f:
                        round_(six + f - 1, loads + f - 1, n + f, 0)
                    round_(six + N_EF - 2, loads + N_EF - 2, n + N_EF - 1, 0, last=True)

                def outputs(six, e):
                    act.wait_ge(e_put, e + 1 + e0)
                    for c in range(2):
                        if c == 0:
                            act.wait_ge(e_left, e + 1 + e0)
                        else:
                            act.wait_ge(gran_done, 6 * six + 42)
                        act.activation(y_part[0][:, c * 512:(c + 1) * 512], A[c][:, :], ACT.Copy,
                                       scale=w_place[:, 0:1]).then_inc(e_yhi, 1)

                if block:
                    split(six0, 0, loads0)
                    split(six0, 1, loads0)
                split(six0, 2, loads0)
                if not block:
                    act.activation(spare[:, 0:1], one[:, :], ACT.Silu)
                gathered(e0 + 1)
                split(six0, 3, loads0)
                silu(6 * six0 + 2)
                split(six0, 4, loads0)
                split(six0, 5, loads0)
                act.wait_ge(early_loaded, 16 * N_EARLY)

                def expert(e, early):
                    six = N_EF * e + six0
                    loads = (N_EF - 1) * e + loads0 if early else six0 + N_EF * e - N_EARLY * (block + 1)
                    rounds(six, e, loads)
                    split(six, 42, loads)
                    gathered(e + 2 + e0)
                    if early:
                        hi_early(six, e)
                    else:
                        split(six, 43, loads)
                    split(six, 44, loads)
                    outputs(six, e)
                    split(six, 45, loads)
                    silu(6 * six + 44)
                    split(six, 46, loads)
                    split(six, 47, loads)

                with act.Fori(0, N_EARLY) as e:
                    expert(e, True)
                for e in range(N_EARLY, N_EXP - 1):
                    expert(e, False)
                over = None
                if not block:
                    act.wait_ge(rt_flag, 1)
                    over = act.value_load(flag[0:1, 0:1], min_val=0, max_val=P)
                rounds(six0 + N_EF * (N_EXP - 1), N_EXP - 1, six0 + N_EF * (N_EXP - 1) - N_EARLY * (block + 1))
                before_norm()
                outputs(six0 + N_EF * (N_EXP - 1), N_EXP - 1)
                return over

            before_norm()
            squares(0, 0)
            norm(0, 0)
            mixers(0)
            norm(1, FFN_G0)
            dense()
            norm(2, LAYER_G0[1])
            mixers(1)
            norm(3, ROUTER_G)
            hi(0, ROUTER_G + 2)
            act.wait_ge(gran_done, ROUTER_G + 1)
            copy(lgT[:, :], A[0][0:8, 0:SEQ]).then_inc(rt_copied, 1)
            act.wait_ge(rt_top, 1)
            act.activation(tw[:, 1, :], tw[:, 0, :], ACT.Exp).then_inc(rt_exp, 1)
            over = experts(0)
            with act.If(over > 0):
                experts(1)
            with act.Else():
                act.wait_ge(rt_flag, 1)
            act.wait_ge(fin_x, 1)
            act.activation(xn[:, 1, :], x[:, 1, :], ACT.Square, scale=float(D) ** -0.5,
                           accum_out=sq[:, 1, 0:1]).then_inc(fin_sq, 1)
            for t in range(NT):
                act.wait_ge(fin_var, t + 1)
                act.activation(ss[:, 2, t:t + 1], ss[:, 1, t:t + 1], ACT.Sqrt).then_inc(fin_root, 1)

        @block.vector
        def _(dve):
            own = [0]

            def link(ins):
                own[0] += 1
                ins.then_inc(dve_own, 1)
                dve.wait_ge(dve_own, own[0])

            def lo(six, local, width=GRAN):
                dve.wait_ge(hi_done, 6 * six + local + 1)
                dve.tensor_tensor(w_lo[:, local % RING, 0:width], raw[:, local % RAW, 0:width],
                                  w_hi[:, local % RING, 0:width].bitcast(f32), ALU.subtract).then_inc(lo_done, 1)

            def lo_early(six, e):
                dve.wait_ge(hi_done, 6 * six + EARLY_LOCAL + 1)
                dve.tensor_tensor(w_lo[:, EARLY_LOCAL % RING, :], mix[:, bass.ds(e * GRAN, GRAN)],
                                  w_hi[:, EARLY_LOCAL % RING, :].bitcast(f32), ALU.subtract).then_inc(lo_done, 1)

            roots = [0]

            def inverse_root(var, n):
                dve.wait_ge(root_done, roots[0])
                link(dve.reciprocal(n, var))

            def add_half(banks, t, c):
                dve.tensor_tensor(x[:, t, c * 512:(c + 1) * 512], banks[c][:, :],
                                  x[:, t, c * 512:(c + 1) * 512], ALU.add).then_inc(x_new, 1)

            def add_tile(banks, t):
                for c in range(2):
                    add_half(banks, t, c)

            def norm_tile(i, t):
                dve.wait_ge(sumsq, 4 * i + 2 * t + 2)
                roots[0] += 1
                dve.scalar_tensor_tensor(out=ss[:, 1, t:t + 1], in0=sq[:, t, 0:1], scalar=EPS, in1=sq[:, t, 1:2],
                                         op0=ALU.add, op1=ALU.add).then_inc(root_in, 1)
                inverse_root(ss[:, 2, t:t + 1], ss[:, 0, t:t + 1])
                dve.wait_ge(s_gain, 16 * (i + 1))
                for c in range(2):
                    half = slice(c * 512, (c + 1) * 512)
                    dve.scalar_tensor_tensor(out=xn[:, t, half], in0=x[:, t, half], scalar=ss[:, 0, t:t + 1],
                                             in1=(gain_exp if i == 3 else gain)[:, half], op0=ALU.mult,
                                             op1=ALU.mult).then_inc(normed, 1)

            def norm(i, following, banks1=None):
                norm_tile(i, 0)
                if i:
                    if i == 2:
                        dve.wait_ge(left_done, 1)
                    else:
                        dve.wait_ge(gran_done, following - 1)
                    add_half(banks1, 1, 0)
                    dve.wait_ge(gran_done, following)
                    add_half(banks1, 1, 1)
                norm_tile(i, 1)
                for t in range(NT):
                    if not i and t:
                        lo(0, following, KT_D * NARROW)
                    for a in range(2):
                        dve.wait_ge(hT_hi_done, 4 * i + 2 * t + a + 1)
                        dst = (slice(None), slice(4 * a, 4 * a + 4), slice(t * P, (t + 1) * P))
                        dve.tensor_tensor(hT[1][dst], A[2 * t + a][:, :].rearrange("p (k s) -> p k s", k=4),
                                          hT[0][dst].bitcast(f32), ALU.subtract).then_inc(hT_done, 1)
                if i < 3:
                    lo(0, following + 1)

            def rotate(i, chunk, t):
                src = pair(chunk)[t]
                v = src[:, :].rearrange("p (h u i) -> p h u i", h=HEADS, u=2)
                w1 = work[:, 1, :].rearrange("p (h u i) -> p h u i", h=HEADS, u=2)
                dve.tensor_tensor(work[:, 0, :].rearrange("p (a i) -> p a i", i=64),
                                  src[:, :].rearrange("p (a i) -> p a i", i=64),
                                  cos[:, t:t + 1, :].to_broadcast([P, 8, 64]), ALU.mult)
                for u in range(2):
                    ins = dve.tensor_tensor(w1[:, :, u, :], v[:, :, 1 - u, :],
                                            sin[:, t, u:u + 1, :].to_broadcast([P, HEADS, 64]), ALU.mult)
                if t == NT - 1:
                    link_read(ins)
                else:
                    link(ins)
                if i >= 2:
                    dve.wait_ge(rot_turned, 4 * layer_no[0] + i - 1)
                dve.tensor_tensor(rot[:, t, :], work[:, 0, :], work[:, 1, :], ALU.add).then_inc(rotated, 1)
                dve.wait_ge(rotated, 4 * layer_no[0] + i + 1)

            layer_no = [0]
            n_read = [0]

            def link_read(ins):
                n_read[0] += 1
                ins.then_inc(dve_read, 1)
                dve.wait_ge(dve_read, n_read[0])

            def head_stats(result, centred):
                for t in range(NT):
                    for h in range(HEADS):
                        ins = dve.bn_stats(stats[:, 4 * t + h, :], result(t, h))
                link(ins)
                for i in range(8):
                    ins = dve.bn_aggr(mv[:, i, :], stats[:, i, :])
                link(ins)
                roots[0] += 1
                if centred:
                    dve.tensor_scalar(rs[:, 0, :], mv[:, :, 1], EPS, None, ALU.add).then_inc(root_in, 1)
                else:
                    link(dve.tensor_tensor(rs[:, 2, :], mv[:, :, 0], mv[:, :, 0], ALU.mult))
                    dve.scalar_tensor_tensor(out=rs[:, 0, :], in0=mv[:, :, 1], scalar=EPS, in1=rs[:, 2, :],
                                             op0=ALU.add, op1=ALU.add).then_inc(root_in, 1)

            def turn_lo(n, bank, hi_part, dst):
                dve.wait_ge(oT_hi_done, n)
                dve.tensor_tensor(dst, bank[:, :].rearrange("p (h q) -> p h q", h=HEADS), hi_part.bitcast(f32),
                                  ALU.subtract).then_inc(oT_done, 1)

            def mixers(layer):
                g0 = LAYER_G0[layer]
                layer_no[0] = layer
                wo_banks = [[pair(22)[t], pair(23)[t]] for t in range(NT)]
                zf, ef = att[32:36, 0, 0:SEQ], att[32:36, 1, 0:SEQ]
                for s in range(MIX_G):
                    if 0 < s < MIX_G - 1:
                        dve.wait_ge(gran_done, g0 + s)
                    if s == 1:
                        dve.wait_ge(s_const, 48)
                        dve.tensor_scalar(zf, A[0][32:36, 0:SEQ], bf[32:36, layer:layer + 1], None,
                                          ALU.add).then_inc(fz_done, 1)
                    if s == 3:
                        dve.wait_ge(fln_done, layer + 1)
                        link(dve.scalar_tensor_tensor(out=ef, in0=zf, scalar=0.0, in1=ef, op0=ALU.min, op1=ALU.subtract))
                        cT = soft[32:36, 0, 0:SEQ]
                        link(dve.tensor_tensor_scan(cT, ones[32:36, 0:1].to_broadcast([HEADS, SEQ]), ef, 0.0,
                                                    ALU.mult, ALU.add))
                        dve.tensor_scalar(ncT[32:36, :], cT, -1.0, None, ALU.mult).then_inc(c_done, 1)
                    if 3 <= s < 7:
                        i = s - 3
                        dve.wait_ge(s_tables, 16)
                        rotate(i, i // 2, i % 2)
                    if s == 4:
                        dve.wait_ge(zln_done, layer + 1)
                        dve.scalar_tensor_tensor(out=o[:, 1, :], in0=A[1][:, :], scalar=0.0, in1=o[:, 0, :],
                                                 op0=ALU.min, op1=ALU.subtract).then_inc(loga_done, 1)
                    if s == 6:
                        dve.wait_ge(cum_done, layer + 1)
                        dve.tensor_scalar(bend[:, :], A[0][:, :].rearrange("p (b i) -> p b i", i=64)[:, :, 63],
                                          1.0 / GLA_TAU, None, ALU.mult).then_inc(bend_done, 1)
                        dve.tensor_copy(cq[:, :], A[1][:, 0:8]).then_inc(cq_done, 1)
                    if 9 <= s < 9 + HEADS:
                        h = s - 9
                        dve.wait_ge(ret_scores, HEADS * layer + h + 1)
                        if h >= 2:
                            dve.wait_ge(ret_out, HEADS * layer + h - 1)
                        src = A[2 + h % 2]
                        dve.tensor_tensor(att[:, h % 2, 0:SEQ], src[:, 0:SEQ], decay[:, h, :], ALU.mult)
                        dve.tensor_tensor(att[:, h % 2, SEQ:384], src[:, SEQ:384], decay[:, h, 0:P],
                                          ALU.mult).then_inc(ret_att, 1)
                    if s == 13:
                        dve.wait_ge(ret_out, HEADS * layer + HEADS)
                        head_stats(by_tile, True)
                    if s == 15:
                        dve.wait_ge(act_read, reads("act", layer, 3))
                        inverse_root(rs[:, 1, :], rs[:, 2, :])
                        for t in range(NT):
                            for h in range(HEADS):
                                i = 4 * t + h
                                ins = dve.tensor_scalar(o[:, t, h * HD:(h + 1) * HD], A[t][:, h * HD:(h + 1) * HD],
                                                        mv[:, i, 0:1], rs[:, 2, i:i + 1], ALU.subtract, ALU.mult)
                        link(ins)
                        for t in range(NT):
                            ins = dve.tensor_tensor(o[:, t, :], o[:, t, :], sgate[:, t, :], ALU.mult)
                        ins.then_inc(o_done, 1)
                    if s == 17:
                        dve.wait_ge(exp_done, layer + 1)
                        bq, bk = pair(7)
                        dve.scalar_tensor_tensor(out=q_dec, in0=bq[:, :].rearrange("p (f q) -> p f q", f=2),
                                                 scalar=float(GLA_DK) ** -0.5,
                                                 in1=work[:, 0, :].rearrange("p (f q) -> p f q", f=2),
                                                 op0=ALU.mult, op1=ALU.mult)
                        dve.tensor_tensor(k_inv, bk[:, :].rearrange("p (f q) -> p f q", f=2),
                                          work[:, 1, :].rearrange("p (f q) -> p f q", f=2), ALU.mult)
                        n_read[0] += 1
                        dve.tensor_tensor(k_end, bk[:, :].rearrange("p (f q) -> p f q", f=2),
                                          rot[:, 0, :].rearrange("p (f q) -> p f q", f=2), ALU.mult).then_inc(dve_read, 1)
                        for t in range(NT):
                            turn_lo(6 * layer + t + 1, A[2 + t], aT[0][:, 0:4, t * P:(t + 1) * P],
                                    aT[1][:, 0:4, t * P:(t + 1) * P])
                        dve.wait_ge(dve_read, n_read[0])
                        dve.tensor_copy(flagf[:, 0:1], bend[:, 0:1]).then_inc(gla_ops, 1)
                    if 18 <= s < 18 + HEADS:
                        h = s - 18
                        dve.wait_ge(fox_scores, HEADS * layer + h + 1)
                        if h >= 2:
                            dve.wait_ge(fox_turned, HEADS * layer + h - 1)
                        row = soft[:, h % 2, :]
                        dve.scalar_tensor_tensor(out=row[:, 0:P], in0=A[2][:, 0:P], scalar=cq[:, h:h + 1], in1=causal,
                                                 op0=ALU.add, op1=ALU.add)
                        dve.tensor_scalar(row[:, P:2 * P], A[2][:, P:2 * P], cq[:, 4 + h:5 + h], None, ALU.add)
                        link(dve.scalar_tensor_tensor(out=row[:, 2 * P:384], in0=A[2][:, 2 * P:384],
                                                      scalar=cq[:, 4 + h:5 + h], in1=causal, op0=ALU.add, op1=ALU.add))
                        dve.tensor_reduce(nmax[:, 0, h:h + 1], row[:, 0:P], AX.X, ALU.max, negate=True)
                        dve.tensor_reduce(nmax[:, 1, h:h + 1], row[:, P:384], AX.X, ALU.max,
                                          negate=True).then_inc(fox_rows, 1)
                    if s == 20:
                        dve.wait_ge(kv_done, 2 * layer + 1)
                        for c in range(2):
                            for f in range(2):
                                for half in range(2):
                                    p0 = 64 * half
                                    kv = A[c][p0:p0 + 64, f * SEQ + half * P:f * SEQ + (half + 1) * P]
                                    if c == 0:
                                        ins = dve.tensor_copy(states[p0:p0 + 64, f, 0, :], kv)
                                    else:
                                        ins = dve.scalar_tensor_tensor(
                                            out=states[p0:p0 + 64, f, 1, :], in0=states[p0:p0 + 64, f, 0, :],
                                            scalar=aend[p0:p0 + 64, 4 * f + 1:4 * f + 2], in1=kv,
                                            op0=ALU.mult, op1=ALU.add)
                            if c == 0:
                                link(ins)
                        ins.then_inc(state_done, 1)
                    if s == 24:
                        dve.wait_ge(fox_out, HEADS * layer + HEADS)
                        dve.wait_ge(fox_exp, HEADS * layer + HEADS)
                        link(dve.reciprocal(rs[:, 3, :], rsum[:, :, :].rearrange("p t h -> p (t h)")))
                        for t in range(NT):
                            for h in range(HEADS):
                                ins = dve.tensor_scalar(o[:, t, h * HD:(h + 1) * HD], A[t][:, h * HD:(h + 1) * HD],
                                                        rs[:, 3, 4 * t + h:4 * t + h + 1], None, ALU.mult)
                        ins.then_inc(o_done, 1)
                    if s == 25:
                        for t in range(NT):
                            turn_lo(6 * layer + 2 + t + 1, A[2 + t], aT[0][:, 4:8, t * P:(t + 1) * P],
                                    aT[1][:, 4:8, t * P:(t + 1) * P])
                        dve.memset(gsc, 0.0).then_inc(ready0, 1)
                    if s == 26:
                        dve.wait_ge(kv_done, 2 * layer + 2)
                        for f in range(2):
                            for half in range(2):
                                p0 = 64 * half
                                ins = dve.scalar_tensor_tensor(
                                    out=states[p0:p0 + 64, f, 2, :], in0=states[p0:p0 + 64, f, 1, :],
                                    scalar=aend[p0:p0 + 64, 4 * f + 2:4 * f + 3],
                                    in1=A[0][p0:p0 + 64, f * SEQ + half * P:f * SEQ + (half + 1) * P],
                                    op0=ALU.mult, op1=ALU.add)
                        ins.then_inc(state_done, 1)
                    if s in (27, 28):
                        t = s - 27
                        dve.wait_ge(gla_scores, 2 * layer + 2)
                        dve.wait_ge(ready0, layer + 1)
                        if t:
                            dve.wait_ge(gla_out, 2 * layer + 1)
                        for h in range(HEADS):
                            ins = dve.copy_predicated(gsc[:, h * P:(h + 1) * P], chunk_tri.bitcast(i32),
                                                      A[1 - h % 2][:, (h // 2 * 2 + t) * P:(h // 2 * 2 + t + 1) * P])
                        ins.then_inc(gla_att, 1)
                    if s == 29:
                        dve.wait_ge(gla_out, 2 * layer + 2)
                        head_stats(gla_result, False)
                    if s == 31:
                        dve.wait_ge(act_read, reads("act", layer, 9))
                        inverse_root(rs[:, 1, :], rs[:, 2, :])
                        for t in range(NT):
                            for h in range(HEADS):
                                ins = dve.scalar_tensor_tensor(
                                    out=o[:, t, h * HD:(h + 1) * HD], in0=gla_result(t, h),
                                    scalar=rs[:, 2, 4 * t + h:4 * t + h + 1], in1=sgate[:, t, h * HD:(h + 1) * HD],
                                    op0=ALU.mult, op1=ALU.mult)
                        ins.then_inc(o_done, 1)
                    if s == 32:
                        for t in range(NT):
                            turn_lo(6 * layer + 4 + t + 1, A[t], aT[0][:, 0:4, t * P:(t + 1) * P],
                                    aT[1][:, 0:4, t * P:(t + 1) * P])
                    if s >= GATE_S0 + 3 and s <= WO_S0 and (s - GATE_S0) % 3 == 0:
                        j = (s - GATE_S0 - 3) // 3
                        c = (j % 2) * 512
                        dve.wait_ge(act_read, reads("act", layer, 10 + 2 * j))
                        dst = [xn[:, t, c:c + 512] if j < 2 else work[:, t, :] for t in range(NT)]
                        for t in range(NT):
                            ins = dve.tensor_tensor(dst[t], pair(11 + 2 * j)[t][:, :], work[:, t, :], ALU.mult)
                        link_read(ins)
                        if j < 2:
                            dve.tensor_copy(flagf[:, 0:1], bend[:, 0:1]).then_inc(merged, 1)
                        else:
                            for t in range(NT):
                                ins = dve.tensor_tensor(xn[:, t, c:c + 512], xn[:, t, c:c + 512], work[:, t, :], ALU.add)
                            ins.then_inc(merged, 1)
                            dve.wait_ge(merged, N_GB * layer + j + 1)
                    if s in (37, 40):
                        h = int(s == 40)
                        for a in range(2):
                            tile = (4, 0)[h] + 2 * a
                            dve.wait_ge(mT_hi_done, 4 * layer + 2 * h + a + 1)
                            dve.tensor_tensor(aT[1][:, tile:tile + 2, :],
                                              A[2 * h + a][:, :].rearrange("p (k q) -> p k q", k=2),
                                              aT[0][:, tile:tile + 2, :].bitcast(f32), ALU.subtract).then_inc(mT_done, 1)
                    if s == MIX_G - 1:
                        dve.wait_ge(tile0_done, 2 * layer + 1)
                        add_tile(wo_banks[0], 0)
                    else:
                        lo(0, g0 + s + 2)
                return wo_banks[1]

            def dense():
                g0 = FFN_G0

                def product(f1, pair_no):
                    dve.wait_ge(f_silu, f1)
                    dve.tensor_tensor(work[:, 1, :], M[2 * pair_no + 1][:, :], work[:, 0, :], ALU.mult).then_inc(f_prod, 1)

                def product_lo(f1, dst=gT):
                    dve.wait_ge(f_hi, f1)
                    dve.tensor_tensor(dst[1], work[:, 1, :].rearrange("p (k s) -> p k s", k=4), dst[0].bitcast(f32),
                                      ALU.subtract).then_inc(f_lo, 1)

                lo(0, g0 + 2)
                lo(0, g0 + 3)
                dve.wait_ge(gran_done, g0 + 2)
                product(1, 0)
                with dve.Fori(0, (N_FF - 1) // 2) as j:
                    for u in range(2):
                        f = 1 + 2 * j + u
                        product_lo(f)
                        lo(j, g0 + 4 + 3 * u)
                        lo(j, g0 + 5 + 3 * u)
                        dve.wait_ge(gran_done, 6 * j + g0 + 4 + 3 * u)
                        dve.wait_ge(f_lo, f)
                        product(f + 1, (1 + u) % 2)
                        lo(j, g0 + 6 + 3 * u)
                product_lo(N_FF, gT_end)
                dve.wait_ge(tile0_done, 2)
                add_tile(A[0:2], 0)
                return A[2:4]

            def router():
                lo(0, MOE_G0)
                lo(0, MOE_G0 + 1)
                dve.wait_ge(rt_turned, 1)
                link(dve.tensor_copy(lg[:, :, :], A[1][:, 0:16].rearrange("p (t e) -> p t e", t=NT)))
                for t in range(NT):
                    ins = dve.max(top[:, t, :], lg[:, t, :])
                link(ins)
                for t in range(NT):
                    ins = dve.max_index(topi[:, t, :], top[:, t, :], lg[:, t, :])
                link(ins)
                dve.tensor_tensor(tw[:, 0, :], top[:, :, 1], top[:, :, 0], ALU.subtract).then_inc(rt_top, 1)
                link(dve.tensor_copy(topf[:, :, :], topi[:, :, :]))
                e8 = iota[:, 0:N_EXP]
                for t in range(NT):
                    ins = dve.tensor_scalar(picked[:, t, 0:N_EXP], e8, topf[:, t, 0:1], None, ALU.is_equal)
                link(ins)
                for t in range(NT):
                    ins = dve.scalar_tensor_tensor(out=picked[:, t, 0:N_EXP], in0=e8, scalar=topf[:, t, 1:2],
                                                   in1=picked[:, t, 0:N_EXP], op0=ALU.is_equal, op1=ALU.add)
                ins.then_inc(rt_picked, 1)
                dve.wait_ge(rt_ranked, 1)
                link(dve.tensor_copy(rank[:, :, 0:N_EXP], A[2][:, 0:16].rearrange("p (t e) -> p t e", t=NT)))

            def token_weights():
                e8 = iota[:, 0:N_EXP]
                dve.wait_ge(rt_exp, 1)
                link(dve.tensor_scalar(tw[:, 0, :], tw[:, 1, :], 1.0, None, ALU.add))
                link(dve.reciprocal(tw[:, 2, :], tw[:, 0, :]))
                link(dve.tensor_tensor(tw[:, 1, :], tw[:, 1, :], tw[:, 2, :], ALU.mult))
                for t in range(NT):
                    dve.tensor_scalar(comb[:, t, 0:N_EXP], e8, topf[:, t, 0:1], tw[:, 2, t:t + 1], ALU.is_equal, ALU.mult)
                    ins = dve.tensor_scalar(lg[:, t, :], e8, topf[:, t, 1:2], tw[:, 1, t:t + 1], ALU.is_equal, ALU.mult)
                link(ins)
                link(dve.tensor_tensor(comb[:, :, 0:N_EXP], comb[:, :, 0:N_EXP], lg[:, :, :], ALU.add))

            def overflow():
                dve.wait_ge(rt_counted, 1)
                link(dve.tensor_reduce(flagf[:, :], A[2][:, 16:24], AX.X, ALU.max))
                link(dve.tensor_scalar(flagf[:, :], flagf[:, :], -float(P), 0.0, ALU.add, ALU.max))
                dve.tensor_copy(flag[:, :], flagf[:, :]).then_inc(rt_flag, 1)

            def experts(block):
                e0, six0 = N_EXP * block, MOE_G0 // 6 + block * N_EXP * N_EF

                def pick_matrix(dst, weight, e):
                    for t in range(NT):
                        ins = dve.tensor_scalar(dst[:, t, :], iota, rank[:, t, bass.ds(e, 1)],
                                                weight[:, t, bass.ds(e, 1)], ALU.is_equal, ALU.mult)
                    return ins

                def gathered(n):
                    for a in range(2):
                        dve.wait_ge(e_xhi, 2 * n - 1 + a)
                        dve.tensor_tensor(xgT[1][:, 4 * a:4 * a + 4, :],
                                          M[2 + a][:, :].rearrange("p (k s) -> p k s", k=4),
                                          xgT[0][:, 4 * a:4 * a + 4, :].bitcast(f32), ALU.subtract).then_inc(e_xlo, 1)

                def product_lo(n, dst=gT):
                    dve.wait_ge(e_hi, n)
                    dve.tensor_tensor(dst[1], A[2][:, :].rearrange("p (k s) -> p k s", k=4), dst[0].bitcast(f32),
                                      ALU.subtract).then_inc(e_lo, 1)

                def product(n, done):
                    dve.wait_ge(gran_done, done)
                    dve.wait_ge(e_silu, n)
                    dve.tensor_tensor(work[:, 1, :], M[1][:, :], work[:, 0, :], ALU.mult).then_inc(e_prod, 1)

                def round_rest(six_f, n, first, last=False):
                    for u in range(first, 6):
                        if u == 4:
                            product(n, 6 * six_f + 8)
                        if u == 5 and last:
                            product_lo(n, gT_last)
                        lo(six_f, 6 + u)

                def rounds(six, e):
                    n = N_EF * e + N_EF * e0
                    round_rest(six, n + 2, 3)
                    with dve.Fori(2, N_EF - 1) as f:
                        lo(six + f - 1, 6)
                        product_lo(n + f)
                        round_rest(six + f - 1, n + f + 1, 1)
                    lo(six + N_EF - 2, 6)
                    product_lo(n + N_EF - 1)
                    round_rest(six + N_EF - 2, n + N_EF, 1, last=True)

                def places(e):
                    dve.wait_ge(e_putw, e + 1 + e0)
                    dve.tensor_reduce(w_place[:, :], A[3][:, 0:SEQ], AX.X, ALU.add)
                    dve.tensor_scalar(put, A[3][:, 0:SEQ], 0.0, None, ALU.is_gt).then_inc(e_put, 1)

                def outputs(e):
                    for c in range(2):
                        half = slice(c * 512, (c + 1) * 512)
                        dve.wait_ge(e_yhi, 2 * e + c + 1 + 2 * e0)
                        dve.scalar_tensor_tensor(out=y_part[1][:, half], in0=A[c][:, :], scalar=w_place[:, 0:1],
                                                 in1=y_part[0][:, half].bitcast(f32), op0=ALU.mult,
                                                 op1=ALU.subtract).then_inc(e_ylo, 1)

                def add_outputs(e, c):
                    dve.wait_ge(e_added[c], e + 1 + e0)
                    half = slice(c * 512, (c + 1) * 512)
                    for t, bank in enumerate((A if c else M[2:])[0:2]):
                        dve.wait_ge(e_scatter, 4 * e + 2 * c + t + 1 + 4 * e0)
                        ins = dve.tensor_tensor(x[:, t, half], bank[:, :], x[:, t, half], ALU.add)
                    ins.then_inc(e_added[c], 1)

                if block:
                    dve.tensor_scalar(rank[:, :, :], rank[:, :, :], -float(P), None, ALU.add).then_inc(e_moved, 1)
                    dve.wait_ge(e_moved, 1)
                else:
                    for c in range(2):
                        dve.memset(spare[:, 1 + c:2 + c], 0.0).then_inc(e_added[c], 1)
                pick_matrix(pick, picked, 0).then_inc(e_pick, 1)
                for L in range(2 if not block else 0, 3):
                    lo(six0, L)
                gathered(e0 + 1)
                if not block:
                    token_weights()
                    overflow()
                for L in range(3, 6):
                    lo(six0, L)
                product(1 + N_EF * e0, 6 * six0 + 4)
                pick_matrix(pick, picked, 1).then_inc(e_pick, 1)
                pick_matrix(pick_w, comb, 0).then_inc(e_pickw, 1)
                lo(six0, 6)
                lo(six0, 7)
                product_lo(1 + N_EF * e0)
                lo(six0, 8)
                def expert(e, early):
                    six = N_EF * e + six0
                    rounds(six, e)
                    lo(six, 42)
                    gathered(e + 2 + e0)
                    places(e)
                    if early:
                        lo_early(six, e)
                    else:
                        lo(six, 43)
                    lo(six, 44)
                    outputs(e)
                    lo(six, 45)
                    pick_matrix(pick, picked, e + 2).then_inc(e_pick, 1)
                    pick_matrix(pick_w, comb, e + 1).then_inc(e_pickw, 1)
                    lo(six, 46)
                    product(N_EF * e + N_EF + 1 + N_EF * e0, 6 * six + 46)
                    lo(six, 47)
                    lo(six, 48)
                    lo(six, 49)
                    product_lo(N_EF * e + N_EF + 1 + N_EF * e0)
                    add_outputs(e, 1)
                    lo(six, 50)
                    add_outputs(e, 0)

                with dve.Fori(0, N_EARLY) as e:
                    expert(e, True)
                for e in range(N_EARLY, N_EXP - 1):
                    expert(e, False)
                over = None if block else dve.value_load(flag[0:1, 0:1], min_val=0, max_val=P)
                rounds(six0 + 7 * (N_EXP - 1), N_EXP - 1)
                places(N_EXP - 1)
                outputs(N_EXP - 1)
                add_outputs(N_EXP - 1, 0)
                add_outputs(N_EXP - 1, 1)
                for added in e_added:
                    dve.wait_ge(added, N_EXP + 1 + e0)
                return over

            dve.memset(zeros[:, :], 0.0).then_inc(zeros_set, 1)
            dve.memset(one[:, :], 1.0).then_inc(one_set, 1)
            for a in (comb, rank, picked):
                dve.memset(a[:, :, :], 0.0)
            link(dve.memset(gaT[:, :], 1.0))
            norm(0, 0)
            norm(1, FFN_G0, mixers(0))
            norm(2, LAYER_G0[1], dense())
            norm(3, ROUTER_G, mixers(1))
            router()
            over = experts(0)
            with dve.If(over > 0):
                experts(1)
            with dve.Else():
                dve.wait_ge(rt_flag, 1)
            dve.memset(spare[:, :], 0.0).then_inc(fin_x, 1)
            link(dve.tensor_tensor_reduce(xn[:, 0, :], x[:, 0, :], x[:, 0, :], 1.0, 0.0, ALU.mult, ALU.add,
                                          ss[:, 0, 0:1]))
            dve.tensor_scalar(ss[:, 1, 0:1], ss[:, 0, 0:1], 1.0 / D, EPS, ALU.mult, ALU.add).then_inc(fin_var, 1)
            dve.wait_ge(fin_sq, 1)
            dve.tensor_scalar(ss[:, 1, 1:2], sq[:, 1, 0:1], EPS, None, ALU.add).then_inc(fin_var, 1)
            dve.wait_ge(s_gain_fin, 16)
            for t in range(NT):
                dve.wait_ge(fin_root, t + 1)
                link(dve.reciprocal(ss[:, 0, t:t + 1], ss[:, 2, t:t + 1]))
                for c in range(2):
                    half = slice(c * 512, (c + 1) * 512)
                    dve.scalar_tensor_tensor(out=xn[:, t, half], in0=x[:, t, half], scalar=ss[:, 0, t:t + 1],
                                             in1=gain_fin[:, half], op0=ALU.mult, op1=ALU.mult).then_inc(fin_done, 1)

        @block.tensor
        def _(pe):
            def mm3(dst, stat, mov, start, stop):
                pe.matmul(dst, stat[0], mov[0], start=start, stop=False, skip_group_check=True)
                pe.matmul(dst, stat[0], mov[1], start=False, stop=False, skip_group_check=True)
                return pe.matmul(dst, stat[1], mov[0], start=False, stop=stop, skip_group_check=True)

            def weights(local, a, b):
                return w_hi[:, local % RING, a:b], w_lo[:, local % RING, a:b]

            def both(tile, k, a, b):
                return tile[0][:, k, a:b], tile[1][:, k, a:b]

            def arrived(six, local):
                pe.wait_ge(lo_done, 6 * six + local + 1)

            def rows_product(local, banks, source, k0, first, last):
                for t, bank in enumerate(banks):
                    ins = tile_product(local, bank, source, k0, t, first, last)
                ins.then_inc(gran_done, 1)

            def tile_product(local, bank, source, k0, t, first, last):
                for k in range(4):
                    ins = mm3(bank[:, :], both(source, k0 + k, t * P, (t + 1) * P),
                              weights(local, k * 512, (k + 1) * 512), first and k == 0, last and k == 3)
                return ins

            def feature_product(local, banks, half):
                for ft in range(4):
                    for k in range(4):
                        a = k * 512 + ft * P
                        ins = mm3(banks[ft // 2][:, (ft % 2) * SEQ:(ft % 2 + 1) * SEQ], weights(local, a, a + P),
                                  both(hT, 4 * half + k, 0, SEQ), half == 0 and k == 0 and ft % 2 == 0,
                                  half == 1 and k == 3)
                ins.then_inc(gran_done, 1)

            def narrow_product(local):
                for k in range(KT_D):
                    ins = mm3(A[0][0:NARROW, 0:SEQ], weights(local, k * NARROW, (k + 1) * NARROW), both(hT, k, 0, SEQ),
                              k == 0, k == KT_D - 1)
                ins.then_inc(gran_done, 1)

            def keep_clock(n):
                for _ in range(n):
                    pe.matmul(M[0][:, 0:P], zeros[:, :], zeros[:, :], start=True, stop=True)

            def norm(i):
                for t in range(NT):
                    if i and t:
                        keep_clock(IDLE_TILE)
                    for a in range(2):
                        pe.wait_ge(normed, 4 * i + 2 * t + a + 1)
                        turn_tokens(xn[:, t, a * 512:(a + 1) * 512], A[2 * t + a]).then_inc(x_turned, 1)
                keep_clock(IDLE_NORM)

            def turn_tokens(src, bank):
                for h in range(HEADS):
                    ins = pe.transpose(bank[:, h * P:(h + 1) * P], src[:, h * P:(h + 1) * P], ident)
                return ins

            def head_out(h, b, att_h):
                v = val[b][:, :, h * HD:(h + 1) * HD]
                dst = slice(h * HD, (h + 1) * HD)
                pe.matmul(A[0][:, dst], att_h[:, 0:P], v[:, 0, :], start=True, stop=True)
                pe.matmul(A[1][:, dst], att_h[:, P:2 * P], v[:, 0, :], start=True, stop=False)
                return pe.matmul(A[1][:, dst], att_h[:, 2 * P:384], v[:, 1, :], start=False, stop=True)

            def mixers(layer):
                g0 = LAYER_G0[layer]
                for s in range(MIX_G):
                    arrived(0, g0 + s)
                    if s == 0:
                        pe.wait_ge(hT_done, 4 * (2 * layer + 1))
                        narrow_product(g0)
                    elif s < GATE_S0:
                        chunk, half = (s - 1) // 2, (s - 1) % 2
                        if half == 0 and chunk >= 2:
                            wait_read(pe, layer, chunk - 2)
                        if CHUNKS[chunk][0] in BY_FEATURE:
                            feature_product(g0 + s, pair(chunk), half)
                        else:
                            rows_product(g0 + s, pair(chunk), hT, 4 * half, half == 0, half == 1)
                    elif s < WO_S0:
                        j, part = (s - GATE_S0) // 3, (s - GATE_S0) % 3
                        chunk = 10 + 2 * j + (part == 2)
                        if part != 1:
                            wait_read(pe, layer, chunk - 2)
                        if part < 2:
                            rows_product(g0 + s, pair(chunk), hT, 4 * part, part == 0, part == 1)
                        else:
                            b = j // 2
                            pe.wait_ge(oT_done, 6 * layer + 2 * b + 2)
                            rows_product(g0 + s, pair(chunk), aT, AT_TILE[BRANCH_ORDER[b]], True, True)
                    else:
                        half, n = (s - WO_S0) // 2, (s - WO_S0) % 2
                        if half == 0:
                            wait_read(pe, layer, 20 + n)
                        pe.wait_ge(mT_done, 4 * layer + 2 * half + 2)
                        if half == 0:
                            rows_product(g0 + s, pair(22 + n), aT, 4, True, False)
                        elif n == 1:
                            for t in range(NT):
                                for m in range(2):
                                    ins = tile_product(g0 + s - 1 + m, pair(22 + m)[t], aT, 0, t, False, True)
                                    if t:
                                        ins.then_inc(gran_done, 1)
                                if t == 0:
                                    ins.then_inc(tile0_done, 1)

                    if s == 1:
                        pe.wait_ge(s_const, 48)
                        pe.wait_ge(ga_done, layer + 1)
                        for t in range(NT):
                            ins = pe.matmul(A[1][:, t * 256:(t + 1) * 256], gaT[0:GLA_RANK + 1, t * P:(t + 1) * P],
                                            a2[:, layer, :], start=True, stop=True)
                        ins.then_inc(z_done, 1)
                    if 3 <= s < 7:
                        i = s - 3
                        pe.wait_ge(rotated, 4 * layer + i + 1)
                        if i >= 2:
                            pe.wait_ge(rot_read, 4 * layer + i - 1)
                        turn_tokens(rot[:, i % 2, :], A[2 + i % 2]).then_inc(rot_turned, 1)
                    if s == 5:
                        pe.wait_ge(s_tables, 16)
                        pe.wait_ge(loga_done, layer + 1)
                        pe.wait_ge(fz_done, layer + 1)
                        for f in range(2):
                            for t in range(NT):
                                ins = pe.matmul(A[0][:, (2 * f + t) * P:(2 * f + t + 1) * P],
                                                o[:, 1, t * 256 + f * P:t * 256 + (f + 1) * P], chunk_tri,
                                                start=True, stop=True)
                        pe.wait_ge(c_done, layer + 1)
                        for t in range(NT):
                            ins = pe.transpose(A[1][:, 4 * t:4 * t + 4], soft[32:36, 0, t * P:(t + 1) * P],
                                               ident[32:36, 32:36])
                        ins.then_inc(cum_done, 1)
                    if 8 <= s < 8 + HEADS:
                        h = s - 8
                        if h == 0:
                            pe.wait_ge(rot_read, 4 * layer + 4)
                        if h >= 2:
                            pe.wait_ge(ret_att, HEADS * layer + h - 1)
                        bank = A[2 + h % 2]
                        pe.matmul(bank[:, 0:SEQ], kT[0][:, h, 0:P], qT[0][:, h, :], start=True, stop=True)
                        pe.matmul(bank[:, SEQ:384], kT[0][:, h, P:SEQ], qT[0][:, h, P:SEQ], start=True,
                                  stop=True).then_inc(ret_scores, 1)
                    if 9 <= s < 9 + HEADS:
                        h = s - 9
                        if h == 0:
                            pe.wait_ge(exp_done, layer + 1)
                            pe.wait_ge(cq_done, layer + 1)
                            pe.wait_ge(act_read, reads("act", layer, 2))
                        pe.wait_ge(ret_att, HEADS * layer + h + 1)
                        head_out(h, 0, att[:, h % 2, :]).then_inc(ret_out, 1)
                    if s == 16:
                        pe.wait_ge(o_done, 3 * layer + 1)
                        for t in range(NT):
                            turn_tokens(o[:, t, :], A[2 + t]).then_inc(o_turned, 1)
                    if 17 <= s < 17 + HEADS:
                        h = s - 17
                        if h == 0:
                            pe.wait_ge(oT_done, 6 * layer + 2)
                            pe.wait_ge(act_read, reads("act", layer, 5))
                        else:
                            pe.wait_ge(fox_rows, HEADS * layer + h)
                        for t in range(NT):
                            dst = A[2][:, t * P:t * P + (t + 1) * P]
                            pe.matmul(dst, qT[1][:, h, t * P:(t + 1) * P], kT[1][:, h, 0:(t + 1) * P],
                                      start=True, stop=False)
                            ins = pe.matmul(dst, ident[32:36, 32 + h:33 + h].to_broadcast([HEADS, P]),
                                            ncT[32:36, 0:(t + 1) * P], start=False, stop=True)
                        ins.then_inc(fox_scores, 1)
                    if s == 18:
                        pe.wait_ge(gla_ops, layer + 1)
                        for t in range(NT):
                            for f in range(2):
                                ins = pe.transpose(A[0][:, (2 * t + f) * P:(2 * t + f + 1) * P],
                                                   k_end[:, f, t * P:(t + 1) * P], ident)
                        ins.then_inc(kend_turned, 1)
                    if s == 19:
                        pe.wait_ge(kend_done, layer + 1)
                        pe.wait_ge(act_read, reads("act", layer, 8))
                        for f in range(2):
                            for c in range(2):
                                p0 = 64 * c
                                ins = pe.matmul(A[c][:, f * SEQ:(f + 1) * SEQ], k_tok[p0:p0 + 64, 0, f * P:(f + 1) * P],
                                                val[0][p0:p0 + 64, 0, f * SEQ:(f + 1) * SEQ], start=True, stop=True)
                        ins.then_inc(kv_done, 1)
                    if 19 <= s < 19 + HEADS:
                        h = s - 19
                        pe.wait_ge(fox_exp, HEADS * layer + h + 1)
                        if h >= 1:
                            pe.wait_ge(fox_att, HEADS * layer + h)
                        for i in range(3):
                            ins = pe.transpose(A[3][:, i * P:(i + 1) * P], soft[:, h % 2, i * P:(i + 1) * P], ident)
                        ins.then_inc(fox_turned, 1)
                    if 20 <= s < 20 + HEADS:
                        h = s - 20
                        if h == 0:
                            pe.wait_ge(state_done, 2 * layer + 1)
                        pe.wait_ge(fox_att, HEADS * layer + h + 1)
                        head_out(h, 1, att[:, h % 2, :]).then_inc(fox_out, 1)
                    if s == 24:
                        pe.wait_ge(o_done, 3 * layer + 2)
                        for t in range(NT):
                            turn_tokens(o[:, t, :], A[2 + t]).then_inc(o_turned, 1)
                    if s == 25:
                        p0 = 0
                        for f in range(2):
                            ins = pe.matmul(A[0][:, f * SEQ:(f + 1) * SEQ], k_tok[p0:p0 + 64, 1, f * P:(f + 1) * P],
                                            val[0][p0:p0 + 64, 1, f * SEQ:(f + 1) * SEQ], start=True, stop=True)
                        ins.then_inc(kv_done, 1)
                    if s in (27, 28):
                        t = s - 27
                        if t == 0:
                            pe.wait_ge(oT_done, 6 * layer + 4)
                        pe.wait_ge(state_done, 2 * layer + 1 + t)
                        pe.wait_ge(gla_att, 2 * layer + t + 1)
                        for h in range(HEADS):
                            f, p0 = h // 2, 64 * (h % 2)
                            out_h = gla_result(t, h)
                            pe.matmul(out_h, gsc[:, h * P:(h + 1) * P],
                                      val[0][:, t, h * HD:(h + 1) * HD], start=True, stop=False, skip_group_check=True)
                            for c in range(2):
                                if 2 * t + c:
                                    ins = pe.matmul(out_h[64 * c:64 * c + 64, :],
                                                    q_dec[p0:p0 + 64, f, t * P + 64 * c:t * P + 64 * c + 64],
                                                    states[p0:p0 + 64, f, 2 * t + c - 1, :], start=False, stop=c == 1,
                                                    skip_group_check=True)
                        ins.then_inc(gla_out, 1)
                    if s in (25, 26):
                        odd = s - 25
                        if odd:
                            pe.wait_ge(state_done, 2 * layer + 2)
                        for f in range(2):
                            for t in range(NT):
                                p0 = 64 * odd
                                ins = pe.matmul(A[1 - odd][:, (2 * f + t) * P:(2 * f + t + 1) * P],
                                                k_inv[p0:p0 + 64, f, t * P:(t + 1) * P],
                                                q_dec[p0:p0 + 64, f, t * P:(t + 1) * P], start=True, stop=True)
                        ins.then_inc(gla_scores, 1)
                    if s == 31:
                        pe.wait_ge(o_done, 3 * layer + 3)
                        for t in range(NT):
                            turn_tokens(o[:, t, :], A[t]).then_inc(o_turned, 1)
                    if s in (36, 39):
                        h = int(s == 39)
                        pe.wait_ge(merged, N_GB * layer + 5 + h)
                        for a in range(2):
                            for k in range(2):
                                for t in range(NT):
                                    at = (4 * h + 2 * a + k) * P
                                    ins = pe.transpose(A[2 * h + a][:, k * SEQ + t * P:k * SEQ + (t + 1) * P],
                                                       xn[:, t, at:at + P], ident)
                        ins.then_inc(m_turned, 1)

            def dense():
                g0 = FFN_G0

                def hidden(six, local, bank):
                    arrived(six, local)
                    for ft in range(2):
                        for k in range(KT_D):
                            a = k * FF + ft * P
                            ins = mm3(bank[:, ft * SEQ:(ft + 1) * SEQ], weights(local, a, a + P), both(hT, k, 0, SEQ),
                                      k == 0 and ft == 0, k == KT_D - 1)
                    ins.then_inc(gran_done, 1)

                def back(six, local, n, first, last):
                    arrived(six, local)
                    pe.wait_ge(f_lo, n)
                    for t in range(NT):
                        for c in range(2):
                            for k in range(2):
                                g = gT_end if last else gT
                                stat = (g[0][:, 2 * k + t, :], g[1][:, 2 * k + t, :])
                                ins = mm3(A[2 * t + c][:, :], stat, weights(local, k * D + c * 512, k * D + (c + 1) * 512),
                                          first and k == 0, last and k == 1)
                            if last and t == 1 and c == 0:
                                ins.then_inc(left_done, 1)
                        if last and t == 0:
                            ins.then_inc(tile0_done, 1)
                    ins.then_inc(gran_done, 1)

                pe.wait_ge(hT_done, 4 * 2)
                hidden(0, g0, M[0])
                hidden(0, g0 + 1, M[1])
                hidden(0, g0 + 2, M[2])
                hidden(0, g0 + 3, M[3])
                back(0, g0 + 4, 1, True, False)
                pe.wait_ge(f_prod, 1)
                hidden(0, g0 + 5, M[0])
                hidden(0, g0 + 6, M[1])
                back(0, g0 + 7, 2, False, False)
                with pe.Fori(1, (N_FF - 1) // 2) as j:
                    for u in range(2):
                        f = 1 + 2 * j + u
                        m = 2 * ((1 + u) % 2)
                        pe.wait_ge(f_prod, f)
                        hidden(j, g0 + 2 + 3 * u, M[m])
                        hidden(j, g0 + 3 + 3 * u, M[m + 1])
                        back(j, g0 + 4 + 3 * u, f, False, False)
                back(0, g0 + FFN_G - 1, N_FF, False, True)

            def router():
                arrived(0, ROUTER_G)
                pe.wait_ge(hT_done, 4 * 4)
                narrow_product(ROUTER_G)
                pe.wait_ge(rt_copied, 1)
                for t in range(NT):
                    ins = pe.transpose(A[1][:, 8 * t:8 * t + 8], lgT[:, t * P:(t + 1) * P], ident[0:8, 0:8])
                ins.then_inc(rt_turned, 1)
                keep_clock(IDLE_PLACES)
                pe.wait_ge(rt_picked, 1)
                pe.matmul(A[2][:, 0:8], strict, picked[:, 0, 0:N_EXP], start=True, stop=True)
                pe.matmul(A[2][:, 8:16], ones, picked[:, 0, 0:N_EXP], start=True, stop=False)
                pe.matmul(A[2][:, 8:16], strict, picked[:, 1, 0:N_EXP], start=False, stop=True).then_inc(rt_ranked, 1)
                keep_clock(IDLE_GATHER)

            def counts():
                pe.matmul(A[2][:, 16:24], ones, picked[:, 0, 0:N_EXP], start=True, stop=False)
                pe.matmul(A[2][:, 16:24], ones, picked[:, 1, 0:N_EXP], start=False, stop=True).then_inc(rt_counted, 1)

            def experts(block):
                e0, six0 = N_EXP * block, MOE_G0 // 6 + block * N_EXP * N_EF

                def gather(n):
                    pe.wait_ge(e_pick, n + block)
                    for k in range(KT_D):
                        for t in range(NT):
                            ins = pe.matmul(M[2 + k // 4][:, (k % 4) * P:(k % 4 + 1) * P], xn[:, t, k * P:(k + 1) * P],
                                            pick[:, t, :], start=t == 0, stop=t == NT - 1)
                        if k % 4 == 3:
                            ins.then_inc(e_gather, 1)

                def hidden(six, local, bank, half):
                    arrived(six, local)
                    rows_product(local, [bank], xgT, 4 * half, half == 0, half == 1)

                def turn_product(n):
                    pe.wait_ge(e_prod, n)
                    turn_tokens(work[:, 1, :], A[2]).then_inc(e_turned, 1)

                def back(six, local, part, first, last, g=gT):
                    arrived(six, local)
                    for c in range(2):
                        for k in range(2):
                            stat = (g[0][:, 2 * part + k, :], g[1][:, 2 * part + k, :])
                            ins = mm3(A[c][:, :], stat, weights(local, k * D + c * 512, k * D + (c + 1) * 512),
                                      first and k == 0, last and k == 1)
                        if last and c == 0:
                            ins.then_inc(e_left, 1)
                    ins.then_inc(gran_done, 1)

                def round0(six, local, e):
                    for L in range(4):
                        if L < 2:
                            pe.wait_ge(e_xlo, 2 * e + L + 1 + 2 * e0)
                        hidden(six, local + L, M[L // 2], L % 2)

                def round_(six_f, e, f, first):
                    if first:
                        pe.wait_ge(e_silu, N_EF * e + 1 + N_EF * e0)
                    hidden(six_f, 4, M[0], 0)
                    if first:
                        turn_product(N_EF * e + 1 + N_EF * e0)
                    hidden(six_f, 5, M[0], 1)
                    hidden(six_f, 6, M[1], 0)
                    hidden(six_f, 7, M[1], 1)
                    pe.wait_ge(e_lo, N_EF * e + f + N_EF * e0)
                    if first:
                        pe.wait_ge(e_added[1], e + 1 + e0)
                    back(six_f, 8, 0, first, False)
                    turn_product(N_EF * e + f + 1 + N_EF * e0)
                    back(six_f, 9, 1, False, False)

                def rounds(six, e, following):
                    round_(six, e, 1, True)
                    with pe.Fori(2, N_EF) as f:
                        round_(six + f - 1, e, f, False)
                    if following:
                        pe.wait_ge(e_added[0], e + 1 + e0)
                        gather(e + 2 + e0)
                    pe.wait_ge(e_pickw, e + 1 + e0)
                    for t in range(NT):
                        ins = pe.transpose(A[3][:, t * P:(t + 1) * P], pick_w[:, t, :], ident)
                    ins.then_inc(e_putw, 1)
                    pe.wait_ge(e_lo, N_EF * e + N_EF + N_EF * e0)
                    back(six, 40, 0, False, False, gT_last)
                    back(six, 41, 1, False, True, gT_last)

                def scatter(e):
                    for i, bank in enumerate((M[2], M[3], A[0], A[1])):
                        t, c = i % 2, i // 2
                        pe.wait_ge(e_ylo, 2 * e + c + 1 + 2 * e0)
                        for h in range(2):
                            ins = pe.matmul(bank[:, :], put[:, t * P:(t + 1) * P], y_part[h][:, c * 512:(c + 1) * 512],
                                            start=h == 0, stop=h == 1)
                        ins.then_inc(e_scatter, 1)

                gather(e0 + 1)
                if not block:
                    counts()
                round0(six0, 0, 0)
                with pe.Fori(0, N_EXP - 1) as e:
                    six = 7 * e + six0
                    rounds(six, e, True)
                    round0(six, 42, e + 1)
                    scatter(e)
                over = None
                if not block:
                    pe.wait_ge(rt_flag, 1)
                    over = pe.value_load(flag[0:1, 0:1], min_val=0, max_val=P)
                rounds(six0 + 7 * (N_EXP - 1), N_EXP - 1, False)
                scatter(N_EXP - 1)
                return over

            pe.wait_ge(zeros_set, 1)
            keep_clock(IDLE_START)
            pe.wait_ge(s_ident, 16)
            norm(0)
            mixers(0)
            norm(1)
            dense()
            norm(2)
            mixers(1)
            norm(3)
            router()
            over = experts(0)
            with pe.If(over > 0):
                experts(1)
            with pe.Else():
                pe.wait_ge(rt_flag, 1)


def _constants():
    f = np.float32
    c = np.zeros((P, C_ALL), f)
    i = np.arange(P)
    c[:, C_ID:C_ID + P] = np.eye(P, dtype=f)
    c[:, C_CAUSAL:C_CAUSAL + P] = np.where(i[:, None] >= i[None, :], 0.0, NEG)
    c[:, C_CHUNK:C_CHUNK + P] = (i[:, None] <= i[None, :]) & (i[:, None] // CHUNK == i[None, :] // CHUNK)
    c[:, C_STRICT:C_STRICT + P] = i[:, None] < i[None, :]
    c[:, C_ONES:C_ONES + P] = 1.0
    c[:, C_IOTA:C_IOTA + P] = i[None, :]
    half = HD // 2
    inv_freq = f(10000.0) ** (-(np.arange(half, dtype=f) / f(half)))
    ang = np.arange(SEQ, dtype=f)[:, None] * inv_freq[None, :].astype(f)
    cos, sin = np.cos(ang).astype(f), np.sin(ang).astype(f)
    c[:, C_COS:C_SIN] = cos.reshape(NT, P, half).transpose(1, 0, 2).reshape(P, -1)
    signed = np.stack([-sin, sin], 1).reshape(NT, P, 2, half)
    c[:, C_SIN:C_DECAY] = signed.transpose(1, 0, 2, 3).reshape(P, -1)
    gamma = np.log1p(-np.exp2(-5.0 - np.arange(HEADS, dtype=np.float64)))
    diff = np.arange(SEQ)[None, :] - i[:, None]
    d = np.where(diff[:, None, :] >= 0, np.exp(np.maximum(diff, 0)[:, None, :] * gamma[None, :, None]), 0.0)
    c[:, C_DECAY:C_ALL] = (d * float(HD) ** -0.5).reshape(P, -1)
    return c


def _stream(w):
    out = np.zeros((TOTAL_G, P, GRAN), np.float32)
    n = 0

    def rows(matrix, k0, nk, c0, nc_):
        nonlocal n
        part = matrix[k0 * P:(k0 + nk) * P, c0:c0 + nc_].reshape(nk, P, nc_)
        out[n].reshape(P, nk, nc_)[:] = part.transpose(1, 0, 2)
        n += 1

    for layer in range(LAYERS):
        w_in = w["w_in"][layer]
        small = out[n][:, 0:KT_D * NARROW].reshape(P, KT_D, NARROW)
        small[:, :, 0:GLA_RANK] = w_in[:, GA:GA + GLA_RANK].reshape(KT_D, P, GLA_RANK).transpose(1, 0, 2)
        small[:, :, 32:32 + HEADS] = w_in[:, FZ:FZ + HEADS].reshape(KT_D, P, HEADS).transpose(1, 0, 2)
        out[n][:, 0:KT_D * NARROW] = small.reshape(P, -1)
        n += 1
        for _, c0 in CHUNKS:
            for half in range(2):
                rows(w_in, 4 * half, 4, c0, 512)
        for b in BRANCH_ORDER:
            for c in range(2):
                for half in range(2):
                    rows(w["w_gate"][layer], 4 * half, 4, b * D + c * 512, 512)
                rows(w["w_branch"][layer][b], 0, 4, c * 512, 512)
        for half in range(2):
            for c in range(2):
                rows(w["w_o"][layer], 4 * half, 4, c * 512, 512)
        if layer == 0:
            for f in range(N_FF + 1):
                if f < N_FF:
                    rows(w["ffn_w1"][0], 0, 8, f * FF, FF)
                    rows(w["ffn_w3"][0], 0, 8, f * FF, FF)
                if f > 0:
                    rows(w["ffn_w2"][0], 2 * (f - 1), 2, 0, D)
    for k in range(KT_D):
        out[n][:, k * NARROW:k * NARROW + N_EXP] = w["router_w"][0][k * P:(k + 1) * P]
    n += 1
    for e in range(N_EXP):
        for f in range(N_EF + 1):
            if f < N_EF:
                for m in ("moe_w1", "moe_w3"):
                    for half in range(2):
                        rows(w[m][0, e], 4 * half, 4, f * EF, EF)
            if f > 0:
                for part in range(2):
                    rows(w["moe_w2"][0, e], 4 * (f - 1) + 2 * part, 2, 0, D)
    assert n == TOTAL_G
    return out


def kernel(**inputs):
    import concourse.bacc as _bacc
    from concourse.bass_utils import run_bass_kernel_spmd as _run

    w = {k: np.asarray(v) for k, v in inputs.items()}
    gains = np.stack([w["norm1_g"][0], w["norm2_g"][0], w["norm1_g"][1], w["norm2_g"][1],
                      w["final_g"]])
    a2 = np.concatenate([w["w_gla_a2"], w["b_gla_a"][:, None, :]], axis=1)
    arrays = {
        "stream": _stream(w),
        "x_in": np.ascontiguousarray(w["x"][0].reshape(NT, P, D).transpose(1, 0, 2)),
        "const_in": _constants(),
        "gains_in": gains,
        "b_forget_in": np.ascontiguousarray(w["b_forget"].T),
        "gla_a2_in": np.ascontiguousarray(a2.transpose(1, 0, 2)),
    }
    nc = _bacc.Bacc("TRN2", target_bir_lowering=False, num_devices=1)
    args = [nc.dram_tensor(name, a.shape, mybir.dt.from_np(a.dtype), kind="ExternalInput").ap()
            for name, a in arrays.items()]
    out = nc.dram_tensor("out", (P, NT, D), mybir.dt.float32, kind="ExternalOutput").ap()
    hybrid_decoder_kernel(nc, *args, out)
    r = _run(nc, [arrays], core_ids=[0])
    return r.results[0]["out"].transpose(1, 0, 2).reshape(1, SEQ, D)
```
